# Optimizing a Trainium2 kernel written in Bass

```python
import math
import jax, jax.numpy as jnp
from jax import lax
import numpy as np

D_MODEL = 2048
BATCH = 1
SEQ = 256
DEPTH = 1

DA_HEADS = 4
DA_HD = 64
DA_W = DA_HEADS * 2 * DA_HD
SW_HEADS = 8
SW_KV = 2
SW_HD = 64
WINDOW = 128
SW_QW = SW_HEADS * SW_HD
SW_KW = SW_KV * SW_HD
MB_HEADS = 8
MB_HD = 64
MB_W = MB_HEADS * MB_HD
MB_BLOCK = 256
MB_TOPK = 3
MB_CHUNK = 32
Q_BLOCK = 128
N_BUCKETS = 32
MAX_DIST = 128
N_ATT_HEADS = DA_HEADS + SW_HEADS + MB_HEADS
N_BRANCH = 3
IN_W = 3 * DA_W + SW_QW + 2 * SW_KW + 3 * MB_W + N_BRANCH * D_MODEL
D_FF = 5632
CONV_W = 3
EPS = 1e-6


def rmsnorm(x, g):
    xf = x.astype(jnp.float32)
    y = xf * lax.rsqrt(jnp.mean(xf * xf, axis=-1, keepdims=True) + EPS)
    return (y * g.astype(jnp.float32)).astype(x.dtype)

def rel_bucket(dist):
    n = jnp.maximum(dist, 0)
    max_exact = N_BUCKETS // 2
    nf = jnp.maximum(n, 1).astype(jnp.float32)
    large = max_exact + (jnp.log(nf / max_exact) / math.log(MAX_DIST / max_exact)
                         * (N_BUCKETS - max_exact)).astype(jnp.int32)
    large = jnp.minimum(large, N_BUCKETS - 1)
    return jnp.where(n < max_exact, n, large)

def diff_attention(q, k, v, lam, lam_init, subln_g, bias_t):
    B, S = q.shape[0], q.shape[1]
    nb = S // Q_BLOCK
    scale = DA_HD ** -0.5
    qb = jnp.moveaxis(q.reshape(B, nb, Q_BLOCK, DA_HEADS, 2, DA_HD), 1, 0)
    kpos = jnp.arange(S)

    def block(args):
        qi, i = args
        qpos = i * Q_BLOCK + jnp.arange(Q_BLOCK)
        dist = qpos[:, None] - kpos[None, :]
        bias = jnp.take(bias_t, rel_bucket(dist), axis=1)
        logits = jnp.einsum('bqhmd,bkhmd->bhmqk', qi, k).astype(jnp.float32) * scale + bias[None, :, None]
        logits = jnp.where(dist >= 0, logits, -jnp.inf)
        p = jax.nn.softmax(logits, axis=-1)
        attn = p[:, :, 0] - lam * p[:, :, 1]
        return jnp.einsum('bhqk,bkhe->bqhe', attn.astype(v.dtype), v)

    o = lax.map(block, (qb, jnp.arange(nb)))
    o = jnp.moveaxis(o, 0, 1).reshape(B, S, DA_HEADS, 2 * DA_HD)
    o = rmsnorm(o, subln_g) * (1.0 - lam_init)
    return o.reshape(B, S, DA_W)

def sliding_window_attention(q, k, v, sinks, bias_t):
    B, S = q.shape[0], q.shape[1]
    nb = S // Q_BLOCK
    G = SW_HEADS // SW_KV
    scale = SW_HD ** -0.5
    qb = q.reshape(B, nb, Q_BLOCK, SW_KV, G, SW_HD)
    kb = k.reshape(B, nb, Q_BLOCK, SW_KV, SW_HD)
    vb = v.reshape(B, nb, Q_BLOCK, SW_KV, SW_HD)
    shift = lambda t: jnp.concatenate([jnp.zeros_like(t[:, :1]), t[:, :-1]], axis=1)
    kc = jnp.concatenate([shift(kb), kb], axis=2)
    vc = jnp.concatenate([shift(vb), vb], axis=2)
    blk = jnp.arange(nb)[:, None] * Q_BLOCK
    qpos = blk + jnp.arange(Q_BLOCK)[None]
    kpos = blk - Q_BLOCK + jnp.arange(2 * Q_BLOCK)[None]
    dist = qpos[:, :, None] - kpos[:, None, :]
    valid = (dist >= 0) & (dist < WINDOW) & (kpos[:, None, :] >= 0)
    bias = jnp.take(bias_t, rel_bucket(dist), axis=1)
    bias = jnp.moveaxis(bias.reshape(SW_KV, G, nb, Q_BLOCK, 2 * Q_BLOCK), 2, 0)
    logits = jnp.einsum('bnqkgd,bnskd->bnkgqs', qb, kc).astype(jnp.float32) * scale + bias[None]
    logits = jnp.where(valid[None, :, None, None], logits, -jnp.inf)
    sink = jnp.broadcast_to(sinks.astype(jnp.float32).reshape(1, 1, SW_KV, G, 1, 1),
                            logits.shape[:-1] + (1,))
    p = jax.nn.softmax(jnp.concatenate([logits, sink], axis=-1), axis=-1)[..., :-1]
    o = jnp.einsum('bnkgqs,bnskd->bnqkgd', p.astype(vc.dtype), vc)
    return o.reshape(B, S, SW_QW)

def moba_attention(q, k, v, bias_t):
    B, S = q.shape[0], q.shape[1]
    nblk = -(-S // MB_BLOCK)
    Sp = nblk * MB_BLOCK
    padw = ((0, 0), (0, Sp - S), (0, 0), (0, 0))
    q, k, v = [jnp.pad(t, padw).transpose(0, 2, 1, 3) for t in (q, k, v)]
    scale = MB_HD ** -0.5
    kblk = k.reshape(B, MB_HEADS, nblk, MB_BLOCK, MB_HD)
    vblk = v.reshape(B, MB_HEADS, nblk, MB_BLOCK, MB_HD)
    kmean = jnp.mean(kblk.astype(jnp.float32), axis=3)
    own = jnp.arange(Sp) // MB_BLOCK
    gate = jnp.einsum('bhtd,bhnd->bhtn', q.astype(jnp.float32), kmean)
    past = jnp.arange(nblk)[None, :] < own[:, None]
    gate = jnp.where(past, gate, -jnp.inf)
    topk = min(MB_TOPK, nblk)
    _, idx = lax.top_k(gate, topk)

    nch = Sp // MB_CHUNK
    per_blk = MB_BLOCK // MB_CHUNK
    qc = q.reshape(B, MB_HEADS, nch, MB_CHUNK, MB_HD).transpose(2, 0, 1, 3, 4)
    idxc = idx.reshape(B, MB_HEADS, nch, MB_CHUNK, topk).transpose(2, 0, 1, 3, 4)
    bi = jnp.arange(B)[:, None, None, None]
    hi = jnp.arange(MB_HEADS)[None, :, None, None]
    hi5 = hi[..., None]
    s_off = jnp.arange(MB_BLOCK)

    def chunk(args):
        qi, ii, c = args
        qpos = c * MB_CHUNK + jnp.arange(MB_CHUNK)
        ob = c // per_blk
        ks = kblk[bi, hi, ii]
        vs = vblk[bi, hi, ii]
        dist_s = qpos[None, None, :, None, None] - (ii[..., None] * MB_BLOCK + s_off)
        ls = (jnp.einsum('bhcd,bhcjsd->bhcjs', qi, ks).astype(jnp.float32) * scale
              + bias_t[hi5, rel_bucket(dist_s)])
        ls = jnp.where((jnp.arange(topk) < ob)[:, None], ls, -jnp.inf)
        ls = ls.reshape(B, MB_HEADS, MB_CHUNK, topk * MB_BLOCK)
        ko = lax.dynamic_slice_in_dim(k, ob * MB_BLOCK, MB_BLOCK, axis=2)
        vo = lax.dynamic_slice_in_dim(v, ob * MB_BLOCK, MB_BLOCK, axis=2)
        dist_o = qpos[:, None] - (ob * MB_BLOCK + s_off)[None, :]
        lo = (jnp.einsum('bhcd,bhsd->bhcs', qi, ko).astype(jnp.float32) * scale
              + jnp.take(bias_t, rel_bucket(dist_o), axis=1)[None])
        lo = jnp.where(dist_o >= 0, lo, -jnp.inf)
        p = jax.nn.softmax(jnp.concatenate([ls, lo], axis=-1), axis=-1).astype(vs.dtype)
        ps = p[..., :topk * MB_BLOCK].reshape(B, MB_HEADS, MB_CHUNK, topk, MB_BLOCK)
        po = p[..., topk * MB_BLOCK:]
        return (jnp.einsum('bhcjs,bhcjsd->bhcd', ps, vs)
                + jnp.einsum('bhcs,bhsd->bhcd', po, vo))

    o = lax.map(chunk, (qc, idxc, jnp.arange(nch)))
    o = o.transpose(1, 0, 3, 2, 4).reshape(B, Sp, MB_W)
    return o[:, :S]

def conv_ffn(h, w_up, conv_w, conv_b, w_down):
    S = h.shape[1]
    u = h @ w_up
    up = jnp.pad(u, ((0, 0), (CONV_W - 1, 0), (0, 0)))
    c = conv_b
    for i in range(CONV_W):
        c = c + up[:, i:i + S] * conv_w[i]
    gate, val = jnp.split(c, 2, axis=-1)
    return (jax.nn.gelu(gate, approximate=True) * val) @ w_down

def first_inputs(seed: int = 0) -> dict:
    key = jax.random.key(seed)
    ks = jax.random.split(key, 24)
    f32 = jnp.float32
    nrm = lambda k, shape, s: jax.random.normal(k, shape, f32) * s
    gain = lambda k: 1.0 + nrm(k, (DEPTH, D_MODEL), 0.02)
    return {
        "x": nrm(ks[0], (BATCH, SEQ, D_MODEL), 1.0),
        "rel_bias_table": nrm(ks[1], (N_BUCKETS, N_ATT_HEADS), 0.5),
        "w_in": nrm(ks[2], (DEPTH, D_MODEL, IN_W), D_MODEL ** -0.5),
        "b_gate": nrm(ks[3], (DEPTH, N_BRANCH * D_MODEL), 0.1),
        "lam_q1": nrm(ks[4], (DEPTH, DA_HD), 0.1),
        "lam_k1": nrm(ks[5], (DEPTH, DA_HD), 0.1),
        "lam_q2": nrm(ks[6], (DEPTH, DA_HD), 0.1),
        "lam_k2": nrm(ks[7], (DEPTH, DA_HD), 0.1),
        "diff_subln_g": 1.0 + nrm(ks[8], (DEPTH, 2 * DA_HD), 0.02),
        "sinks": nrm(ks[9], (DEPTH, SW_HEADS), 0.5),
        "w_oa": nrm(ks[10], (DEPTH, DA_W, D_MODEL), DA_W ** -0.5),
        "w_ob": nrm(ks[11], (DEPTH, SW_QW, D_MODEL), SW_QW ** -0.5),
        "w_oc": nrm(ks[12], (DEPTH, MB_W, D_MODEL), MB_W ** -0.5),
        "w_out": nrm(ks[13], (DEPTH, D_MODEL, D_MODEL), D_MODEL ** -0.5),
        "pre_mix_g": gain(ks[14]),
        "post_mix_g": gain(ks[15]),
        "pre_ffn_g": gain(ks[16]),
        "post_ffn_g": gain(ks[17]),
        "w_up": nrm(ks[18], (DEPTH, D_MODEL, 2 * D_FF), D_MODEL ** -0.5),
        "conv_w": nrm(ks[19], (DEPTH, CONV_W, 2 * D_FF), CONV_W ** -0.5),
        "conv_b": nrm(ks[20], (DEPTH, 2 * D_FF), 0.02),
        "w_down": nrm(ks[21], (DEPTH, D_FF, D_MODEL), D_FF ** -0.5),
    }

def first_block(x, rel_bias_table, w_in, b_gate, lam_q1, lam_k1, lam_q2, lam_k2, diff_subln_g,
              sinks, w_oa, w_ob, w_oc, w_out, pre_mix_g, post_mix_g, pre_ffn_g, post_ffn_g,
              w_up, conv_w, conv_b, w_down):
    B, S = x.shape[0], x.shape[1]
    tab_t = rel_bias_table.T
    tab_a = tab_t[:DA_HEADS]
    tab_b = tab_t[DA_HEADS:DA_HEADS + SW_HEADS]
    tab_c = tab_t[DA_HEADS + SW_HEADS:]
    cuts = list(np.cumsum([DA_W, DA_W, DA_W, SW_QW, SW_KW, SW_KW, MB_W, MB_W, MB_W]))
    for l in range(DEPTH):
        h = rmsnorm(x, pre_mix_g[l])
        proj = h @ w_in[l]
        qa, ka, va, qb, kb, vb, qc, kc, vc, g = jnp.split(proj, cuts, axis=-1)
        gates = jax.nn.sigmoid((g + b_gate[l]).astype(jnp.float32)).astype(x.dtype)
        ga, gb, gc = jnp.split(gates, N_BRANCH, axis=-1)

        lam_init = 0.8 - 0.6 * math.exp(-0.3 * l)
        lam = (jnp.exp(jnp.sum(lam_q1[l].astype(jnp.float32) * lam_k1[l].astype(jnp.float32)))
               - jnp.exp(jnp.sum(lam_q2[l].astype(jnp.float32) * lam_k2[l].astype(jnp.float32)))
               + lam_init)
        ya = diff_attention(qa.reshape(B, S, DA_HEADS, 2, DA_HD), ka.reshape(B, S, DA_HEADS, 2, DA_HD),
                            va.reshape(B, S, DA_HEADS, 2 * DA_HD), lam, lam_init, diff_subln_g[l], tab_a)
        yb = sliding_window_attention(qb.reshape(B, S, SW_HEADS, SW_HD), kb.reshape(B, S, SW_KV, SW_HD),
                                      vb.reshape(B, S, SW_KV, SW_HD), sinks[l], tab_b)
        yc = moba_attention(qc.reshape(B, S, MB_HEADS, MB_HD), kc.reshape(B, S, MB_HEADS, MB_HD),
                            vc.reshape(B, S, MB_HEADS, MB_HD), tab_c)
        mix = ga * (ya @ w_oa[l]) + gb * (yb @ w_ob[l]) + gc * (yc @ w_oc[l])
        x = x + rmsnorm(mix @ w_out[l], post_mix_g[l])
        h = rmsnorm(x, pre_ffn_g[l])
        x = x + rmsnorm(conv_ffn(h, w_up[l], conv_w[l], conv_b[l], w_down[l]), post_ffn_g[l])
    return x


DEPTH_2 = 2

N_MIXERS = 2
GRID_W = 64
N_META = 16
NORM_EPS = 1e-6

ATTN_HEADS = 16
ATTN_KV_HEADS = 8
ATTN_GROUP = ATTN_HEADS // ATTN_KV_HEADS
ATTN_HEAD_DIM = 128
ATTN_WIDTH = ATTN_HEADS * ATTN_HEAD_DIM
ATTN_KV_WIDTH = ATTN_KV_HEADS * ATTN_HEAD_DIM
ATTN_IN = 2 * ATTN_WIDTH + 2 * ATTN_KV_WIDTH
ROPE_THETA = 10000.0
ROPE_AXIS_DIM = ATTN_HEAD_DIM // 2

GLA_HEADS = 4
GLA_KEY_DIM = D_MODEL // 2
GLA_VALUE_DIM = D_MODEL
GLA_HEAD_K = GLA_KEY_DIM // GLA_HEADS
GLA_HEAD_V = GLA_VALUE_DIM // GLA_HEADS
GLA_GATE_RANK = 16
GLA_GATE_NORMALIZER = 16.0
GLA_CHUNK = 64
GLA_IN = 2 * GLA_KEY_DIM + 2 * GLA_VALUE_DIM + 2 * GLA_GATE_RANK

N_ATTN_LAYERS = (DEPTH_2 + 1) // 2
N_GLA_LAYERS = DEPTH_2 // 2


def rmsnorm_2(x, w):
    xf = x.astype(jnp.float32)
    y = xf * lax.rsqrt(jnp.mean(xf * xf, axis=-1, keepdims=True) + NORM_EPS)
    return (y * w.astype(jnp.float32)).astype(x.dtype)

def axial_rope_angles(seq_len):
    rows = seq_len // GRID_W
    row = jnp.repeat(jnp.arange(rows), GRID_W).astype(jnp.float32)
    col = jnp.tile(jnp.arange(GRID_W), rows).astype(jnp.float32)
    inv_freq = ROPE_THETA ** (-jnp.arange(0, ROPE_AXIS_DIM, 2, dtype=jnp.float32) / ROPE_AXIS_DIM)
    meta = jnp.zeros((N_META, ROPE_AXIS_DIM // 2), jnp.float32)
    ang_row = jnp.concatenate([meta, row[:, None] * inv_freq[None]], axis=0)
    ang_col = jnp.concatenate([meta, col[:, None] * inv_freq[None]], axis=0)
    return ang_row, ang_col

def _rotate(x, ang):
    cos = jnp.cos(ang)[None, :, None, :].astype(x.dtype)
    sin = jnp.sin(ang)[None, :, None, :].astype(x.dtype)
    x1, x2 = jnp.split(x, 2, axis=-1)
    return jnp.concatenate([x1 * cos - x2 * sin, x2 * cos + x1 * sin], axis=-1)

def apply_axial_rope(x, ang_row, ang_col):
    return jnp.concatenate([_rotate(x[..., :ROPE_AXIS_DIM], ang_row),
                            _rotate(x[..., ROPE_AXIS_DIM:], ang_col)], axis=-1)

def _attend(qb, k, v):
    s = jnp.einsum('bqkgd,bskd->bkgqs', qb, k) * (ATTN_HEAD_DIM ** -0.5)
    p = jax.nn.softmax(s.astype(jnp.float32), axis=-1).astype(v.dtype)
    return jnp.einsum('bkgqs,bskd->bqkgd', p, v)

def attention_mixer(h, w_in, q_norm, k_norm, w_out, ang_row, ang_col):
    B, L, _ = h.shape
    proj = h @ w_in
    q, k, v, gate = jnp.split(
        proj, [ATTN_WIDTH, ATTN_WIDTH + ATTN_KV_WIDTH, ATTN_WIDTH + 2 * ATTN_KV_WIDTH], axis=-1)
    q = q.reshape(B, L, ATTN_HEADS, ATTN_HEAD_DIM)
    k = k.reshape(B, L, ATTN_KV_HEADS, ATTN_HEAD_DIM)
    v = v.reshape(B, L, ATTN_KV_HEADS, ATTN_HEAD_DIM)
    q = apply_axial_rope(rmsnorm_2(q, q_norm), ang_row, ang_col)
    k = apply_axial_rope(rmsnorm_2(k, k_norm), ang_row, ang_col)
    q = q.reshape(B, L, ATTN_KV_HEADS, ATTN_GROUP, ATTN_HEAD_DIM)
    o_meta = _attend(q[:, :N_META], k, v)
    n_real = L - N_META
    nb = n_real // Q_BLOCK
    q_blocks = q[:, N_META:].reshape(B, nb, Q_BLOCK, ATTN_KV_HEADS, ATTN_GROUP, ATTN_HEAD_DIM)
    o_real = lax.map(lambda qb: _attend(qb, k, v), jnp.swapaxes(q_blocks, 0, 1))
    o_real = jnp.swapaxes(o_real, 0, 1).reshape(B, n_real, ATTN_KV_HEADS, ATTN_GROUP, ATTN_HEAD_DIM)
    o = jnp.concatenate([o_meta, o_real], axis=1).reshape(B, L, ATTN_WIDTH)
    return (o * jax.nn.silu(gate)) @ w_out

def gla_chunked(q, k, v, g, strict):
    B, H, T, dk = q.shape
    dv = v.shape[-1]
    n = T // GLA_CHUNK

    def chunks(t):
        return t.reshape(B, H, n, GLA_CHUNK, t.shape[-1]).astype(jnp.float32)

    qc, kc, vc, gc = chunks(q), chunks(k), chunks(v), chunks(g)
    b = jnp.cumsum(gc, axis=3)
    b_last = b[:, :, :, -1:, :]
    q_dec = qc * jnp.exp(b)
    k_inv = kc * jnp.exp(-b)
    k_end = kc * jnp.exp(b_last - b)
    scores = jnp.einsum('bhncd,bhnsd->bhncs', q_dec, k_inv)
    mask = jnp.tril(jnp.ones((GLA_CHUNK, GLA_CHUNK), bool), k=-1 if strict else 0)
    o_intra = jnp.einsum('bhncs,bhnse->bhnce', jnp.where(mask, scores, 0.0), vc)

    def step(S, xs):
        q_t, k_t, v_t, dl = xs
        o = jnp.einsum('bhcd,bhde->bhce', q_t, S)
        S = S * dl[..., None] + jnp.einsum('bhcd,bhce->bhde', k_t, v_t)
        return S, o

    xs = (jnp.moveaxis(q_dec, 2, 0), jnp.moveaxis(k_end, 2, 0), jnp.moveaxis(vc, 2, 0),
          jnp.moveaxis(jnp.exp(b_last[:, :, :, 0, :]), 2, 0))
    S0 = jnp.zeros((B, H, dk, dv), jnp.float32)
    _, o_inter = lax.scan(step, S0, xs)
    o = o_intra + jnp.moveaxis(o_inter, 0, 2)
    return o.reshape(B, H, T, dv).astype(q.dtype)

def gla_mixer(h, w_in, gk_up, gk_bias, o_norm, w_out):
    B, L, _ = h.shape
    pad = GLA_CHUNK - N_META
    hp = jnp.pad(h, ((0, 0), (pad, 0), (0, 0)))
    T = L + pad
    proj = hp @ w_in
    s1 = GLA_KEY_DIM
    s2 = s1 + GLA_KEY_DIM
    s3 = s2 + GLA_VALUE_DIM
    s4 = s3 + GLA_VALUE_DIM
    s5 = s4 + GLA_GATE_RANK
    q, k, v, g_out, lr_f, lr_b = jnp.split(proj, [s1, s2, s3, s4, s5], axis=-1)

    def heads(t, d):
        return t.reshape(B, T, GLA_HEADS, d).transpose(0, 2, 1, 3)

    def log_gate(lr, up, bias):
        z = (lr @ up + bias).astype(jnp.float32)
        return heads(jax.nn.log_sigmoid(z) / GLA_GATE_NORMALIZER, GLA_HEAD_K)

    q = heads(q, GLA_HEAD_K) * (GLA_HEAD_K ** -0.5)
    k = heads(k, GLA_HEAD_K)
    v = heads(v, GLA_HEAD_V)
    flip = lambda t: jnp.flip(t, axis=2)
    o_f = gla_chunked(q, k, v, log_gate(lr_f, gk_up[0], gk_bias[0]), strict=False)
    o_b = flip(gla_chunked(flip(q), flip(k), flip(v),
                           flip(log_gate(lr_b, gk_up[1], gk_bias[1])), strict=True))
    o = (o_f + o_b).transpose(0, 2, 1, 3)[:, pad:]
    o = rmsnorm_2(o, o_norm).reshape(B, L, GLA_VALUE_DIM)
    return (o * jax.nn.silu(g_out[:, pad:])) @ w_out

def second_inputs(seed: int = 0) -> dict:
    key = jax.random.key(seed)
    ks = jax.random.split(key, 13)
    f32 = jnp.float32
    nrm = lambda k, shape, scale: jax.random.normal(k, shape, f32) * scale
    return {
        "x": nrm(ks[0], (BATCH, SEQ, D_MODEL), 1.0),
        "meta_tokens": nrm(ks[1], (N_META, D_MODEL), 1.0),
        "pre_norm": 1.0 + nrm(ks[2], (DEPTH_2, D_MODEL), 0.02),
        "post_norm": 1.0 + nrm(ks[3], (DEPTH_2, D_MODEL), 0.02),
        "attn_w_in": nrm(ks[4], (N_ATTN_LAYERS, D_MODEL, ATTN_IN), D_MODEL ** -0.5),
        "attn_q_norm": 1.0 + nrm(ks[5], (N_ATTN_LAYERS, ATTN_HEAD_DIM), 0.02),
        "attn_k_norm": 1.0 + nrm(ks[6], (N_ATTN_LAYERS, ATTN_HEAD_DIM), 0.02),
        "attn_w_out": nrm(ks[7], (N_ATTN_LAYERS, ATTN_WIDTH, D_MODEL), ATTN_WIDTH ** -0.5),
        "gla_w_in": nrm(ks[8], (N_GLA_LAYERS, D_MODEL, GLA_IN), D_MODEL ** -0.5),
        "gla_gk_up": nrm(ks[9], (N_GLA_LAYERS, 2, GLA_GATE_RANK, GLA_KEY_DIM), GLA_GATE_RANK ** -0.5),
        "gla_gk_bias": nrm(ks[10], (N_GLA_LAYERS, 2, GLA_KEY_DIM), 0.1),
        "gla_o_norm": 1.0 + nrm(ks[11], (N_GLA_LAYERS, GLA_HEAD_V), 0.02),
        "gla_w_out": nrm(ks[12], (N_GLA_LAYERS, GLA_VALUE_DIM, D_MODEL), GLA_VALUE_DIM ** -0.5),
    }

def second_block(x, meta_tokens, pre_norm, post_norm, attn_w_in, attn_q_norm, attn_k_norm,
              attn_w_out, gla_w_in, gla_gk_up, gla_gk_bias, gla_o_norm, gla_w_out):
    B, S, D = x.shape
    meta = jnp.broadcast_to(meta_tokens.astype(x.dtype)[None], (B, N_META, D))
    h = jnp.concatenate([meta, x], axis=1)
    ang_row, ang_col = axial_rope_angles(S)
    for i in range(DEPTH_2):
        y = rmsnorm_2(h, pre_norm[i])
        j = i // N_MIXERS
        if i % N_MIXERS == 0:
            y = attention_mixer(y, attn_w_in[j], attn_q_norm[j], attn_k_norm[j], attn_w_out[j],
                                ang_row, ang_col)
        else:
            y = gla_mixer(y, gla_w_in[j], gla_gk_up[j], gla_gk_bias[j], gla_o_norm[j], gla_w_out[j])
        h = h + rmsnorm_2(y, post_norm[i])
    return h[:, N_META:]


def setup_inputs(seed=0):
    out = dict(first_inputs(seed))
    for name, value in second_inputs(seed + 1).items():
        if name != "x":
            out[name + "_2"] = value
    return out


def reference(
    x, rel_bias_table, w_in, b_gate, lam_q1, lam_k1, lam_q2, lam_k2, diff_subln_g, sinks, w_oa,
    w_ob, w_oc, w_out, pre_mix_g, post_mix_g, pre_ffn_g, post_ffn_g, w_up, conv_w, conv_b,
    w_down, meta_tokens_2, pre_norm_2, post_norm_2, attn_w_in_2, attn_q_norm_2, attn_k_norm_2,
    attn_w_out_2, gla_w_in_2, gla_gk_up_2, gla_gk_bias_2, gla_o_norm_2, gla_w_out_2,
):
    x = first_block(
        x, rel_bias_table, w_in, b_gate, lam_q1, lam_k1, lam_q2, lam_k2, diff_subln_g, sinks,
        w_oa, w_ob, w_oc, w_out, pre_mix_g, post_mix_g, pre_ffn_g, post_ffn_g, w_up, conv_w,
        conv_b, w_down,
    )
    return second_block(
        x, meta_tokens_2, pre_norm_2, post_norm_2, attn_w_in_2, attn_q_norm_2, attn_k_norm_2,
        attn_w_out_2, gla_w_in_2, gla_gk_up_2, gla_gk_bias_2, gla_o_norm_2, gla_w_out_2,
    )


_drawn_inputs = setup_inputs


def setup_inputs(seed=0):
    import zlib

    import numpy as np

    out = dict(_drawn_inputs(seed))
    spreads = {}
    factors = {'sinks': 4.641,
     'post_ffn_g': 3.465,
     'post_norm_2': 3.469,
     'attn_q_norm_2': 8.0,
     'attn_k_norm_2': 8.0,
     'gla_gk_bias_2': 2.671,
     'gla_o_norm_2': 6.124}
    for name, (base, spread) in spreads.items():
        noise = np.random.default_rng([zlib.crc32(name.encode()), seed]).standard_normal(out[name].shape)
        drawn = base * np.exp(spread * noise) if base else spread * noise
        out[name] = __import__('jax').numpy.asarray(drawn.astype(out[name].dtype))
    for name, factor in factors.items():
        out[name] = (out[name] * factor).astype(out[name].dtype)
    return out
```

```python
import math
from contextlib import ExitStack

import numpy as np

import concourse.bass as bass
from concourse import mybir

F32 = mybir.dt.float32
F32R = mybir.dt.float32r
ALU = mybir.AluOpType
ACT = mybir.ActivationFunctionType
AX = mybir.AxisListType

P = 128
D = 2048
KD = D // P
TB = 256
TM = 16
T2 = TB + TM
EPS = 1e-6

DA_HEADS, SW_HEADS, MB_HEADS, HD = 4, 8, 8, 64
N_HEADS = DA_HEADS + SW_HEADS + MB_HEADS
WINDOW = 128
N_BUCKETS, MAX_DIST = 32, 128
QKV = 512
IN_GATES = 3 * QKV + QKV + 2 * P + 3 * QKV
D_FF = 5632
FT = D_FF // P
LAM_INIT = 0.8 - 0.6 * math.exp(-0.3 * 0)
MASKED = -float(2 ** 100)
LINE = 2 * P + P - 1

AT_HEADS, AT_KV, AT_HD = 16, 8, 128
GRID_W, ROPE_THETA, ROPE_AXIS = 64, 10000.0, 64
GL_HEADS, GL_K, GL_V, GL_RANK, GL_CHUNK = 4, 256, 512, 16, 64
GL_NORMALIZER = 16.0
KT = 8

UNIT = 1024
RAW, RING, LEAD = 8, 4, 3

STREAM = [("qkv", 2, 24, 3), ("qb", 1, 8, 1), ("kvb", 1, 4, 1), ("gates", 12, 8, 1), ("oabc", 4, 8, 3),
          ("wout", 4, 8, 1), ("up", 22, 8, 1), ("down", 4, 24, 1), ("aqk", 6, 8, 1), ("av", 2, 8, 1),
          ("ag", 4, 8, 1), ("aout", 4, 8, 1), ("gqk", 4, 8, 1), ("gv", 4, 8, 1), ("gg", 4, 8, 1),
          ("lr", 1, 1, 1), ("gout", 4, 8, 1)]
TRIPS, UNITS, CHUNKS, U0, C0 = {}, {}, {}, {}, {}
_u = _c = 0
for _name, _trips, _units, _chunks in STREAM:
    TRIPS[_name], UNITS[_name], CHUNKS[_name], U0[_name], C0[_name] = _trips, _units, _chunks, _u, _c
    _u += _trips * _units
    _c += _trips * _chunks
N_UNITS = _u

PARAMS = [("pre_mix_g", 16), ("subln", 1), ("b_gate", 48), ("post_mix_g", 16), ("pre_ffn_g", 16), ("conv_w", 264),
          ("conv_b", 88), ("post_ffn_g", 16), ("pre_norm_2", 32), ("post_norm_2", 32), ("attn_q_norm_2", 1),
          ("attn_k_norm_2", 1), ("gla_gk_bias_2", 16), ("gla_o_norm_2", 4)]
PAR = {}
_r = 0
for _name, _rows in PARAMS:
    PAR[_name] = _r
    _r += _rows
N_PAR = _r
PAR_GROUPS = -(-N_PAR // P)
N_SMALL = sum((PAR[n] + r - 1) // P - PAR[n] // P + 1 for n, r in PARAMS) + 5


def at(const, trip, per_trip):
    return trip * per_trip + const


def under(const, trip, per_trip, bound):
    return isinstance(trip, int) and trip * per_trip + const < bound


def shape_constants():
    f32 = np.float32
    dist = 255 - np.arange(LINE)
    n = np.maximum(dist, 0)
    half = N_BUCKETS // 2
    large = half + (np.log(np.maximum(n, 1).astype(f32) / f32(half)) / f32(math.log(MAX_DIST / half))
                    * f32(N_BUCKETS - half)).astype(np.int32)
    bucket = np.where(n < half, n, np.minimum(large, N_BUCKETS - 1))

    def one_hot(valid):
        row = np.where(valid, bucket, N_BUCKETS)
        return (np.arange(N_BUCKETS + 1)[:, None] == row[None]).astype(f32)

    token = np.arange(TB)
    inv = f32(ROPE_THETA) ** (-np.arange(0, ROPE_AXIS, 2, dtype=f32) / f32(ROPE_AXIS))
    angle = np.zeros((P, T2), f32)
    for axis, pos in enumerate((token // GRID_W, token % GRID_W)):
        for half_ in range(2):
            r0 = axis * 64 + half_ * 32
            angle[r0:r0 + 32, :TB] = inv[:, None] * pos.astype(f32)[None]
    turn = np.zeros((P, P), f32)
    for d in range(P):
        if d % 64 < 32:
            turn[d + 32, d] = -1.0
        else:
            turn[d - 32, d] = 1.0
    s, c = np.arange(P)[:, None], np.arange(P)[None]
    same = s // GL_CHUNK == c // GL_CHUNK
    reset = np.ones((P, T2), f32)
    reset[:, 0:T2:GL_CHUNK] = 0.0
    return {
        "c_hot_full": one_hot(dist >= 0), "c_hot_window": one_hot((dist >= 0) & (dist < WINDOW)),
        "c_cos": np.cos(angle).astype(f32), "c_sin": np.sin(angle).astype(f32), "c_turn": turn,
        "c_ident": np.eye(P, dtype=f32), "c_mask_f": (same & (s <= c)).astype(f32),
        "c_mask_b": (same & (s > c)).astype(f32), "c_reset": reset,
    }


def two_blocks_kernel(nc, A, out):
    ctx = ExitStack()
    with ctx:
        place_at = [(nc.sbuf_base + 31) // 32 * 32]

        def sb(name, shape, dt=F32, at_=None):
            size = int(np.prod(shape[1:])) * 4
            off = place_at[0] if at_ is None else at_
            t = nc.alloc_sbuf_tensor_at(name, shape, dt, offset=off)
            if at_ is None:
                place_at[0] = off + (size + 31) // 32 * 32
            return t

        def sem(name):
            return ctx.enter_context(nc.semaphore(name))

        raw = sb("raw", [P, RAW, UNIT])
        whi = sb("whi", [P, RING, UNIT], F32R)
        wlo = sb("wlo", [P, RING, UNIT], F32R)
        SPARE = P - TM
        act_at = place_at[0]
        ahi = sb("ahi", [P, KD * T2 + SPARE], F32R)
        alo = sb("alo", [P, KD * T2 + SPARE], F32R)
        par = sb("par", [P, N_PAR])
        ident = sb("ident", [P, P])
        ones = sb("ones", [P, P])
        lam = sb("lam", [P, 4])
        sinkn = sb("sinkn", [P, SW_HEADS])
        subg = sb("subg", [P, 1])
        qgain = sb("qgain", [P, 1])
        xT_at = place_at[0]
        xT = sb("xT", [P, KD, T2])
        msq = sb("msq", [P, T2])
        rstd = sb("rstd", [P, T2])
        sqacc = sb("sqacc", [P, T2])
        tmp = sb("tmp", [P, 2, T2])
        sqb_at = place_at[0]
        sqb = sb("sqb", [P, 2, T2])
        R2 = place_at[0]
        LIMIT = nc.sbuf_usable_end

        def region(*parts):
            off, made = R2, []
            for name, shape, dt in parts:
                made.append(sb(name, shape, dt, at_=off))
                off += (int(np.prod(shape[1:])) * 4 + 31) // 32 * 32
            assert off <= LIMIT, (parts[0][0], off, LIMIT)
            return made

        def ha(t, k, c0, n):
            return t[:, k * T2 + c0:k * T2 + c0 + n]

        xrow, mrow, prow, tabx, hots, line, lamv = region(
            ("xrow", [P, 2, D], F32), ("mrow", [TM, D], F32), ("prow", [P, PAR_GROUPS, P], F32),
            ("tabx", [N_BUCKETS + 1, N_HEADS], F32), ("hots", [N_BUCKETS + 1, 2, LINE], F32),
            ("line", [N_HEADS, 2, LINE], F32), ("lamv", [HD, 6], F32))
        (qT, kT, vtok, qbT, kbT, vbtok, bias, yhi, ylo, sbias, prob, probT, osb, sinkb, nmax, ssum,
         esink) = region(
            ("qT", [P, 8, TB], F32), ("kT", [P, 8, TB], F32), ("vtok", [P, 4, QKV], F32),
            ("qbT", [P, 4, TB], F32), ("kbT", [P, 2, TB], F32), ("vbtok", [P, 2, P], F32),
            ("bias", [P, N_HEADS, TB], F32), ("yhi", [P, 12, TB], F32R), ("ylo", [P, 12, TB], F32R),
            ("sbias", [P, 2, 384], F32), ("prob", [P, 4, 384], F32), ("probT", [P, 2, 384], F32),
            ("osb", [P, 4, TB], F32), ("sinkb", [P, SW_HEADS], F32), ("nmax", [P, 24, 2], F32),
            ("ssum", [P, 24, 2], F32), ("esink", [P, 8, 2], F32))
        bias_at = R2 + 4 * (8 * TB * 2 + 4 * QKV + 4 * TB + 2 * TB + 2 * P)
        osq = sb("osq", [P, 4, TB], F32, at_=bias_at)
        ors = sb("ors", [P, 4, TB], F32, at_=bias_at + 4096)
        yn = sb("yn", [P, 4, TB], F32, at_=bias_at + 8192)
        (gate,) = region(("gate", [P, 48, TB], F32))
        assert R2 + 48 * TB * 4 <= bias_at + N_HEADS * TB * 4
        mixtmp = sb("mixtmp", [P, 2, 4, TB], F32, at_=bias_at + N_HEADS * TB * 4 + 24 * TB * 4)
        (yT,) = region(("yT", [P, KD, T2], F32))
        ghi, glo, cv, pr = region(("ghi", [P, FT, TB], F32R), ("glo", [P, FT, TB], F32R), ("cv", [P, 4, TB], F32),
                                  ("pr", [P, 2, TB], F32))
        yT_ffn = sb("yT_ffn", [P, KD, T2], F32, at_=act_at)
        qk2, v2, gs2, cos, sin, turn, sq2, rs2, n2, nc2, p2, pT2, z2, nm2, sum2 = region(
            ("qk2", [P, 24, T2], F32), ("v2", [P, 3, 1024], F32), ("gs2", [P, KD, T2], F32), ("cos", [P, T2], F32),
            ("sin", [P, T2], F32), ("turn", [P, P], F32), ("sq2", [P, 2, T2], F32), ("rs2", [P, 2, T2], F32),
            ("n2", [P, 2, T2], F32), ("nc2", [P, 2, T2], F32), ("p2", [P, 2, 3, T2], F32), ("pT2", [P, 2, 3, T2], F32),
            ("z2", [P, 2, T2], F32), ("nm2", [P, AT_HEADS, 3], F32), ("sum2", [P, AT_HEADS, 3], F32))
        cum = sb("cum", [P, 16, T2], F32, at_=xT_at)
        (gqk, v3, gg, maskf, maskb, reset, qdec, kinv, kendf, kendb, keT, keTm, sc, osq3, stf, stb) = region(
            ("gqk", [P, 16, T2], F32), ("v3", [P, 3, D], F32), ("gg", [P, KD, TB], F32), ("maskf", [P, P], F32),
            ("maskb", [P, P], F32), ("reset", [P, T2], F32), ("qdec", [P, 2, 2, TB], F32),
            ("kinv", [P, 2, 2, TB], F32), ("kendf", [P, 2, T2], F32), ("kendb", [P, 2, TB], F32),
            ("keT", [P, 2, 2, GL_K], F32), ("keTm", [TM, GL_K], F32), ("sc", [P, 2, P], F32),
            ("osq3", [P, 4, TB], F32), ("stf", [P, 2, 2, GL_V], F32), ("stb", [P, 2, 2, GL_V], F32))
        dec = sb("dec", [P, 2, 2, 5], F32, at_=sqb_at)
        gate_at = R2 + 4 * (16 * T2 + 3 * D + KD * TB + 2 * P + T2 + 4 * TB * 2 + 2 * T2 + 2 * TB + 4 * GL_K + GL_K + 2 * P)
        lrT = sb("lrT", [GL_RANK, 2, T2], F32, at_=gate_at)
        up_w = sb("up_w", [GL_RANK, 2, KT * P], F32, at_=gate_at + 2 * T2 * 4)
        zabs = sb("zabs", [P, 2, 4, T2], F32, at_=gate_at + 2 * T2 * 4 + 2 * KT * P * 4)
        orow = sb("orow", [P, 2, D], F32, at_=R2 + KD * T2 * 4)

        bank = ctx.enter_context(nc.psum_tensor("bank", [P, 8, 512], F32))

        def rows_of(w, c0, width, k0, nk):
            return w.rearrange("(k p) n -> p k n", p=P)[:, k0:k0 + nk, bass.ds(c0, width)]

        w_in, w_out, w_up, w_down = A["w_in"][0], A["w_out"][0], A["w_up"][0], A["w_down"][0]
        w_o = [A["w_oa"][0], A["w_ob"][0], A["w_oc"][0]]
        attn_in, attn_out = A["attn_w_in_2"][0], A["attn_w_out_2"][0]
        gla_in, gla_out = A["gla_w_in_2"][0], A["gla_w_out_2"][0]
        lines_dram = nc.dram_tensor("bias_lines", [N_HEADS, P, LINE + 1], F32, kind="Internal").ap()
        park_dram = nc.dram_tensor("parked_x", [P, KD * T2], F32, kind="Internal").ap()

        def unit_tiles(ph, j):
            if ph == "kvb":
                return 4 * j, 4
            if ph == "oabc":
                return (2 * (j % 2), 2) if j < 4 else (j - 4, 1)
            if ph == "down":
                return (2 * j, 2) if j < 20 else (20 + j, 1)
            if ph == "up":
                return 4 * (j // 2), 4
            if ph == "lr":
                return 0, KD
            return 2 * (j % 8), 2

        def chunk_of(ph, j):
            if ph == "kvb":
                return 0, j == 0, j == 3
            if ph == "oabc":
                return min(j // 2, 2), j in (0, 2, 4), j in (1, 3, 7)
            if ph == "down":
                return 0, j == 0, j == 23
            if ph == "lr":
                return 0, True, True
            return j // 8, j % 8 == 0, j % 8 == 7

        def unit_source(ph, i, j):
            k0, nk = unit_tiles(ph, j)

            def col(c, per):
                return at(c, i, per)

            if ph == "qkv":
                return ((0, 1024), rows_of(w_in, col(QKV * (j // 8), 3 * QKV + QKV + 2 * P), QKV, k0, nk))
            if ph == "qb":
                return ((0, 1024), rows_of(w_in, 3 * QKV, QKV, k0, nk))
            if ph == "kvb":
                return ((0, 1024), rows_of(w_in, 4 * QKV, 2 * P, k0, nk))
            if ph == "gates":
                return ((0, 1024), rows_of(w_in, col(IN_GATES, 512), 512, k0, nk))
            if ph == "oabc":
                return ((0, nk * 512), rows_of(w_o[chunk_of(ph, j)[0]], col(0, 512), 512, k0, nk))
            if ph == "up":
                return ((0, 1024), rows_of(w_up, col((j % 2) * D_FF, 256), 256, k0, nk))
            if ph == "down":
                return ((0, nk * 512), rows_of(w_down, col(0, 512), 512, k0, nk))
            if ph == "lr":
                return ((0, KD * 2 * GL_RANK), rows_of(gla_in, 3 * D, 2 * GL_RANK, 0, KD))
            w, c0 = {"wout": (w_out, 0), "aqk": (attn_in, 0), "av": (attn_in, 3072), "ag": (attn_in, 4096),
                     "aout": (attn_out, 0), "gqk": (gla_in, 0), "gv": (gla_in, 2048), "gg": (gla_in, 4096),
                     "gout": (gla_out, 0)}[ph]
            return ((0, 1024), rows_of(w, col(c0, 512), 512, k0, nk))

        raw_loaded = [sem(f"raw_loaded{n}") for n in range(RAW)]
        whi_ready, wlo_ready, tile_pass, acc_free = map(sem, "whi_ready wlo_ready tile_pass acc_free".split())
        rows_in, small_in, hots_in, start_set, spare_set, row_turned, row_taken, par_ready = map(
            sem, "rows_in small_in hots_in start_set spare_set row_turned row_taken par_ready".split())
        lam_prod, lam_sum, lam_exp, lam_ready = map(sem, "lam_prod lam_sum lam_exp lam_ready".split())
        line_sum, line_ready, lines_stored, bias_in = map(sem, "line_sum line_ready lines_stored bias_in".split())
        y_squared, y_summed, mean_ready, mean_eps, inv_ready, rstd_ready, y_scaled, x_updated, \
            sq_ready, sq_used, h_ready, hhi_ready, act_ready = map(
                sem, "y_squared y_summed mean_ready mean_eps inv_ready rstd_ready y_scaled x_updated "
                     "sq_ready sq_used h_ready hhi_ready act_ready".split())
        s_ready, s_biased, max_ready, max_sink, p_ready, sink_ready, sum_sink, inv_sum, p_second, p_scaled, \
            p_turned, pT_ready, o_ready, o_free, yhi_ready, a_out, a_squared, a_summed, a_mean, a_inv, a_rstd, \
            a_normed, ya_hi, y_done = map(
                sem, "s_ready s_biased max_ready max_sink p_ready sink_ready sum_sink inv_sum p_second p_scaled "
                     "p_turned pT_ready o_ready o_free yhi_ready a_out a_squared a_summed a_mean a_inv a_rstd "
                     "a_normed ya_hi y_done".split())
        mix_two, mix_part, mix_sum = map(sem, "mix_two mix_part mix_sum".split())
        tap2, tap1, gelu_done, ff_prod, ffhi_ready = map(
            sem, "tap2 tap1 gelu_done ff_prod ffhi_ready".split())
        rope_in, qk_sq, qk_sum, qk_mean, qk_inv, qk_rstd, qk_normed, qk_turned, qk_cos, qk_sin, qk_done = map(
            sem, "rope_in qk_sq qk_sum qk_mean qk_inv qk_rstd qk_normed qk_turned qk_cos qk_sin qk_done".split())
        s2_ready, max2_ready, p2_ready, inv2, p2_scaled, p2_turned, pT2_act, pT2_dve, o2_ready, z2_ready, z2hi = \
            map(sem, "s2_ready max2_ready p2_ready inv2 p2_scaled p2_turned pT2_act pT2_dve o2_ready "
                               "z2_ready z2hi".split())
        x_parked, x_back, gla_const, z_sum, z_abs, z_min, z_exp, z_ln, z_sub, cum_ready = map(
            sem, "x_parked x_back gla_const z_sum z_abs z_min z_exp z_ln z_sub cum_ready".split())
        e_q, e_k, e_d, e_dec, d_sub, q_dec, k_inv, k_end, ke_turned, ke_act, ke_dve, sc_sum, sc_part, sc_ready, \
            ds_ready, st_ready, o3_part, o3_sq, o3_sum, o3_mean, o3_inv, o3_rstd, o3_scaled, z3_ready, z3hi = \
            map(
                sem, "e_q e_k e_d e_dec d_sub q_dec k_inv k_end ke_turned ke_act ke_dve sc_sum sc_part sc_ready "
                     "ds_ready st_ready o3_part o3_sq o3_sum o3_mean o3_inv o3_rstd o3_scaled z3_ready z3hi".split())
        out_turned, out_taken, stored = map(sem, "out_turned out_taken stored".split())

        LO, lo_tiles = {}, 0
        for name, tiles in (("norm0", KD), ("mix", KD), ("norm1", KD), ("ff", FT), ("norm2", KD), ("z2", AT_HEADS),
                            ("norm3", KD), ("z3", GL_HEADS)):
            LO[name] = lo_tiles
            lo_tiles += tiles

        PRE, POST = (lambda b: 2 * b), (lambda b: 2 * b - 1)
        T_PRE = [TB, TB, T2, T2]
        T_POST = [None, TB, TB, T2, TB]
        G_PRE = [PAR["pre_mix_g"], PAR["pre_ffn_g"], PAR["pre_norm_2"], PAR["pre_norm_2"] + KD]
        G_POST = [None, PAR["post_mix_g"], PAR["post_ffn_g"], PAR["post_norm_2"], PAR["post_norm_2"] + KD]
        OUT_STREAM = [None, "wout", "down", "aout", "gout"]
        Y = [None, yT, yT_ffn, yT, yT]

        def job_of(m):
            return m // 2 if m < 2 * DA_HEADS else m - DA_HEADS

        def ends_job(m):
            return m < 24 and (m >= 2 * DA_HEADS or m % 2 == 1)

        def ahi_tile(i, t):
            return ahi[:, 0:KD * T2].rearrange("p (k t) -> p k t", t=T2)[:, bass.ds(i * 4 + t, 1), 0:TB]

        def alo_tile(i, t):
            return alo[:, 0:KD * T2].rearrange("p (k t) -> p k t", t=T2)[:, bass.ds(i * 4 + t, 1), 0:TB]

        def ring_waits(eng, ph, i, u, n, landed):
            if landed:
                eng.wait_ge(raw_loaded[u % RAW], at(16 * (u // RAW + 1), i, 2 * n))
            if not under(u, i, n, RING):
                eng.wait_ge(tile_pass, at(4 * (u - RING + 1), i, 4 * n))

        block = ctx.enter_context(nc.Block())

        @block.sync
        def _(sp):
            def load_trip(ph, i):
                n = UNITS[ph]
                for j in range(n):
                    u = U0[ph] + j
                    if not under(u, i, n, RAW):
                        sp.wait_ge(wlo_ready, at(u - RAW + 1, i, n))
                    (c0, c1), src = unit_source(ph, i, j)
                    dst = raw[:, u % RAW, c0:c1].rearrange("p (k n) -> p k n", k=src.shape[1])
                    sp.dma_start(dst, src).then_inc(raw_loaded[u % RAW], 16)

            def load(ph):
                if TRIPS[ph] <= 2:
                    for i in range(TRIPS[ph]):
                        load_trip(ph, i)
                else:
                    with sp.Fori(0, TRIPS[ph]) as i:
                        load_trip(ph, i)

            for tt in range(2):
                sp.dma_start(xrow[:, tt, :], A["x"][0, tt * P:(tt + 1) * P, :]).then_inc(rows_in, 16)
            sp.dma_start(mrow[:, :], A["meta_tokens_2"]).then_inc(rows_in, 16)
            load("qkv")
            sp.wait_ge(lines_stored, 48)
            skewed = bass.AP(tensor=lines_dram.tensor, offset=P - 1, ap=[[LINE, P], [P * (LINE + 1), N_HEADS], [1, TB]])
            sp.dma_start(bias[:, :, :], skewed).then_inc(bias_in, 16)
            for ph in ("qb", "kvb", "gates", "oabc", "wout", "up", "down", "aqk", "av", "ag", "aout", "gqk", "gv", "gg",
                       "lr", "gout"):
                load(ph)
            sp.wait_ge(x_parked, 16)
            sp.wait_ge(e_dec, 3 * GL_HEADS)
            sp.wait_ge(d_sub, 3 * GL_HEADS)
            sp.dma_start(xT[:, :, :].rearrange("p k t -> p (k t)"), park_dram).then_inc(x_back, 16)
            for tt in range(2):
                sp.wait_ge(out_taken, 4 * (tt + 1))
                sp.dma_start(out[tt * P:(tt + 1) * P, :], orow[:, tt, :]).then_inc(stored, 16)
            sp.wait_ge(stored, 32)

        @block.scalar
        def _(act):
            def split(u, i=0, n=0):
                if not under(u, i, n, N_UNITS) and isinstance(i, int):
                    return
                ring_waits(act, None, i, u, n, landed=True)
                act.activation(whi[:, u % RING, :], raw[:, u % RAW, :], ACT.Copy).then_inc(whi_ready, 1)

            def trip(ph, i, read_out):
                n = UNITS[ph]
                for j in range(n):
                    split(U0[ph] + j + LEAD, i, n)
                    chunk, _, ends = chunk_of(ph, j)
                    if ends and read_out:
                        read_out(i, chunk, U0[ph] + j, n)

            def stream(ph, read_out):
                if TRIPS[ph] <= 2:
                    for i in range(TRIPS[ph]):
                        trip(ph, i, read_out)
                else:
                    with act.Fori(0, TRIPS[ph]) as i:
                        trip(ph, i, read_out)

            def passed(u, tile, i, n):
                act.wait_ge(tile_pass, at(4 * u + tile, i, 4 * n))

            def tiles_to(dst_of, ready, func=ACT.Copy, T=TB):
                def read_out(i, chunk, u, n):
                    for t in range(4):
                        passed(u, t + 1, i, n)
                        act.activation(dst_of(i, chunk, t), bank[:, t, 0:T], func).then_inc(acc_free, 1)
                return read_out

            act.dma_start(ident[:, :], A["c_ident"]).then_inc(rows_in, 16)
            n_small = 0
            for name, rows in PARAMS:
                src = A[name]
                if name == "conv_w":
                    flat = src[0].rearrange("w (r c) -> (w r) c", c=P)
                elif name == "gla_gk_bias_2":
                    flat = src[0].rearrange("w (r c) -> (w r) c", c=P)
                else:
                    flat = src.rearrange("w (r c) -> (w r) c", c=P)
                r = 0
                while r < rows:
                    g, p0 = divmod(PAR[name] + r, P)
                    m = min(rows - r, P - p0)
                    act.dma_start(prow[p0:p0 + m, g, :], flat[r:r + m, :]).then_inc(small_in, 16)
                    n_small += 1
                    r += m
            for c, name in enumerate(("lam_q1", "lam_k1", "lam_q2", "lam_k2")):
                act.dma_start(lamv[:, c:c + 1], A[name].rearrange("a d -> d a")).then_inc(small_in, 16)
            sink_all = bass.AP(tensor=A["sinks"].tensor, offset=0, ap=[[0, P], [1, SW_HEADS]])
            act.dma_start(sinkb[:, :], sink_all).then_inc(small_in, 16)
            assert n_small + 5 == N_SMALL
            act.dma_start(tabx[0:N_BUCKETS, :], A["rel_bias_table"]).then_inc(hots_in, 16)
            act.dma_start(hots[:, 0, :], A["c_hot_full"]).then_inc(hots_in, 16)
            act.dma_start(hots[:, 1, :], A["c_hot_window"]).then_inc(hots_in, 16)
            for u in range(LEAD):
                split(u)
            for g in range(9):
                act.wait_ge(row_turned, g + 1)
                if g < 8:
                    tt, k = g // 4, 4 * (g % 4)
                    act.activation(xT[:, k:k + 4, tt * P:(tt + 1) * P],
                                   bank[:, g % 8, :].rearrange("p (k t) -> p k t", k=4), ACT.Copy).then_inc(row_taken, 1)
                else:
                    act.activation(xT[:, :, TB:T2], bank[:, g % 8, 0:KD * TM].rearrange("p (k t) -> p k t", k=KD),
                                   ACT.Copy).then_inc(row_taken, 1)
            act.wait_ge(lam_sum, 1)
            act.activation(lam[:, 0:2], bank[:, 6, 0:2], ACT.Exp).then_inc(lam_exp, 1)
            for w in range(2):
                act.wait_ge(line_sum, w + 1)
                act.activation(line[:, w, :], bank[0:N_HEADS, 4 + w, 0:LINE], ACT.Copy).then_inc(line_ready, 1)
            act.wait_ge(line_ready, 2)
            for w, h0, h1 in ((0, 0, DA_HEADS), (1, DA_HEADS, DA_HEADS + SW_HEADS), (0, DA_HEADS + SW_HEADS, N_HEADS)):
                act.dma_start(lines_dram[h0:h1, :, 0:LINE], line[h0:h1, w:w + 1, :].to_broadcast([h1 - h0, P, LINE]))\
                   .then_inc(lines_stored, 16)

            def root(use, T):
                act.wait_ge(inv_ready, use + 1)
                act.activation(rstd[:, 0:T], msq[:, 0:T], ACT.Sqrt).then_inc(rstd_ready, 1)

            def norm_before(b):
                T = T_PRE[b]
                for k in range(KD):
                    m = KD * b + k
                    if b == 0:
                        act.wait_ge(row_taken, 9)
                    else:
                        act.wait_ge(x_updated, KD * (b - 1) + k + 1)
                    if m >= 2:
                        act.wait_ge(sq_used, m - 1)
                    act.activation(sqb[:, k % 2, 0:T], xT[:, k, 0:T], ACT.Square).then_inc(sq_ready, 1)
                root(PRE(b), T)
                for k in range(KD):
                    act.wait_ge(h_ready, KD * b + k + 1)
                    act.activation(ha(ahi, k, 0, T), tmp[:, k % 2, 0:T], ACT.Copy).then_inc(hhi_ready, 1)

            norm_before(0)

            def qkv_out(i, chunk, u, n):
                if chunk < 2:
                    for t in range(4):
                        passed(u, t + 1, i, n)
                        dst = (qT, kT)[chunk][:, bass.ds(i * 4 + t, 1), :]
                        act.activation(dst, bank[:, t:t + 1, 0:TB], ACT.Copy).then_inc(acc_free, 1)
                else:
                    for tt in range(2):
                        passed(u, (1, 4)[tt], i, n)
                        act.activation(vtok[:, bass.ds(i * 2 + tt, 1), :], bank[:, tt:tt + 1, :], ACT.Copy)\
                           .then_inc(acc_free, (1, 3)[tt])

            stream("qkv", qkv_out)
            act.wait_ge(lines_stored, 48)
            stream("qb", tiles_to(lambda i, chunk, t: qbT[:, t, :], None))

            def kvb_out(i, chunk, u, n):
                passed(u, 1, i, n)
                act.activation(kbT[:, 0, :], bank[:, 0, 0:TB], ACT.Copy)
                act.activation(kbT[0:64, 1, :], bank[64:128, 0, 0:TB], ACT.Copy)
                act.activation(kbT[64:128, 1, :], bank[0:64, 0, 0:TB], ACT.Copy).then_inc(acc_free, 1)
                for tt in range(2):
                    passed(u, (2, 4)[tt], i, n)
                    ins = act.activation(vbtok[:, tt, :], bank[:, 1 + tt, 0:P], ACT.Copy)
                    ins.then_inc(acc_free, (1, 2)[tt])

            stream("kvb", kvb_out)

            for m in range(24 + 5):
                if m < 24:
                    if 8 <= m < 16:
                        act.wait_ge(max_sink, m - 8 + 1)
                    else:
                        act.wait_ge(max_ready, 2 * m + 2)
                    if m >= 4:
                        act.wait_ge(p_turned, job_of(m - 4) + 1)
                    for q, (c0, c1) in enumerate(((0, P), (P, 384))):
                        act.activation(prob[:, m % 4, c0:c1], sbias[:, m % 2, c0:c1], ACT.Exp, bias=nmax[:, m, q:q + 1],
                                       accum_out=ssum[:, m, q:q + 1]).then_inc(p_ready, 1)
                    if 8 <= m < 16:
                        act.activation(esink[:, m - 8, :], nmax[:, m, :], ACT.Exp, bias=sinkb[:, m - 8:m - 7])\
                           .then_inc(sink_ready, 1)
                if m >= 2 and ends_job(m - 2):
                    job = job_of(m - 2)
                    act.wait_ge(p_turned, job + 1)
                    if job >= 2:
                        act.wait_ge(o_ready, job - 1)
                    act.activation(probT[:, job % 2, :], bank[:, 6, 0:384], ACT.Copy).then_inc(pT_ready, 1)
                if m >= 4 and (m - 4) % 2 and m - 4 < 24:
                    unit = (m - 4) // 2
                    act.wait_ge(o_ready, job_of(m - 4) + 1)
                    if unit < DA_HEADS:
                        act.activation(osb[:, unit, :], bank[:, 7, 0:TB], ACT.Copy).then_inc(o_free, 1)
                    else:
                        act.activation(yhi[:, unit, :], bank[:, 7, 0:TB], ACT.Copy).then_inc(yhi_ready, 1)
            act.wait_ge(o_free, DA_HEADS)
            act.activation(osq[:, :, :], osb[:, :, :], ACT.Square).then_inc(a_squared, 1)
            act.wait_ge(a_inv, 1)
            act.activation(ors[:, :, :], ors[:, :, :], ACT.Sqrt).then_inc(a_rstd, 1)
            act.wait_ge(a_normed, 1)
            act.activation(yhi[:, 0:DA_HEADS, :], yn[:, :, :], ACT.Copy).then_inc(ya_hi, 1)

            act.wait_ge(o_free, 12)
            act.wait_ge(y_done, 1)

            def gates_out(i, chunk, u, n):
                for t in range(4):
                    passed(u, t + 1, i, n)
                    act.activation(gate[:, bass.ds(i * 4 + t, 1), :], bank[:, t:t + 1, 0:TB], ACT.Sigmoid,
                                   bias=par[:, bass.ds(i * 4 + (PAR["b_gate"] + t), 1)]).then_inc(acc_free, 1)

            stream("gates", gates_out)

            def mix_out(i, chunk, u, n):
                if chunk == 2:
                    for t in range(4):
                        act.wait_ge(mix_sum, at(t + 1, i, 4))
                        act.activation(ahi_tile(i, t), mixtmp[:, 0, t:t + 1, :], ACT.Copy).then_inc(mix_part, 1)

            stream("oabc", mix_out)

            def y_out(b):
                def read_out(i, chunk, u, n):
                    for t in range(4):
                        passed(u, t + 1, i, n)
                        dst = Y[b][:, bass.ds(i * 4 + t, 1), 0:T_POST[b]]
                        act.activation(dst, bank[:, t:t + 1, 0:T_POST[b]], ACT.Copy).then_inc(acc_free, 1)
                return read_out

            stream("wout", y_out(1))
            root(POST(1), TB)
            norm_before(1)

            def up_out(i, chunk, u, n):
                for t in range(4):
                    r = (t % 2) + (t // 2) * FT
                    passed(u, 2 * t - 2, i, n)
                    act.activation(cv[:, t, :], bank[:, t, 0:TB], ACT.Identity,
                                   bias=par[:, bass.ds(i * 2 + (PAR["conv_b"] + r), 1)],
                                   scale=par[:, bass.ds(i * 2 + (PAR["conv_w"] + 2 * 2 * FT + r), 1)]).then_inc(tap2, 1)
                for t in range(2):
                    act.wait_ge(acc_free, at(4 * C0["up"] + t + 1, i, 4))
                    act.activation(cv[:, t, :], cv[:, t, :], ACT.Gelu_apprx_tanh).then_inc(gelu_done, 1)
                for t in range(2):
                    act.wait_ge(ff_prod, at(t + 1, i, 2))
                    act.activation(ghi[:, bass.ds(i * 2 + t, 1), :], pr[:, t:t + 1, :], ACT.Copy).then_inc(ffhi_ready, 1)

            stream("up", up_out)
            stream("down", y_out(2))
            act.wait_ge(tile_pass, 4 * U0["aqk"])
            for t, name in ((cos, "c_cos"), (sin, "c_sin"), (turn, "c_turn")):
                act.dma_start(t[:, :], A[name]).then_inc(rope_in, 16)
            root(POST(2), TB)
            norm_before(2)

            stream("aqk", lambda i, chunk, u, n: [
                (passed(u, t + 1, i, n),
                 act.activation(qk2[:, bass.ds(i * 4 + t, 1), :], bank[:, t:t + 1, 0:T2], ACT.Copy).then_inc(acc_free, 1))
                for t in range(4)])

            def v2_out(i, chunk, u, n):
                for tt in range(3):
                    rows = (P, P, TM)[tt]
                    passed(u, (1, 2, 4)[tt], i, n)
                    act.activation(v2[0:rows, tt:tt + 1, bass.ds(i * 512, 512)], bank[0:rows, tt:tt + 1, :], ACT.Copy)\
                       .then_inc(acc_free, (1, 1, 2)[tt])

            stream("av", v2_out)

            def ag_out(i, chunk, u, n):
                for t in range(4):
                    passed(u, t + 1, i, n)
                    act.activation(gs2[:, bass.ds(i * 4 + t, 1), :], bank[:, t:t + 1, 0:T2], ACT.Silu).then_inc(acc_free, 1)

            stream("ag", ag_out)
            for n in range(24 + 1):
                if n < 24:
                    if n >= 2:
                        act.wait_ge(qk_sum, n - 1)
                    act.activation(sq2[:, n % 2, :], qk2[:, n, :], ACT.Square).then_inc(qk_sq, 1)
                if n >= 1:
                    act.wait_ge(qk_inv, n)
                    act.activation(rs2[:, (n - 1) % 2, :], rs2[:, (n - 1) % 2, :], ACT.Sqrt).then_inc(qk_rstd, 1)
            for h in range(AT_HEADS + 3):
                if h < AT_HEADS:
                    if h >= 2:
                        act.wait_ge(p2_turned, 3 * (h - 1))
                    for q in range(3):
                        rows = (P, P, TM)[q]
                        act.wait_ge(max2_ready, 3 * h + q + 1)
                        act.activation(p2[0:rows, h % 2, q, :], bank[0:rows, 4 + q, 0:T2], ACT.Exp,
                                       bias=nm2[0:rows, h, q:q + 1], accum_out=sum2[0:rows, h, q:q + 1])\
                           .then_inc(p2_ready, 1)
                if 1 <= h <= AT_HEADS:
                    hh = h - 1
                    if hh >= 2:
                        act.wait_ge(o2_ready, hh - 1)
                    for kt, rows in ((0, P), (2, TM)):
                        act.wait_ge(p2_turned, 3 * hh + kt + 1)
                        act.activation(pT2[0:rows, hh % 2, kt, :], bank[0:rows, kt % 2, 0:T2], ACT.Copy)\
                           .then_inc(pT2_act, 1)
                if h >= 3:
                    hh = h - 3
                    act.wait_ge(z2_ready, hh + 1)
                    act.activation(ha(ahi, hh, 0, T2), z2[:, hh % 2, :], ACT.Copy).then_inc(z2hi, 1)
            stream("aout", y_out(3))
            root(POST(3), T2)
            norm_before(3)

            act.wait_ge(h_ready, KD * 4)
            act.dma_start(park_dram, xT[:, :, :].rearrange("p k t -> p (k t)")).then_inc(x_parked, 16)
            for t, name in ((maskf, "c_mask_f"), (maskb, "c_mask_b"), (reset, "c_reset")):
                act.dma_start(t[:, :], A[name]).then_inc(gla_const, 16)
            act.dma_start(up_w[:, :, :], A["gla_gk_up_2"][0].rearrange("d r n -> r d n")).then_inc(gla_const, 16)

            def feature_out(dst, T, func):
                def read_out(i, chunk, u, n):
                    for t in range(4):
                        passed(u, t + 1, i, n)
                        act.activation(dst[:, bass.ds(i * 4 + t, 1), 0:T], bank[:, t:t + 1, 0:T], func).then_inc(acc_free, 1)
                return read_out

            stream("gqk", feature_out(gqk, T2, ACT.Copy))

            def v3_out(i, chunk, u, n):
                for tt in range(3):
                    rows = (P, P, TM)[tt]
                    passed(u, (1, 2, 4)[tt], i, n)
                    act.activation(v3[0:rows, tt:tt + 1, bass.ds(i * 512, 512)], bank[0:rows, tt:tt + 1, :], ACT.Copy)\
                       .then_inc(acc_free, (1, 1, 2)[tt])

            stream("gv", v3_out)
            stream("gg", feature_out(gg, TB, ACT.Silu))

            def lr_out(i, chunk, u, n):
                for d in range(2):
                    passed(u, (1, 4)[d], i, n)
                    act.activation(lrT[:, d, :], bank[0:GL_RANK, d, 0:T2], ACT.Copy).then_inc(acc_free, (1, 3)[d])

            stream("lr", lr_out)
            for grp in range(4 + 1):
                if grp < 4:
                    for t in range(4):
                        n = 4 * grp + t
                        act.wait_ge(z_sum, n + 1)
                        if grp >= 2:
                            act.wait_ge(z_sub, grp - 1)
                        act.activation(zabs[:, grp % 2, t, :], bank[:, 4 + t, 0:T2], ACT.Abs,
                                       bias=par[:, PAR["gla_gk_bias_2"] + n:PAR["gla_gk_bias_2"] + n + 1]).then_inc(z_abs, 1)
                if grp >= 1:
                    a = zabs[:, (grp - 1) % 2, :, :]
                    act.wait_ge(z_abs, 4 * grp)
                    act.activation(a, a, ACT.Exp, scale=-1.0).then_inc(z_exp, 1)
                    act.wait_ge(z_exp, grp)
                    act.activation(a, a, ACT.Ln, bias=1.0).then_inc(z_ln, 1)
            SC = 1.0 / GL_NORMALIZER
            for h in range(GL_HEADS):
                lf, lb = cum[:, 2 * h:2 * h + 2, :], cum[:, 8 + 2 * h:10 + 2 * h, 0:TB]
                act.wait_ge(cum_ready, 16)
                if h:
                    act.wait_ge(st_ready, 14 * h)
                act.activation(dec[:, 0, :, 0:4], lf[:, :, GL_CHUNK - 1:TB:GL_CHUNK], ACT.Exp, scale=SC).then_inc(e_dec, 1)
                act.activation(dec[:, 0, :, 4:5], lf[:, :, T2 - 1:T2], ACT.Exp, scale=SC).then_inc(e_dec, 1)
                act.activation(dec[:, 1, :, 0:4], lb[:, :, 0:TB:GL_CHUNK], ACT.Exp, scale=SC).then_inc(e_dec, 1)
                if h:
                    act.wait_ge(o3_part, h)
                for d, l in ((0, lf[:, :, 0:TB]), (1, lb)):
                    act.activation(kinv[:, d, :, :], l, ACT.Exp, scale=-SC).then_inc(e_k, 1)
                    act.activation(qdec[:, d, :, :], l, ACT.Exp, scale=SC).then_inc(e_q, 1)
                act.wait_ge(d_sub, 3 * h + 2)
                act.activation(kendf[:, :, :], kendf[:, :, :], ACT.Exp, scale=SC).then_inc(e_d, 1)
                act.wait_ge(d_sub, 3 * h + 3)
                act.activation(kendb[:, :, :], kendb[:, :, :], ACT.Exp, scale=SC).then_inc(e_d, 1)
                act.wait_ge(ke_turned, 3 * h + 1)
                act.activation(keT[:, 0, :, :], bank[:, 0, :].rearrange("p (t k) -> p t k", t=2), ACT.Copy).then_inc(ke_act, 1)
                act.wait_ge(ke_turned, 3 * h + 2)
                act.activation(keTm[:, :], bank[0:TM, 2, 0:GL_K], ACT.Copy).then_inc(ke_act, 1)
                act.wait_ge(o3_part, h + 1)
                if h:
                    act.wait_ge(act_ready, LO["z3"] + h)
                for c in range(2):
                    act.activation(osq3[:, 2 * c:2 * c + 2, :], bank[:, 6 + c, :].rearrange("p (v t) -> p v t", v=2),
                                   ACT.Square).then_inc(o3_sq, 1)
                act.wait_ge(o3_inv, h + 1)
                act.activation(rstd[:, 0:TB], msq[:, 0:TB], ACT.Sqrt).then_inc(o3_rstd, 1)
                act.wait_ge(z3_ready, h + 1)
                zhi = ahi[:, 0:KD * T2].rearrange("p (k t) -> p k t", t=T2)[:, 4 * h:4 * h + 4, 0:TB]
                act.activation(zhi, osq3[:, :, :], ACT.Copy).then_inc(z3hi, 1)
            with act.Fori(0, TRIPS["gout"] - 1) as i:
                trip("gout", i, y_out(4))
            trip("gout", TRIPS["gout"] - 1, y_out(4))
            root(POST(4), TB)
            for tt in range(2):
                for g in range(4):
                    act.wait_ge(out_turned, 4 * tt + g + 1)
                    act.activation(orow[:, tt, 512 * g:512 * g + 512], bank[:, 4 * tt + g, :], ACT.Copy)\
                       .then_inc(out_taken, 1)

        @block.vector
        def _(dve):
            def split(u, i=0, n=0):
                if not under(u, i, n, N_UNITS) and isinstance(i, int):
                    return
                dve.wait_ge(whi_ready, at(u + 1, i, n))
                dve.tensor_tensor(wlo[:, u % RING, :], raw[:, u % RAW, :], whi[:, u % RING, :].bitcast(F32),
                                  ALU.subtract).then_inc(wlo_ready, 1)

            def trip(ph, i, read_out=None):
                n = UNITS[ph]
                for j in range(n):
                    split(U0[ph] + j + LEAD, i, n)
                    chunk, _, ends = chunk_of(ph, j)
                    if ends and read_out:
                        read_out(i, chunk, U0[ph] + j, n)

            def stream(ph, read_out=None):
                if TRIPS[ph] <= 2:
                    for i in range(TRIPS[ph]):
                        trip(ph, i, read_out)
                else:
                    with dve.Fori(0, TRIPS[ph]) as i:
                        trip(ph, i, read_out)

            def column(name, k=0):
                return par[:, PAR[name] + k:PAR[name] + k + 1]

            dve.memset(ones[:, :], 1.0).then_inc(start_set, 1)
            dve.memset(tabx[N_BUCKETS:N_BUCKETS + 1, :], MASKED).then_inc(start_set, 1)
            for u in range(LEAD):
                split(u)
            dve.wait_ge(small_in, 16 * N_SMALL)
            dve.tensor_tensor(lamv[:, 4:5], lamv[:, 0:1], lamv[:, 1:2], ALU.mult).then_inc(lam_prod, 1)
            dve.tensor_tensor(lamv[:, 5:6], lamv[:, 2:3], lamv[:, 3:4], ALU.mult).then_inc(lam_prod, 1)
            dve.tensor_scalar(sinkn[:, :], sinkb[:, :], -1.0, None, ALU.mult).then_inc(lam_ready, 1)
            for g in range(PAR_GROUPS):
                m = min(P, N_PAR - g * P)
                dve.wait_ge(row_turned, 9 + g + 1)
                dve.tensor_copy(par[:, g * P:g * P + m], bank[:, (9 + g) % 8, 0:m]).then_inc(par_ready, 1)
            dve.wait_ge(lam_exp, 1)
            dve.tensor_tensor(lam[:, 2:3], lam[:, 1:2], lam[:, 0:1], ALU.subtract).then_inc(lam_ready, 1)
            dve.wait_ge(par_ready, PAR_GROUPS)
            dve.tensor_scalar(subg[:, :], column("subln"), 1.0 - LAM_INIT, None, ALU.mult).then_inc(lam_ready, 1)
            dve.tensor_scalar(qgain[:, :], column("attn_q_norm_2"), AT_HD ** -0.5, None, ALU.mult).then_inc(lam_ready, 1)
            dve.wait_ge(lam_ready, 2)
            dve.tensor_scalar(lam[:, 3:4], lam[:, 2:3], -LAM_INIT, None, ALU.add).then_inc(lam_ready, 1)

            def inverse(use, T, sums, width=D):
                dve.tensor_scalar(msq[:, 0:T], sums, 1.0 / width, EPS, ALU.mult, ALU.add).then_inc(mean_eps, 1)
                dve.wait_ge(mean_eps, use + 1)
                dve.reciprocal(msq[:, 0:T], msq[:, 0:T]).then_inc(inv_ready, 1)
                dve.wait_ge(rstd_ready, use + 1)

            def norm_before(b):
                T = T_PRE[b]
                dve.wait_ge(sq_used, KD * (b + 1))
                inverse(PRE(b), T, bank[:, 4, 0:T])
                for k in range(KD):
                    if k >= 2:
                        dve.wait_ge(act_ready, LO[f"norm{b}"] + k - 1)
                    dve.scalar_tensor_tensor(tmp[:, k % 2, 0:T], xT[:, k, 0:T], par[:, G_PRE[b] + k:G_PRE[b] + k + 1],
                                             rstd[:, 0:T], ALU.mult, ALU.mult).then_inc(h_ready, 1)

            def norm_after(b):
                T = T_POST[b]
                dve.wait_ge(mean_ready, b)
                inverse(POST(b), T, bank[:, 5, 0:T])
                if b == 4:
                    dve.wait_ge(x_back, 16)
                for k in range(KD + 1):
                    if k < KD:
                        if k >= 2:
                            dve.wait_ge(x_updated, KD * (b - 1) + k - 1)
                        dve.scalar_tensor_tensor(tmp[:, k % 2, 0:T], Y[b][:, k, 0:T],
                                                 par[:, G_POST[b] + k:G_POST[b] + k + 1], rstd[:, 0:T],
                                                 ALU.mult, ALU.mult).then_inc(y_scaled, 1)
                    if k >= 1:
                        dve.wait_ge(y_scaled, KD * (b - 1) + k)
                        dve.tensor_tensor(xT[:, k - 1, 0:T], xT[:, k - 1, 0:T], tmp[:, (k - 1) % 2, 0:T], ALU.add)\
                           .then_inc(x_updated, 1)

            norm_before(0)
            for ph in ("qkv", "qb", "kvb"):
                stream(ph)

            dve.wait_ge(bias_in, 16)
            for m in range(24 + 5):
                if m < 24:
                    head = m // 2 if m < 8 else m - 8 + DA_HEADS
                    dve.wait_ge(s_ready, m + 1)
                    if m >= 2:
                        dve.wait_ge(p_ready, 2 * m - 2)
                    dve.scalar_tensor_tensor(sbias[:, m % 2, 0:P], bank[:, 4 + m % 2, 0:P], HD ** -0.5,
                                             bias[:, head, P:TB], ALU.mult, ALU.add).then_inc(s_biased, 1)
                    dve.scalar_tensor_tensor(sbias[:, m % 2, P:384], bank[:, 4 + m % 2, P:384], HD ** -0.5,
                                             bias[:, head, :], ALU.mult, ALU.add).then_inc(s_biased, 1)
                    for q, (c0, c1) in enumerate(((0, P), (P, 384))):
                        dve.wait_ge(s_biased, 2 * m + q + 1)
                        dve.tensor_reduce(nmax[:, m, q:q + 1], sbias[:, m % 2, c0:c1], AX.X, ALU.max, negate=True)\
                           .then_inc(max_ready, 1)
                    if 8 <= m < 16:
                        dve.wait_ge(max_ready, 2 * m + 2)
                        dve.tensor_scalar(nmax[:, m, :], nmax[:, m, :], sinkn[:, m - 8:m - 7], None, ALU.min)\
                           .then_inc(max_sink, 1)
                if 1 <= m <= 24:
                    mm = m - 1
                    dve.wait_ge(p_ready, 2 * mm + 2)
                    if 8 <= mm < 16:
                        dve.wait_ge(sink_ready, mm - 8 + 1)
                        dve.tensor_tensor(ssum[:, mm, :], ssum[:, mm, :], esink[:, mm - 8, :], ALU.add).then_inc(sum_sink, 1)
                        dve.wait_ge(sum_sink, mm - 8 + 1)
                    dve.reciprocal(ssum[:, mm, :], ssum[:, mm, :]).then_inc(inv_sum, 1)
                    dve.wait_ge(inv_sum, mm + 1)
                    cols = ((0, P), (P, 384))
                    if mm >= 8:
                        for q, (c0, c1) in enumerate(cols):
                            dve.tensor_scalar(prob[:, mm % 4, c0:c1], prob[:, mm % 4, c0:c1], ssum[:, mm, q:q + 1], None,
                                              ALU.mult).then_inc(p_scaled, 1)
                    elif mm % 2:
                        dve.tensor_scalar(ssum[:, mm, :], ssum[:, mm, :], lam[:, 3:4], None, ALU.mult).then_inc(p_second, 1)
                        dve.wait_ge(p_second, 3 * (mm // 2) + 1)
                        for q, (c0, c1) in enumerate(cols):
                            dve.tensor_scalar(prob[:, mm % 4, c0:c1], prob[:, mm % 4, c0:c1], ssum[:, mm, q:q + 1], None,
                                              ALU.mult).then_inc(p_second, 1)
                        for q, (c0, c1) in enumerate(cols):
                            dve.wait_ge(p_second, 3 * (mm // 2) + 2 + q)
                            dve.scalar_tensor_tensor(prob[:, (mm - 1) % 4, c0:c1], prob[:, (mm - 1) % 4, c0:c1],
                                                     ssum[:, mm - 1, q:q + 1], prob[:, mm % 4, c0:c1], ALU.mult, ALU.add)\
                               .then_inc(p_scaled, 1)
                if m >= 4 and (m - 4) % 2 and (m - 4) // 2 >= DA_HEADS:
                    unit = (m - 4) // 2
                    dve.wait_ge(yhi_ready, unit - DA_HEADS + 1)
                    dve.tensor_tensor(ylo[:, unit, :], bank[:, 7, 0:TB], yhi[:, unit, :].bitcast(F32), ALU.subtract)\
                       .then_inc(o_free, 1)
            for c in range(2):
                dve.wait_ge(a_summed, c + 1)
                dve.tensor_scalar(ors[:, 2 * c:2 * c + 2, :], bank[:, 4 + c, :].rearrange("p (h t) -> p h t", h=2), 1.0 / P,
                                  EPS, ALU.mult, ALU.add).then_inc(a_mean, 1)
            dve.wait_ge(a_mean, 2)
            dve.reciprocal(ors[:, :, :], ors[:, :, :]).then_inc(a_inv, 1)
            dve.wait_ge(a_rstd, 1)
            dve.scalar_tensor_tensor(yn[:, :, :], osb[:, :, :], subg[:, 0:1], ors[:, :, :], ALU.mult, ALU.mult)\
               .then_inc(a_normed, 1)

            stream("gates")

            def mix_out(i, chunk, u, n):
                c = C0["oabc"] + chunk
                for t in range(4):
                    dve.wait_ge(tile_pass, at(4 * u + t + 1, i, 4 * n))
                    if chunk == 0:
                        dve.wait_ge(act_ready, at(LO["mix"], i, 4))
                    dst = mixtmp[:, min(chunk, 1), t:t + 1, :]
                    dve.tensor_tensor(dst, bank[:, t:t + 1, 0:TB], gate[:, bass.ds(i * 4 + (KD * chunk + t), 1), :],
                                      ALU.mult).then_inc(acc_free, 1)
                if chunk:
                    for t in range(4):
                        dve.wait_ge(acc_free, at(4 * c + t + 1, i, 12))
                        if chunk == 2:
                            dve.wait_ge(mix_two, at(t + 1, i, 4))
                        dve.tensor_tensor(mixtmp[:, 0, t, :], mixtmp[:, 0, t, :], mixtmp[:, 1, t, :], ALU.add)\
                           .then_inc((mix_two, mix_sum)[chunk - 1], 1)

            stream("oabc", mix_out)
            stream("wout")
            norm_after(1)
            norm_before(1)

            def up_out(i, chunk, u, n):
                for t in range(4):
                    r = (t % 2) + (t // 2) * FT
                    for back in (1, 2):
                        dve.wait_ge(*((tap2, at(t + 1, i, 4)) if back == 1 else (tap1, at(t + 1, i, 4))))
                        tap = par[:, bass.ds(i * 2 + (PAR["conv_w"] + (2 - back) * 2 * FT + r), 1)]
                        dve.scalar_tensor_tensor(cv[:, t, back:TB], bank[:, t, 0:TB - back], tap, cv[:, t, back:TB],
                                                 ALU.mult, ALU.add).then_inc((tap1, acc_free)[back - 1], 1)
                for t in range(2):
                    dve.wait_ge(gelu_done, at(t + 1, i, 2))
                    dve.wait_ge(acc_free, at(4 * C0["up"] + t + 3, i, 4))
                    dve.wait_ge(act_ready, at(LO["ff"], i, 2))
                    dve.tensor_tensor(pr[:, t, :], cv[:, t, :], cv[:, 2 + t, :], ALU.mult).then_inc(ff_prod, 1)

            stream("up", up_out)
            stream("down")
            norm_after(2)
            norm_before(2)
            for ph in ("aqk", "av", "ag"):
                stream(ph)

            for n in range(24 + 2):
                if n < 24:
                    dve.wait_ge(qk_sum, n + 1)
                    dve.tensor_scalar(rs2[:, n % 2, :], bank[:, 4 + n % 2, 0:T2], 1.0 / AT_HD, EPS, ALU.mult, ALU.add)\
                       .then_inc(qk_mean, 1)
                    dve.wait_ge(qk_mean, n + 1)
                    dve.reciprocal(rs2[:, n % 2, :], rs2[:, n % 2, :]).then_inc(qk_inv, 1)
                if 1 <= n <= 24:
                    k = n - 1
                    dve.wait_ge(qk_rstd, k + 1)
                    if k >= 2:
                        dve.wait_ge(qk_turned, k - 1)
                        dve.wait_ge(qk_cos, k - 1)
                    gain = qgain[:, 0:1] if k < AT_HEADS else column("attn_k_norm_2")
                    dve.scalar_tensor_tensor(n2[:, k % 2, :], qk2[:, k, :], gain, rs2[:, k % 2, :], ALU.mult, ALU.mult)\
                       .then_inc(qk_normed, 1)
                if n >= 2:
                    k = n - 2
                    if k == 0:
                        dve.wait_ge(rope_in, 48)
                    dve.wait_ge(qk_turned, k + 1)
                    dve.tensor_tensor(qk2[:, k, :], bank[:, 6 + k % 2, 0:T2], sin[:, :], ALU.mult).then_inc(qk_sin, 1)
                    dve.wait_ge(qk_sin, k + 1)
                    dve.wait_ge(qk_cos, k + 1)
                    dve.tensor_tensor(qk2[:, k, :], qk2[:, k, :], nc2[:, k % 2, :], ALU.add).then_inc(qk_done, 1)
            for h in range(AT_HEADS + 3):
                if h < AT_HEADS:
                    for q in range(3):
                        rows = (P, P, TM)[q]
                        dve.wait_ge(s2_ready, 3 * h + q + 1)
                        dve.tensor_reduce(nm2[0:rows, h, q:q + 1], bank[0:rows, 4 + q, 0:T2], AX.X, ALU.max, negate=True)\
                           .then_inc(max2_ready, 1)
                if 1 <= h <= AT_HEADS:
                    hh = h - 1
                    dve.wait_ge(p2_ready, 3 * hh + 3)
                    dve.reciprocal(sum2[:, hh, 0:2], sum2[:, hh, 0:2]).then_inc(inv2, 1)
                    dve.reciprocal(sum2[0:TM, hh, 2:3], sum2[0:TM, hh, 2:3]).then_inc(inv2, 1)
                    dve.wait_ge(inv2, 2 * hh + 2)
                    for q in range(3):
                        rows = (P, P, TM)[q]
                        dve.tensor_scalar(p2[0:rows, hh % 2, q, :], p2[0:rows, hh % 2, q, :], sum2[0:rows, hh, q:q + 1],
                                          None, ALU.mult).then_inc(p2_scaled, 1)
                    dve.wait_ge(p2_turned, 3 * hh + 2)
                    if hh >= 2:
                        dve.wait_ge(o2_ready, hh - 1)
                    dve.tensor_copy(pT2[:, hh % 2, 1, :], bank[:, 1, 0:T2]).then_inc(pT2_dve, 1)
                if h >= 3:
                    hh = h - 3
                    dve.wait_ge(o2_ready, hh + 1)
                    if hh >= 2:
                        dve.wait_ge(act_ready, LO["z2"] + hh - 1)
                    dve.tensor_tensor(z2[:, hh % 2, :], bank[:, 2 + hh % 2, 0:T2], gs2[:, hh, :], ALU.mult)\
                       .then_inc(z2_ready, 1)
            stream("aout")
            norm_after(3)
            norm_before(3)
            for ph in ("gqk", "gv", "gg", "lr"):
                stream(ph)

            dve.wait_ge(x_parked, 16)
            dve.wait_ge(gla_const, 64)
            for grp in range(4 + 1):
                if grp < 4:
                    for t in range(4):
                        n = 4 * grp + t
                        dve.wait_ge(z_abs, n + 1)
                        dve.tensor_scalar(cum[:, n, :], bank[:, 4 + t, 0:T2], column("gla_gk_bias_2", n), 0.0, ALU.add,
                                          ALU.min).then_inc(z_min, 1)
                if grp >= 1:
                    g0 = 4 * (grp - 1)
                    dve.wait_ge(z_ln, grp)
                    dve.wait_ge(z_min, 4 * grp)
                    dve.tensor_tensor(cum[:, g0:g0 + 4, :], cum[:, g0:g0 + 4, :], zabs[:, (grp - 1) % 2, :, :], ALU.subtract)\
                       .then_inc(z_sub, 1)
                    dve.wait_ge(z_sub, grp)
                    for n in range(g0, g0 + 4):
                        if n < KT:
                            dve.tensor_tensor_scan(cum[:, n, :], reset[:, :], cum[:, n, :], 0.0, ALU.mult, ALU.add)\
                               .then_inc(cum_ready, 1)
                        else:
                            back = cum[:, n, 0:TB][:, ::-1]
                            dve.tensor_tensor_scan(back, reset[:, 0:TB], back, 0.0, ALU.mult, ALU.add).then_inc(cum_ready, 1)

            def spread(ap, n):
                return bass.AP(tensor=ap.tensor, offset=ap.offset, ap=[list(d) for d in ap.ap] + [[0, n]])

            for h in range(GL_HEADS):
                lf, lb = cum[:, 2 * h:2 * h + 2, :], cum[:, 8 + 2 * h:10 + 2 * h, 0:TB]
                chunks = "p k (c t) -> p k c t"
                dve.wait_ge(cum_ready, 16)
                if h:
                    dve.wait_ge(ke_turned, 3 * h)
                dve.tensor_tensor(kendf[:, :, 0:TB].rearrange(chunks, t=GL_CHUNK),
                                  spread(lf[:, :, GL_CHUNK - 1:TB:GL_CHUNK], GL_CHUNK),
                                  lf[:, :, 0:TB].rearrange(chunks, t=GL_CHUNK), ALU.subtract).then_inc(d_sub, 1)
                dve.tensor_tensor(kendf[:, :, TB:T2], lf[:, :, T2 - 1:T2].to_broadcast([P, 2, TM]), lf[:, :, TB:T2],
                                  ALU.subtract).then_inc(d_sub, 1)
                dve.tensor_tensor(kendb[:, :, :].rearrange(chunks, t=GL_CHUNK), spread(lb[:, :, 0:TB:GL_CHUNK], GL_CHUNK),
                                  lb.rearrange(chunks, t=GL_CHUNK), ALU.subtract).then_inc(d_sub, 1)
                for d in range(2):
                    dve.wait_ge(e_q, 2 * h + d + 1)
                    dve.scalar_tensor_tensor(qdec[:, d, :, :], qdec[:, d, :, :], GL_K ** -0.5, gqk[:, 2 * h:2 * h + 2, 0:TB],
                                             ALU.mult, ALU.mult).then_inc(q_dec, 1)
                dve.wait_ge(ke_turned, 3 * h + 3)
                dve.tensor_copy(keT[:, 1, :, :], bank[:, 1, :].rearrange("p (t k) -> p t k", t=2)).then_inc(ke_dve, 1)
                for d, (dst, mask) in enumerate(((sc[:, :, :], maskf), (tmp[:, 0, 0:TB].rearrange("p (t c) -> p t c", t=2),
                                                                         maskb))):
                    dve.wait_ge(sc_sum, 2 * h + d + 1)
                    both = bass.AP(tensor=mask[:, :].tensor, offset=mask[:, :].offset,
                                   ap=[list(mask[:, :].ap[0]), [0, 2], list(mask[:, :].ap[1])])
                    dve.tensor_tensor(dst, bank[:, 2 + d, 0:TB].rearrange("p (t c) -> p t c", t=2), both, ALU.mult)\
                       .then_inc(sc_part, 1)
                dve.wait_ge(sc_part, 2 * h + 2)
                dve.tensor_tensor(sc[:, :, :], sc[:, :, :], tmp[:, 0, 0:TB].rearrange("p (t c) -> p t c", t=2), ALU.add)\
                   .then_inc(sc_ready, 1)
                dve.wait_ge(e_dec, 3 * h + 3)
                for s in range(7):
                    d, k = s % 2, s // 2
                    st = (stf, stb)[d]
                    added = (k - 1, 3 - k)[d]
                    for f in range(2):
                        dve.wait_ge(ds_ready, 14 * h + 2 * s + f + 1)
                        if k == 0:
                            dve.tensor_copy(st[:, 0, f, :], bank[:, 4 + f, :]).then_inc(st_ready, 1)
                        else:
                            dve.wait_ge(st_ready, 14 * h + 2 * (s - 2) + f + 1)
                            dve.scalar_tensor_tensor(st[:, k % 2, f, :], st[:, (k - 1) % 2, f, :],
                                                     dec[:, d, f, added:added + 1], bank[:, 4 + f, :], ALU.mult, ALU.add)\
                               .then_inc(st_ready, 1)
                dve.wait_ge(o3_sum, h + 1)
                dve.tensor_scalar(msq[:, 0:TB], bank[:, 3, 0:TB], 1.0 / GL_V, EPS, ALU.mult, ALU.add).then_inc(o3_mean, 1)
                dve.wait_ge(o3_mean, h + 1)
                dve.reciprocal(msq[:, 0:TB], msq[:, 0:TB]).then_inc(o3_inv, 1)
                dve.wait_ge(o3_rstd, h + 1)
                for v in range(4):
                    dve.scalar_tensor_tensor(osq3[:, v, :], bank[:, 6 + v // 2, (v % 2) * TB:(v % 2 + 1) * TB],
                                             column("gla_o_norm_2", v), rstd[:, 0:TB], ALU.mult, ALU.mult)\
                       .then_inc(o3_scaled, 1)
                dve.wait_ge(o3_scaled, 4 * h + 4)
                dve.tensor_tensor(osq3[:, :, :], osq3[:, :, :], gg[:, 4 * h:4 * h + 4, :], ALU.mult).then_inc(z3_ready, 1)
            with dve.Fori(0, TRIPS["gout"] - 1) as i:
                trip("gout", i)
            trip("gout", TRIPS["gout"] - 1)
            norm_after(4)

        @block.tensor
        def _(pe):
            PASSES = ((0, 0), (0, 1), (1, 0))

            def unit_begin(ph, i, j):
                n = UNITS[ph]
                u = U0[ph] + j
                pe.wait_ge(wlo_ready, at(u + 1, i, n))
                chunk, begins, ends = chunk_of(ph, j)
                return u, C0[ph] + chunk, begins, ends

            def bank_free(ph, c, t, i):
                if not under(c, i, CHUNKS[ph], 1):
                    pe.wait_ge(acc_free, at(4 * (c - 1) + t + 1, i, 4 * CHUNKS[ph]))

            def features(ph, i, j, rhs, T):
                u, c, begins, ends = unit_begin(ph, i, j)
                k0, nk = unit_tiles(ph, j)
                w = [t[:, u % RING, :].rearrange("p (k n) -> p k n", k=2 if nk == 1 else nk) for t in (whi, wlo)]
                of_unit = (0, 1, 2, 3)
                if ph == "up":
                    of_unit, begins, ends = ((0, 1), (2, 3))[j % 2], j < 2, j > 5
                for t in of_unit:
                    col = t * P if ph != "up" else (t % 2) * P
                    if begins:
                        bank_free(ph, c, t, i)
                    for k in range(nk):
                        for wp, ap in PASSES:
                            mm = pe.matmul(bank[:, t, 0:T], w[wp][:, k, col:col + P], rhs(ap, k0 + k),
                                           start=begins and k == 0 and (wp, ap) == (0, 0),
                                           stop=ends and k == nk - 1 and wp == 1)
                    mm.then_inc(tile_pass, 4 // len(of_unit))

            def tokens(ph, i, j, n_tiles, passes, first_bank=0, cols=(0, 512), begun=None):
                u, c, begins, ends = unit_begin(ph, i, j) if begun is None else begun
                k0, nk = unit_tiles(ph, j)
                w = [t[:, u % RING, :].rearrange("p (k n) -> p k n", k=nk) for t in (whi, wlo)]
                for tt in range(n_tiles):
                    if begins:
                        bank_free(ph, c, first_bank + tt, i)
                    for k in range(nk):
                        for wp, ap in PASSES:
                            mm = pe.matmul(bank[:, first_bank + tt, 0:cols[1] - cols[0]], ha((ahi, alo)[ap], k0 + k, tt * P, P),
                                           w[wp][:, k, cols[0]:cols[1]],
                                           start=begins and k == 0 and (wp, ap) == (0, 0),
                                           stop=ends and k == nk - 1 and wp == 1)
                    mm.then_inc(tile_pass, passes[tt])

            def model(T):
                return lambda part, k: ha((ahi, alo)[part], k, 0, T)

            def feature_stream(ph, T, made=None, per_unit=2, base=0, rhs=None):
                with pe.Fori(0, TRIPS[ph]) as i:
                    for j in range(UNITS[ph]):
                        if made is not None:
                            pe.wait_ge(made, base + per_unit * (j + 1))
                        features(ph, i, j, rhs or model(T), T)

            pe.wait_ge(rows_in, 64)
            for g in range(8):
                tt, k = g // 4, 4 * (g % 4)
                for n in range(4):
                    mm = pe.transpose(bank[:, g % 8, n * P:(n + 1) * P], xrow[:, tt, (k + n) * P:(k + n + 1) * P], ident[:, :])
                mm.then_inc(row_turned, 1)
            pe.wait_ge(row_taken, 1)
            for k in range(KD):
                mm = pe.transpose(bank[:, 0, k * TM:(k + 1) * TM], mrow[:, k * P:(k + 1) * P], ident[0:TM, 0:TM])
            mm.then_inc(row_turned, 1)
            pe.wait_ge(small_in, 16 * N_SMALL)
            for g in range(PAR_GROUPS):
                m = min(P, N_PAR - g * P)
                pe.wait_ge(row_taken, (9 + g) - 8 + 1)
                pe.transpose(bank[:, (9 + g) % 8, 0:m], prow[0:m, g, :], ident[0:m, 0:m]).then_inc(row_turned, 1)
            pe.wait_ge(lam_prod, 2)
            pe.wait_ge(start_set, 2)
            pe.wait_ge(row_taken, 7)
            pe.matmul(bank[:, 6, 0:2], ones[0:HD, :], lamv[:, 4:6], start=True, stop=True).then_inc(lam_sum, 1)
            pe.wait_ge(hots_in, 48)
            pe.wait_ge(par_ready, PAR_GROUPS)
            for w in range(2):
                pe.matmul(bank[0:N_HEADS, 4 + w, 0:LINE], tabx[:, :], hots[:, w, :], start=True, stop=True).then_inc(line_sum, 1)

            def norm_before(b):
                T = T_PRE[b]
                if b == 0:
                    pe.wait_ge(line_ready, 2)
                for k in range(KD):
                    pe.wait_ge(sq_ready, KD * b + k + 1)
                    pe.matmul(bank[:, 4, 0:T], ones[:, :], sqb[:, k % 2, 0:T], start=k == 0, stop=k == KD - 1).then_inc(sq_used, 1)

            def norm_after(b):
                T = T_POST[b]
                pe.wait_ge(y_summed, (KD + 1) * b)
                pe.matmul(bank[:, 5, 0:T], ones[:, :], sqacc[:, 0:T], start=True, stop=True).then_inc(mean_ready, 1)

            norm_before(0)
            pe.wait_ge(spare_set, 2)
            for i in range(TRIPS["qkv"]):
                for j in range(UNITS["qkv"]):
                    if j < 8:
                        pe.wait_ge(act_ready, 2 * j + 2)
                    if j < 16:
                        features("qkv", i, j, model(TB), TB)
                    else:
                        tokens("qkv", i, j, 2, (1, 3))
            for j in range(UNITS["qb"]):
                features("qb", 0, j, model(TB), TB)
            for j in range(UNITS["kvb"]):
                unit = unit_begin("kvb", 0, j)
                u, c, begins, ends = unit
                k0, nk = unit_tiles("kvb", j)
                w = [t[:, u % RING, :].rearrange("p (k n) -> p k n", k=nk) for t in (whi, wlo)]
                if begins:
                    bank_free("kvb", c, 0, 0)
                for k in range(nk):
                    for wp, ap in PASSES:
                        mm = pe.matmul(bank[:, 0, 0:TB], w[wp][:, k, 0:P], ha((ahi, alo)[ap], k0 + k, 0, TB),
                                       start=begins and k == 0 and (wp, ap) == (0, 0), stop=ends and k == nk - 1 and wp == 1)
                mm.then_inc(tile_pass, 1)
                tokens("kvb", 0, j, 2, (1, 2), first_bank=1, cols=(P, 2 * P), begun=unit)

            pe.wait_ge(acc_free, 4 * (C0["kvb"] + 1))
            for m in range(24 + 4):
                if m < 24:
                    r = 64 * (m % 2)
                    if m < 8:
                        q, k = qT[r:r + 64, m // 2, :], kT[r:r + 64, m // 2, :]
                    elif m < 16:
                        q, k = qbT[r:r + 64, (m - 8) // 2, :], kbT[r:r + 64, int((m - 8) // 4 != m % 2), :]
                    else:
                        q, k = qT[r:r + 64, 4 + (m - 16) // 2, :], kT[r:r + 64, 4 + (m - 16) // 2, :]
                    if m >= 2:
                        pe.wait_ge(s_biased, 2 * (m - 1))
                    pe.matmul(bank[:, 4 + m % 2, 0:P], q[:, 0:P], k[:, 0:P], start=True, stop=True)
                    pe.matmul(bank[:, 4 + m % 2, P:384], q[:, P:TB], k[:, :], start=True, stop=True).then_inc(s_ready, 1)
                if m >= 2 and ends_job(m - 2):
                    mm_, job = m - 2, job_of(m - 2)
                    src = prob[:, (mm_ if mm_ >= 8 else mm_ - 1) % 4, :]
                    pe.wait_ge(p_scaled, 2 * job + 2)
                    if job >= 1:
                        pe.wait_ge(pT_ready, job)
                    for c in range(3):
                        mm = pe.transpose(bank[:, 6, c * P:(c + 1) * P], src[:, c * P:(c + 1) * P], ident[:, :])
                    mm.then_inc(p_turned, 1)
                if m >= 3 and ends_job(m - 3):
                    mm_, job = m - 3, job_of(m - 3)
                    unit = mm_ // 2
                    pe.wait_ge(pT_ready, job + 1)
                    if mm_ < 8 or mm_ % 2 == 0:
                        pe.wait_ge(o_free, unit)
                    if mm_ < 8:
                        o, v = bank[:, 7, 0:TB], [vtok[:, tt, P * unit:P * unit + P] for tt in range(2)]
                    else:
                        r = 64 * (mm_ % 2)
                        o = bank[r:r + 64, 7, 0:TB]
                        if mm_ < 16:
                            kv = (mm_ - 8) // 4
                            v = [vbtok[:, tt, 64 * kv:64 * kv + 64] for tt in range(2)]
                        else:
                            v = [vtok[:, 2 + tt, 64 * (mm_ - 16):64 * (mm_ - 16) + 64] for tt in range(2)]
                    pe.matmul(o, v[0], probT[:, job % 2, 0:TB], start=True, stop=False)
                    pe.matmul(o[:, P:TB], v[1], probT[:, job % 2, TB:384], start=False, stop=True).then_inc(o_ready, 1)
            pe.wait_ge(a_squared, 1)
            pe.wait_ge(s_biased, 48)
            for c in range(2):
                pe.matmul(bank[:, 4 + c, :], ones[:, :], osq[:, 2 * c:2 * c + 2, :].rearrange("p h t -> p (h t)"),
                          start=True, stop=True).then_inc(a_summed, 1)

            feature_stream("gates", TB)
            pe.wait_ge(o_free, 12)
            pe.wait_ge(y_done, 1)
            with pe.Fori(0, TRIPS["oabc"]) as i:
                for j in range(UNITS["oabc"]):
                    branch = chunk_of("oabc", j)[0]
                    features("oabc", i, j, lambda part, k: (yhi, ylo)[part][:, 4 * branch + k, :], TB)
            feature_stream("wout", TB, act_ready, 2, LO["mix"])
            norm_after(1)
            norm_before(1)
            with pe.Fori(0, TRIPS["up"]) as i:
                for j in range(UNITS["up"]):
                    pe.wait_ge(act_ready, LO["norm1"] + 4 * (j // 2) + 4)
                    features("up", i, j, model(TB), TB)
            pe.wait_ge(act_ready, LO["ff"] + FT)
            feature_stream("down", TB, rhs=lambda part, k: (ghi, glo)[part][:, k, :])
            norm_after(2)
            norm_before(2)
            feature_stream("aqk", T2, act_ready, 2, LO["norm2"])
            for i in range(TRIPS["av"]):
                for j in range(UNITS["av"]):
                    tokens("av", i, j, 3, (1, 1, 2))
            feature_stream("ag", T2)

            pe.wait_ge(acc_free, 4 * (C0["ag"] + TRIPS["ag"]))
            pe.wait_ge(rope_in, 48)
            for n in range(24 + 2):
                if n < 24:
                    pe.wait_ge(qk_sq, n + 1)
                    if n >= 2:
                        pe.wait_ge(qk_mean, n - 1)
                    pe.matmul(bank[:, 4 + n % 2, 0:T2], ones[:, :], sq2[:, n % 2, :], start=True, stop=True).then_inc(qk_sum, 1)
                if 1 <= n <= 24:
                    k = n - 1
                    pe.wait_ge(qk_normed, k + 1)
                    if k >= 2:
                        pe.wait_ge(qk_sin, k - 1)
                    pe.matmul(bank[:, 6 + k % 2, 0:T2], turn[:, :], n2[:, k % 2, :], start=True, stop=True).then_inc(qk_turned, 1)
            pe.wait_ge(qk_done, 24)
            TOK = ((0, P), (P, P), (TB, TM))
            for h in range(AT_HEADS + 2):
                if h < AT_HEADS:
                    for q, (c0, rows) in enumerate(TOK):
                        if h:
                            pe.wait_ge(p2_ready, 3 * (h - 1) + q + 1)
                        pe.matmul(bank[0:rows, 4 + q, 0:T2], qk2[:, h, c0:c0 + rows], qk2[:, AT_HEADS + h // 2, :],
                                  start=True, stop=True).then_inc(s2_ready, 1)
                if 1 <= h <= AT_HEADS:
                    hh = h - 1
                    pe.wait_ge(p2_scaled, 3 * hh + 3)
                    for kt, (k0, krows) in enumerate(TOK):
                        if kt == 0 and hh:
                            pe.wait_ge(pT2_act, 2 * hh)
                        if kt == 1 and hh:
                            pe.wait_ge(pT2_dve, hh)
                        if kt == 2:
                            pe.wait_ge(pT2_act, 2 * hh + 1)
                        for q, (c0, rows) in enumerate(TOK):
                            mm = pe.transpose(bank[0:krows, kt % 2, c0:c0 + rows], p2[0:rows, hh % 2, q, k0:k0 + krows],
                                              ident[0:rows, 0:rows])
                        mm.then_inc(p2_turned, 1)
                if h >= 2:
                    hh = h - 2
                    kv = hh // 2
                    pe.wait_ge(pT2_act, 2 * hh + 2)
                    pe.wait_ge(pT2_dve, hh + 1)
                    if hh >= 2:
                        pe.wait_ge(z2_ready, hh - 1)
                    for kt, (k0, krows) in enumerate(TOK):
                        mm = pe.matmul(bank[:, 2 + hh % 2, 0:T2], v2[0:krows, kt, kv * P:(kv + 1) * P],
                                       pT2[0:krows, hh % 2, kt, :], start=kt == 0, stop=kt == 2)
                    mm.then_inc(o2_ready, 1)
            pe.wait_ge(z2_ready, AT_HEADS)
            feature_stream("aout", T2, act_ready, 2, LO["z2"])
            norm_after(3)
            norm_before(3)
            feature_stream("gqk", T2, act_ready, 2, LO["norm3"])
            with pe.Fori(0, TRIPS["gv"]) as i:
                for j in range(UNITS["gv"]):
                    tokens("gv", i, j, 3, (1, 1, 2))
            feature_stream("gg", TB)
            u, c, _, _ = unit_begin("lr", 0, 0)
            for d in range(2):
                bank_free("lr", c, d, 0)
                for k in range(KD):
                    col = (2 * k + d) * GL_RANK
                    for wp, ap in PASSES:
                        mm = pe.matmul(bank[:, d, 0:T2], (whi, wlo)[wp][:, u % RING, col:col + P], ha((ahi, alo)[ap], k, 0, T2),
                                       start=k == 0 and (wp, ap) == (0, 0), stop=k == KD - 1 and wp == 1)
                mm.then_inc(tile_pass, (1, 3)[d])

            pe.wait_ge(acc_free, 4 * (C0["lr"] + 1))
            pe.wait_ge(gla_const, 64)
            for n in range(16):
                d, k = divmod(n, KT)
                if n >= 4:
                    pe.wait_ge(z_min, n - 3)
                pe.matmul(bank[:, 4 + n % 4, 0:T2], up_w[:, d, k * P:(k + 1) * P], lrT[:, d, :], start=True, stop=True)\
                  .then_inc(z_sum, 1)
            pe.wait_ge(z_min, 16)
            for h in range(GL_HEADS):
                pe.wait_ge(k_end, 2 * h + 1)
                if h:
                    pe.wait_ge(ke_act, 2 * h)
                for tt in range(2):
                    for f in range(2):
                        mm = pe.transpose(bank[:, 0, tt * GL_K + f * P:tt * GL_K + (f + 1) * P],
                                          kendf[:, f, tt * P:(tt + 1) * P], ident[:, :])
                mm.then_inc(ke_turned, 1)
                if h:
                    pe.wait_ge(sc_part, 2 * h)
                for f in range(2):
                    mm = pe.transpose(bank[0:TM, 2, f * P:(f + 1) * P], kendf[:, f, TB:T2], ident[:, :])
                mm.then_inc(ke_turned, 1)
                pe.wait_ge(k_end, 2 * h + 2)
                if h:
                    pe.wait_ge(ke_dve, h)
                for tt in range(2):
                    for f in range(2):
                        mm = pe.transpose(bank[:, 1, tt * GL_K + f * P:tt * GL_K + (f + 1) * P],
                                          kendb[:, f, tt * P:(tt + 1) * P], ident[:, :])
                mm.then_inc(ke_turned, 1)
                pe.wait_ge(ke_act, 2 * h + 2)
                for d in range(2):
                    pe.wait_ge(q_dec, 2 * h + d + 1)
                    pe.wait_ge(k_inv, 2 * h + d + 1)
                    if d and h:
                        pe.wait_ge(o3_mean, h)
                    for tt in range(2):
                        for f in range(2):
                            mm = pe.matmul(bank[:, 2 + d, tt * P:(tt + 1) * P], kinv[:, d, f, tt * P:(tt + 1) * P],
                                           qdec[:, d, f, tt * P:(tt + 1) * P], start=f == 0, stop=f == 1)
                    mm.then_inc(sc_sum, 1)

                def state_step(s):
                    d, k = s % 2, s // 2
                    for f in range(2):
                        if s or h:
                            pe.wait_ge(st_ready, 14 * h + 2 * (s - 1) + f + 1)
                        if s == 0:
                            keys, vals = keTm[:, f * P:(f + 1) * P], v3[0:TM, 2, h * GL_V:(h + 1) * GL_V]
                        else:
                            cc = (k - 1, 3 - k)[d]
                            r = GL_CHUNK * (cc % 2)
                            keys = keT[r:r + GL_CHUNK, d, cc // 2, f * P:(f + 1) * P]
                            vals = v3[r:r + GL_CHUNK, cc // 2, h * GL_V:(h + 1) * GL_V]
                        pe.matmul(bank[:, 4 + f, :], keys, vals, start=True, stop=True).then_inc(ds_ready, 1)

                def from_state(s):
                    d, k = s % 2, s // 2
                    cc = (k, 2 - k)[d]
                    pe.wait_ge(st_ready, 14 * h + 2 * s + 2)
                    for v in range(4):
                        c0 = (v % 2) * TB + cc * GL_CHUNK
                        for f in range(2):
                            mm = pe.matmul(bank[:, 6 + v // 2, c0:c0 + GL_CHUNK], (stf, stb)[d][:, k % 2, f, v * P:(v + 1) * P],
                                           qdec[:, d, f, cc * GL_CHUNK:(cc + 1) * GL_CHUNK], start=False,
                                           stop=s == 6, skip_group_check=True)
                    return mm

                state_step(0)
                pe.wait_ge(ke_dve, h + 1)
                state_step(1)
                pe.wait_ge(sc_ready, h + 1)
                if h:
                    pe.wait_ge(o3_scaled, 4 * h)
                for v in range(4):
                    for tt in range(2):
                        c0 = (v % 2) * TB + tt * P
                        pe.matmul(bank[:, 6 + v // 2, c0:c0 + P], v3[:, tt, h * GL_V + v * P:h * GL_V + (v + 1) * P],
                                  sc[:, tt, :], start=v % 2 == 0 and tt == 0, stop=False, skip_group_check=True)
                for s in range(7):
                    if s + 2 < 7:
                        from_state(s)
                        state_step(s + 2)
                    else:
                        mm = from_state(s)
                mm.then_inc(o3_part, 1)
                for v in range(4):
                    pe.wait_ge(o3_sq, 2 * h + v // 2 + 1)
                    mm = pe.matmul(bank[:, 3, 0:TB], ones[:, :], osq3[:, v, :], start=v == 0, stop=v == 3)
                mm.then_inc(o3_sum, 1)
            pe.wait_ge(o3_mean, GL_HEADS)
            with pe.Fori(0, TRIPS["gout"] - 1) as i:
                for j in range(8):
                    pe.wait_ge(act_ready, LO["z3"] + j // 2 + 1)
                    features("gout", i, j, model(TB), TB)
            for j in range(8):
                features("gout", TRIPS["gout"] - 1, j, model(TB), TB)
            norm_after(4)
            pe.wait_ge(acc_free, 4 * (C0["gout"] + TRIPS["gout"]))
            for tt in range(2):
                for g in range(4):
                    if (tt, g) == (1, 0):
                        pe.wait_ge(rstd_ready, POST(4) + 1)
                    for n in range(4):
                        k = 4 * g + n
                        pe.wait_ge(x_updated, KD * 3 + k + 1)
                        mm = pe.transpose(bank[:, 4 * tt + g, n * P:(n + 1) * P], xT[:, k, tt * P:(tt + 1) * P], ident[:, :])
                    mm.then_inc(out_turned, 1)

        @block.gpsimd
        def _(pool):
            pool.memset(ahi[:, KD * T2:].bitcast(F32), 0.0).then_inc(spare_set, 1)
            pool.memset(alo[:, KD * T2:].bitcast(F32), 0.0).then_inc(spare_set, 1)

            def low(dst, whole, high, done):
                pool.tensor_tensor(dst, whole, high.bitcast(F32), ALU.subtract).then_inc(done, 1)

            def norm_before(b):
                T = T_PRE[b]
                for k in range(KD):
                    pool.wait_ge(hhi_ready, KD * b + k + 1)
                    low(ha(alo, k, 0, T), tmp[:, k % 2, 0:T], ha(ahi, k, 0, T), act_ready)

            def sum_squares(b):
                ph, T = OUT_STREAM[b], T_POST[b]
                if b > 1:
                    pool.wait_ge(mean_ready, b - 1)
                pool.memset(sqacc[:, :], 0.0).then_inc(y_summed, 1)
                with pool.Fori(0, TRIPS[ph]) as i:
                    for t in range(4):
                        pool.wait_ge(acc_free, at(4 * C0[ph] + t + 1, i, 4))
                        y = Y[b][:, bass.ds(i * 4 + t, 1), 0:T]
                        pool.tensor_tensor(sqb[:, t % 2:t % 2 + 1, 0:T], y, y, ALU.mult).then_inc(y_squared, 1)
                        pool.wait_ge(y_squared, at(KD * (b - 1) + t + 1, i, 4))
                        pool.wait_ge(y_summed, at((KD + 1) * (b - 1) + t + 1, i, 4))
                        pool.tensor_tensor(sqacc[:, 0:T], sqacc[:, 0:T], sqb[:, t % 2, 0:T], ALU.add).then_inc(y_summed, 1)

            norm_before(0)
            pool.wait_ge(ya_hi, 1)
            low(ylo[:, 0:DA_HEADS, :], yn[:, :, :], yhi[:, 0:DA_HEADS, :], y_done)
            with pool.Fori(0, TRIPS["oabc"]) as i:
                for t in range(4):
                    pool.wait_ge(mix_part, at(t + 1, i, 4))
                    low(alo_tile(i, t), mixtmp[:, 0, t:t + 1, :], ahi_tile(i, t), act_ready)
            sum_squares(1)
            norm_before(1)
            with pool.Fori(0, TRIPS["up"]) as i:
                for t in range(2):
                    pool.wait_ge(ffhi_ready, at(t + 1, i, 2))
                    low(glo[:, bass.ds(i * 2 + t, 1), :], pr[:, t:t + 1, :], ghi[:, bass.ds(i * 2 + t, 1), :], act_ready)
            sum_squares(2)
            norm_before(2)
            pool.wait_ge(rope_in, 48)
            for n in range(24):
                pool.wait_ge(qk_normed, n + 1)
                if n >= 2:
                    pool.wait_ge(qk_done, n - 1)
                pool.tensor_tensor(nc2[:, n % 2, :], n2[:, n % 2, :], cos[:, :], ALU.mult).then_inc(qk_cos, 1)
            for h in range(AT_HEADS):
                pool.wait_ge(z2hi, h + 1)
                low(ha(alo, h, 0, T2), z2[:, h % 2, :], ha(ahi, h, 0, T2), act_ready)
            sum_squares(3)
            norm_before(3)
            for h in range(GL_HEADS):
                keys = gqk[:, KT + 2 * h:KT + 2 * h + 2, :]
                for d in range(2):
                    pool.wait_ge(e_k, 2 * h + d + 1)
                    pool.tensor_tensor(kinv[:, d, :, :], kinv[:, d, :, :], keys[:, :, 0:TB], ALU.mult).then_inc(k_inv, 1)
                for d, (t, T) in enumerate(((kendf, T2), (kendb, TB))):
                    pool.wait_ge(e_d, 2 * h + d + 1)
                    pool.tensor_tensor(t[:, :, :], t[:, :, :], keys[:, :, 0:T], ALU.mult).then_inc(k_end, 1)
                pool.wait_ge(z3hi, h + 1)
                tiles = [t[:, 0:KD * T2].rearrange("p (k t) -> p k t", t=T2)[:, 4 * h:4 * h + 4, 0:TB] for t in (alo, ahi)]
                low(tiles[0], osq3[:, :, :], tiles[1], act_ready)
            sum_squares(4)


INS = ["x", "rel_bias_table", "w_in", "b_gate", "lam_q1", "lam_k1", "lam_q2", "lam_k2", "diff_subln_g", "sinks", "w_oa",
       "w_ob", "w_oc", "w_out", "pre_mix_g", "post_mix_g", "pre_ffn_g", "post_ffn_g", "w_up", "conv_w", "conv_b", "w_down",
       "meta_tokens_2", "pre_norm_2", "post_norm_2", "attn_w_in_2", "attn_q_norm_2", "attn_k_norm_2", "attn_w_out_2",
       "gla_w_in_2", "gla_gk_up_2", "gla_gk_bias_2", "gla_o_norm_2", "gla_w_out_2"]


def kernel(**inputs):
    import concourse.bacc as bacc
    from concourse.bass_utils import run_bass_kernel_spmd

    nc = bacc.Bacc("TRN2", target_bir_lowering=False, num_devices=1, dynamic_dma_scratch_size=64)
    arrays = {name: np.ascontiguousarray(inputs[name]) for name in INS}
    arrays |= shape_constants()
    access = {name: nc.dram_tensor(f"in_{name}", a.shape, mybir.dt.from_np(a.dtype), kind="ExternalInput").ap()
              for name, a in arrays.items()}
    access["subln"] = access["diff_subln_g"]
    out = nc.dram_tensor("out", (TB, D), F32, kind="ExternalOutput").ap()
    two_blocks_kernel(nc, access, out)
    result = run_bass_kernel_spmd(nc, [{f"in_{name}": a for name, a in arrays.items()}], core_ids=[0])
    return result.results[0]["out"].reshape(1, TB, D)
```

```python
import math
from contextlib import ExitStack

import numpy as np

import concourse.bass as bass
from concourse import mybir

F32 = mybir.dt.float32
F32R = mybir.dt.float32r
ALU = mybir.AluOpType
ACT = mybir.ActivationFunctionType
AX = mybir.AxisListType

P = 128
D = 2048
KD = D // P
TB = 256
TM = 16
T2 = TB + TM
EPS = 1e-6

DA_HEADS, SW_HEADS, MB_HEADS, HD = 4, 8, 8, 64
N_HEADS = DA_HEADS + SW_HEADS + MB_HEADS
WINDOW = 128
N_BUCKETS, MAX_DIST = 32, 128
QKV = 512
IN_GATES = 3 * QKV + QKV + 2 * P + 3 * QKV
D_FF = 5632
FT = D_FF // P
LAM_INIT = 0.8 - 0.6 * math.exp(-0.3 * 0)
MASKED = -float(2 ** 100)
LINE = 2 * P + P - 1

AT_HEADS, AT_KV, AT_HD = 16, 8, 128
GRID_W, ROPE_THETA, ROPE_AXIS = 64, 10000.0, 64
GL_HEADS, GL_K, GL_V, GL_RANK, GL_CHUNK = 4, 256, 512, 16, 64
GL_NORMALIZER = 16.0
KT = 8

UNIT = 1024
RAW, RING, LEAD = 8, 4, 3

STREAM = [("qkva", 1, 24, 3), ("qb", 1, 8, 1), ("kvb", 1, 4, 1), ("qkvc", 1, 24, 3),
          ("gates", 12, 8, 1), ("oabc", 4, 8, 3),
          ("wout", 4, 8, 1), ("up", 11, 16, 2), ("down", 4, 24, 1), ("aqk", 6, 8, 1), ("av", 2, 8, 1),
          ("ag", 4, 8, 1), ("aout", 4, 8, 1), ("gqk", 4, 8, 1), ("lr", 1, 1, 1), ("gv", 4, 8, 1),
          ("gg", 4, 8, 1), ("gout", 4, 8, 1)]
TRIPS, UNITS, CHUNKS, U0, C0 = {}, {}, {}, {}, {}
_u = _c = 0
for _name, _trips, _units, _chunks in STREAM:
    TRIPS[_name], UNITS[_name], CHUNKS[_name], U0[_name], C0[_name] = _trips, _units, _chunks, _u, _c
    _u += _trips * _units
    _c += _trips * _chunks
N_UNITS = _u

PARAMS = [("pre_mix_g", 16), ("subln", 1), ("b_gate", 48), ("post_mix_g", 16), ("pre_ffn_g", 16), ("conv_w", 264),
          ("conv_b", 88), ("post_ffn_g", 16), ("pre_norm_2", 32), ("post_norm_2", 32), ("attn_q_norm_2", 1),
          ("attn_k_norm_2", 1), ("gla_gk_bias_2", 16), ("gla_o_norm_2", 4)]
PAR = {}
_r = 0
for _name, _rows in PARAMS:
    PAR[_name] = _r
    _r += _rows
N_PAR = _r
PAR_GROUPS = -(-N_PAR // P)
N_SMALL = sum((PAR[n] + r - 1) // P - PAR[n] // P + 1 for n, r in PARAMS) + 5


def at(const, trip, per_trip):
    return trip * per_trip + const


def under(const, trip, per_trip, bound):
    return isinstance(trip, int) and trip * per_trip + const < bound


def shape_constants():
    f32 = np.float32
    dist = 255 - np.arange(LINE)
    n = np.maximum(dist, 0)
    half = N_BUCKETS // 2
    large = half + (np.log(np.maximum(n, 1).astype(f32) / f32(half)) / f32(math.log(MAX_DIST / half))
                    * f32(N_BUCKETS - half)).astype(np.int32)
    bucket = np.where(n < half, n, np.minimum(large, N_BUCKETS - 1))

    def one_hot(valid):
        row = np.where(valid, bucket, N_BUCKETS)
        return (np.arange(N_BUCKETS + 1)[:, None] == row[None]).astype(f32)

    token = np.arange(TB)
    inv = f32(ROPE_THETA) ** (-np.arange(0, ROPE_AXIS, 2, dtype=f32) / f32(ROPE_AXIS))
    angle = np.zeros((P, T2), f32)
    for axis, pos in enumerate((token // GRID_W, token % GRID_W)):
        for half_ in range(2):
            r0 = axis * 64 + half_ * 32
            angle[r0:r0 + 32, :TB] = inv[:, None] * pos.astype(f32)[None]
    turn = np.zeros((P, P), f32)
    for d in range(P):
        if d % 64 < 32:
            turn[d + 32, d] = -1.0
        else:
            turn[d - 32, d] = 1.0
    s, c = np.arange(P)[:, None], np.arange(P)[None]
    same = s // GL_CHUNK == c // GL_CHUNK
    reset = np.ones((P, T2), f32)
    reset[:, 0:T2:GL_CHUNK] = 0.0
    return {
        "c_hot_full": one_hot(dist >= 0), "c_hot_window": one_hot((dist >= 0) & (dist < WINDOW)),
        "c_cos": np.cos(angle).astype(f32), "c_sin": np.sin(angle).astype(f32), "c_turn": turn,
        "c_ident": np.eye(P, dtype=f32), "c_mask_f": (same & (s <= c)).astype(f32),
        "c_mask_b": (same & (s > c)).astype(f32), "c_reset": reset,
    }


def two_blocks_kernel(nc, A, out):
    ctx = ExitStack()
    with ctx:
        place_at = [(nc.sbuf_base + 31) // 32 * 32]

        def sb(name, shape, dt=F32, at_=None):
            size = int(np.prod(shape[1:])) * 4
            off = place_at[0] if at_ is None else at_
            t = nc.alloc_sbuf_tensor_at(name, shape, dt, offset=off)
            if at_ is None:
                place_at[0] = off + (size + 31) // 32 * 32
            return t

        def sem(name):
            return ctx.enter_context(nc.semaphore(name))

        raw = sb("raw", [P, RAW, UNIT])
        whi = sb("whi", [P, RING, UNIT], F32R)
        wlo = sb("wlo", [P, RING, UNIT], F32R)
        SPARE = P - TM
        act_at = place_at[0]
        ahi = sb("ahi", [P, KD * T2 + SPARE], F32R)
        alo = sb("alo", [P, KD * T2 + SPARE], F32R)
        par = sb("par", [P, N_PAR])
        ident = sb("ident", [P, P])
        ones = sb("ones", [P, P])
        lam = sb("lam", [P, 8])
        subg = lam[:, 4:5]
        qkgain = sb("qkgain", [P, 24])
        xT_at = place_at[0]
        xT = sb("xT", [P, KD, T2])
        msq = sb("msq", [P, T2])
        rstd = sb("rstd", [P, T2])
        sqacc = sb("sqacc", [P, T2])
        tmp = sb("tmp", [P, 2, T2])
        sqb_at = place_at[0]
        sqb = sb("sqb", [P, 2, T2])
        R2 = place_at[0]
        LIMIT = nc.sbuf_usable_end

        def region(*parts):
            off, made = R2, []
            for name, shape, dt in parts:
                made.append(sb(name, shape, dt, at_=off))
                off += (int(np.prod(shape[1:])) * 4 + 31) // 32 * 32
            assert off <= LIMIT, (parts[0][0], off, LIMIT)
            return made

        def ha(t, k, c0, n):
            return t[:, k * T2 + c0:k * T2 + c0 + n]

        xrow, mrow, prow, tabx, hots, line, lamv = region(
            ("xrow", [P, 2, D], F32), ("mrow", [TM, D], F32), ("prow", [P, PAR_GROUPS, P], F32),
            ("tabx", [N_BUCKETS + 1, N_HEADS], F32), ("hots", [N_BUCKETS + 1, 2, LINE], F32),
            ("line", [N_HEADS, 2, LINE], F32), ("lamv", [HD, 6], F32))
        (qaT, kaT, vatok, qbT, kbT, vbtok, qcT, kcT, vctok, bias, yhi, ylo, sbias, prob, probT, osb, sinkb, sinkn, nmax, ssum,
         esink) = region(
            ("qaT", [P, 4, TB], F32), ("kaT", [P, 4, TB], F32), ("vatok", [P, 2, QKV], F32),
            ("qbT", [P, 4, TB], F32), ("kbT", [P, 2, TB], F32), ("vbtok", [P, 2, P], F32),
            ("qcT", [P, 4, TB], F32), ("kcT", [P, 4, TB], F32), ("vctok", [P, 2, QKV], F32),
            ("bias", [P, N_HEADS, TB], F32), ("yhi", [P, 12, TB], F32R), ("ylo", [P, 12, TB], F32R),
            ("sbias", [P, 2, 384], F32), ("prob", [P, 4, 384], F32), ("probT", [P, 2, 384], F32),
            ("osb", [P, 4, TB], F32), ("sinkb", [P, SW_HEADS], F32), ("sinkn", [P, SW_HEADS], F32), ("nmax", [P, 24, 2], F32),
            ("ssum", [P, 24, 2], F32), ("esink", [P, 8, 2], F32))
        bias_at = R2 + 4 * (8 * TB * 2 + 4 * QKV + 4 * TB + 2 * TB + 2 * P)
        osq = sb("osq", [P, 4, TB], F32, at_=bias_at)
        ors = sb("ors", [P, 4, TB], F32, at_=bias_at + 4096)
        yn = sb("yn", [P, 4, TB], F32, at_=bias_at + 8192)
        (gate,) = region(("gate", [P, 48, TB], F32))
        assert R2 + 48 * TB * 4 <= bias_at + N_HEADS * TB * 4
        mixtmp = sb("mixtmp", [P, 2, 4, TB], F32, at_=bias_at + N_HEADS * TB * 4 + 24 * TB * 4)
        (yT,) = region(("yT", [P, KD, T2], F32))
        ghi, glo, cv, pr = region(("ghi", [P, FT, TB], F32R), ("glo", [P, FT, TB], F32R), ("cv", [P, 4, TB], F32),
                                  ("pr", [P, 2, TB], F32))
        yT_ffn = sb("yT_ffn", [P, KD, T2], F32, at_=act_at)
        qk2, v2, gs2, cos, sin, turn, sq2, rs2, n2, nc2, p2, pT2, nm2, sum2 = region(
            ("qk2", [P, 24, T2], F32), ("v2", [P, 3, 1024], F32), ("gs2", [P, KD, T2], F32), ("cos", [P, T2], F32),
            ("sin", [P, T2], F32), ("turn", [P, P], F32), ("sq2", [P, 2, T2], F32), ("rs2", [P, 2, T2], F32),
            ("n2", [P, 2, T2], F32), ("nc2", [P, 2, T2], F32), ("p2", [P, 2, 3, T2], F32), ("pT2", [P, 2, 3, T2], F32),
            ("nm2", [P, AT_HEADS, 3], F32), ("sum2", [P, AT_HEADS, 3], F32))
        cum = sb("cum", [P, 16, T2], F32, at_=xT_at)
        (gqk, v3, gg, maskf, maskb, reset, qdec, kinv, kendf, kendb, keT, keTm, sc, osq3, stf, stb) = region(
            ("gqk", [P, 16, T2], F32), ("v3", [P, 3, D], F32), ("gg", [P, KD, TB], F32), ("maskf", [P, P], F32),
            ("maskb", [P, P], F32), ("reset", [P, T2], F32), ("qdec", [P, 2, 2, TB], F32),
            ("kinv", [P, 2, 2, TB], F32), ("kendf", [P, 2, T2], F32), ("kendb", [P, 2, TB], F32),
            ("keT", [P, 2, 2, GL_K], F32), ("keTm", [TM, GL_K], F32), ("sc", [P, 2, P], F32),
            ("osq3", [P, 4, TB], F32), ("stf", [P, 2, 2, GL_V], F32), ("stb", [P, 2, 2, GL_V], F32))
        dec = sb("dec", [P, 2, 2, 5], F32, at_=sqb_at)
        gate_at = R2 + 4 * (16 * T2 + 3 * D + KD * TB + 2 * P + T2 + 4 * TB * 2 + 2 * T2 + 2 * TB + 4 * GL_K + GL_K + 2 * P)
        lrT = sb("lrT", [GL_RANK, 2, T2], F32, at_=gate_at)
        up_w = sb("up_w", [GL_RANK, 2, KT * P], F32, at_=gate_at + 2 * T2 * 4)
        zabs = sb("zabs", [P, 2, 4, T2], F32, at_=gate_at + 2 * T2 * 4 + 2 * KT * P * 4)
        orow = sb("orow", [P, 2, D], F32, at_=R2 + KD * T2 * 4)

        bank = ctx.enter_context(nc.psum_tensor("bank", [P, 8, 512], F32))

        def rows_of(w, c0, width, k0, nk):
            return w.rearrange("(k p) n -> p k n", p=P)[:, k0:k0 + nk, bass.ds(c0, width)]

        w_in, w_out, w_up, w_down = A["w_in"][0], A["w_out"][0], A["w_up"][0], A["w_down"][0]
        w_o = [A["w_oa"][0], A["w_ob"][0], A["w_oc"][0]]
        attn_in, attn_out = A["attn_w_in_2"][0], A["attn_w_out_2"][0]
        gla_in, gla_out = A["gla_w_in_2"][0], A["gla_w_out_2"][0]
        lines_dram = nc.dram_tensor("bias_lines", [N_HEADS, P, LINE + 1], F32, kind="Internal").ap()
        park_dram = nc.dram_tensor("parked_x", [P, KD * T2], F32, kind="Internal").ap()

        def unit_tiles(ph, j):
            if ph == "kvb":
                return 4 * j, 4
            if ph == "oabc":
                return (2 * (j % 2), 2) if j < 4 else (j - 4, 1)
            if ph == "down":
                return (2 * j, 2) if j < 20 else (20 + j, 1)
            if ph == "up":
                return 4 * (j % 8 // 2), 4
            if ph == "lr":
                return 0, KD
            return 2 * (j % 8), 2

        def chunk_of(ph, j):
            if ph == "kvb":
                return 0, j == 0, j == 3
            if ph == "oabc":
                return min(j // 2, 2), j in (0, 2, 4), j in (1, 3, 7)
            if ph == "down":
                return 0, j == 0, j == 23
            if ph == "lr":
                return 0, True, True
            return j // 8, j % 8 == 0, j % 8 == 7

        def unit_source(ph, i, j):
            k0, nk = unit_tiles(ph, j)

            def col(c, per):
                return at(c, i, per)

            if ph in ("qkva", "qkvc"):
                first = 0 if ph == "qkva" else 3 * QKV + QKV + 2 * P
                return ((0, 1024), rows_of(w_in, first + QKV * (j // 8), QKV, k0, nk))
            if ph == "qb":
                return ((0, 1024), rows_of(w_in, 3 * QKV, QKV, k0, nk))
            if ph == "kvb":
                return ((0, 1024), rows_of(w_in, 4 * QKV, 2 * P, k0, nk))
            if ph == "gates":
                return ((0, 1024), rows_of(w_in, col(IN_GATES, 512), 512, k0, nk))
            if ph == "oabc":
                return ((0, nk * 512), rows_of(w_o[chunk_of(ph, j)[0]], col(0, 512), 512, k0, nk))
            if ph == "up":
                return ((0, 1024), rows_of(w_up, col((j % 2) * D_FF + 256 * (j // 8), 512), 256, k0, nk))
            if ph == "down":
                return ((0, nk * 512), rows_of(w_down, col(0, 512), 512, k0, nk))
            if ph == "lr":
                return ((0, KD * 2 * GL_RANK), rows_of(gla_in, 3 * D, 2 * GL_RANK, 0, KD))
            w, c0 = {"wout": (w_out, 0), "aqk": (attn_in, 0), "av": (attn_in, 3072), "ag": (attn_in, 4096),
                     "aout": (attn_out, 0), "gqk": (gla_in, 0), "gv": (gla_in, 2048), "gg": (gla_in, 4096),
                     "gout": (gla_out, 0)}[ph]
            return ((0, 1024), rows_of(w, col(c0, 512), 512, k0, nk))

        raw_loaded = [sem(f"raw_loaded{n}") for n in range(RAW)]
        whi_ready, wlo_ready, tile_pass, acc_free = map(sem, "whi_ready wlo_ready tile_pass acc_free".split())
        rows_in, small_in, hots_in, start_set, spare_set, row_turned, row_taken, par_ready = map(
            sem, "rows_in small_in hots_in start_set spare_set row_turned row_taken par_ready".split())
        lam_prod, lam_sum, lam_exp, lam_ready = map(sem, "lam_prod lam_sum lam_exp lam_ready".split())
        line_sum, line_ready, lines_stored, bias_in = map(sem, "line_sum line_ready lines_stored bias_in".split())
        y_squared, y_summed, mean_ready, mean_eps, inv_ready, rstd_ready, y_scaled, x_updated, \
            sq_ready, sq_used, h_ready, hhi_ready, act_ready = map(
                sem, "y_squared y_summed mean_ready mean_eps inv_ready rstd_ready y_scaled x_updated "
                     "sq_ready sq_used h_ready hhi_ready act_ready".split())
        s_ready, s_biased, max_ready, max_sink, p_ready, sink_ready, sum_sink, inv_sum, p_second, p_scaled, \
            p_turned, pT_ready, o_ready, o_free, yhi_ready, a_out, a_squared, a_summed, a_mean, a_inv, a_rstd, \
            a_normed, ya_hi, y_done = map(
                sem, "s_ready s_biased max_ready max_sink p_ready sink_ready sum_sink inv_sum p_second p_scaled "
                     "p_turned pT_ready o_ready o_free yhi_ready a_out a_squared a_summed a_mean a_inv a_rstd "
                     "a_normed ya_hi y_done".split())
        mix_two, mix_part, mix_sum = map(sem, "mix_two mix_part mix_sum".split())
        tap2, tap1, gelu_done, ff_prod, ffhi_ready = map(
            sem, "tap2 tap1 gelu_done ff_prod ffhi_ready".split())
        rope_in, qk_sq, qk_sum, qk_mean, qk_inv, qk_rstd, qk_normed, qk_turned, qk_cos, qk_sin, qk_done = map(
            sem, "rope_in qk_sq qk_sum qk_mean qk_inv qk_rstd qk_normed qk_turned qk_cos qk_sin qk_done".split())
        s2_ready, max2_ready, p2_ready, inv2, p2_scaled, p2_turned, pT2_act, pT2_dve, o2_ready, o2_taken, z2_ready, \
            z2hi = map(sem, "s2_ready max2_ready p2_ready inv2 p2_scaled p2_turned pT2_act pT2_dve o2_ready o2_taken "
                            "z2_ready z2hi".split())
        x_parked, x_back, gla_const, z_sum, z_abs, z_min, z_exp, z_ln, z_sub, cum_ready = map(
            sem, "x_parked x_back gla_const z_sum z_abs z_min z_exp z_ln z_sub cum_ready".split())
        e_q, e_k, e_d, e_dec, d_sub, q_dec, k_inv, k_end, ke_turned, ke_act, ke_dve, sc_sum, sc_part, sc_ready, \
            ds_ready, st_ready, o3_part, o3_sq, o3_sum, o3_mean, o3_inv, o3_rstd, o3_scaled, z3_ready, z3hi = \
            map(
                sem, "e_q e_k e_d e_dec d_sub q_dec k_inv k_end ke_turned ke_act ke_dve sc_sum sc_part sc_ready "
                     "ds_ready st_ready o3_part o3_sq o3_sum o3_mean o3_inv o3_rstd o3_scaled z3_ready z3hi".split())
        out_turned, out_taken, stored = map(sem, "out_turned out_taken stored".split())

        LO, lo_tiles = {}, 0
        for name, tiles in (("norm0", KD), ("mix", KD), ("norm1", KD), ("ff", FT), ("norm2", KD), ("z2", AT_HEADS),
                            ("norm3", KD), ("z3", GL_HEADS)):
            LO[name] = lo_tiles
            lo_tiles += tiles

        PRE, POST = (lambda b: 2 * b), (lambda b: 2 * b - 1)
        T_PRE = [TB, TB, T2, T2]
        T_POST = [None, TB, TB, T2, TB]
        G_PRE = [PAR["pre_mix_g"], PAR["pre_ffn_g"], PAR["pre_norm_2"], PAR["pre_norm_2"] + KD]
        G_POST = [None, PAR["post_mix_g"], PAR["post_ffn_g"], PAR["post_norm_2"], PAR["post_norm_2"] + KD]
        OUT_STREAM = [None, "wout", "down", "aout", "gout"]
        Y = [None, yT, yT_ffn, yT, yT]

        def job_of(m):
            return m // 2 if m < 2 * DA_HEADS else m - DA_HEADS

        def ends_job(m):
            return m < 24 and (m >= 2 * DA_HEADS or m % 2 == 1)

        def step_beside(ph, i, j):
            if ph == "qb":
                return j
            if ph == "qkvc" and j < 16 and j % 2 == 0:
                return 8 + j // 2
            if ph == "qkvc" and j in (17, 19, 21):
                return 16 + (j - 17) // 2
            if ph == "gates" and 8 * i + j < 10:
                return 19 + 8 * i + j
            return None

        def ahi_tile(i, t):
            return ahi[:, 0:KD * T2].rearrange("p (k t) -> p k t", t=T2)[:, bass.ds(i * 4 + t, 1), 0:TB]

        def alo_tile(i, t):
            return alo[:, 0:KD * T2].rearrange("p (k t) -> p k t", t=T2)[:, bass.ds(i * 4 + t, 1), 0:TB]

        def ring_waits(eng, ph, i, u, n, landed):
            if landed:
                eng.wait_ge(raw_loaded[u % RAW], at(16 * (u // RAW + 1), i, 2 * n))
            if not under(u, i, n, RING):
                eng.wait_ge(tile_pass, at(4 * (u - RING + 1), i, 4 * n))

        block = ctx.enter_context(nc.Block())

        @block.sync
        def _(sp):
            def load_trip(ph, i):
                n = UNITS[ph]
                for j in range(n):
                    u = U0[ph] + j
                    if not under(u, i, n, RAW):
                        sp.wait_ge(wlo_ready, at(u - RAW + 1, i, n))
                    (c0, c1), src = unit_source(ph, i, j)
                    dst = raw[:, u % RAW, c0:c1].rearrange("p (k n) -> p k n", k=src.shape[1])
                    sp.dma_start(dst, src).then_inc(raw_loaded[u % RAW], 16)

            def load(ph):
                if TRIPS[ph] <= 2:
                    for i in range(TRIPS[ph]):
                        load_trip(ph, i)
                else:
                    with sp.Fori(0, TRIPS[ph]) as i:
                        load_trip(ph, i)

            for tt in range(2):
                sp.dma_start(xrow[:, tt, :], A["x"][0, tt * P:(tt + 1) * P, :]).then_inc(rows_in, 16)
            sp.dma_start(mrow[:, :], A["meta_tokens_2"]).then_inc(rows_in, 16)
            load("qkva")
            sp.wait_ge(lines_stored, 48)
            skewed = bass.AP(tensor=lines_dram.tensor, offset=P - 1, ap=[[LINE, P], [P * (LINE + 1), N_HEADS], [1, TB]])
            sp.dma_start(bias[:, :, :], skewed).then_inc(bias_in, 16)
            for ph in ("qb", "kvb", "qkvc", "gates", "oabc", "wout", "up", "down", "aqk", "av", "ag", "aout", "gqk", "lr", "gv",
                       "gg", "gout"):
                load(ph)
            sp.wait_ge(x_parked, 16)
            sp.wait_ge(e_dec, 3 * GL_HEADS)
            sp.wait_ge(d_sub, 3 * GL_HEADS)
            sp.wait_ge(e_k, 2 * GL_HEADS)
            sp.wait_ge(e_q, 2 * GL_HEADS)
            sp.dma_start(xT[:, :, :].rearrange("p k t -> p (k t)"), park_dram).then_inc(x_back, 16)
            for tt in range(2):
                sp.wait_ge(out_taken, 4 * (tt + 1))
                sp.dma_start(out[tt * P:(tt + 1) * P, :], orow[:, tt, :]).then_inc(stored, 16)
            sp.wait_ge(stored, 32)

        @block.scalar
        def _(act):
            def split(u, i=0, n=0):
                if not under(u, i, n, N_UNITS) and isinstance(i, int):
                    return
                ring_waits(act, None, i, u, n, landed=True)
                act.activation(whi[:, u % RING, :], raw[:, u % RAW, :], ACT.Copy).then_inc(whi_ready, 1)

            def trip(ph, i, read_out, before=None, after=None):
                n = UNITS[ph]
                for j in range(n):
                    if before:
                        before(i, j)
                    split(U0[ph] + j + LEAD, i, n)
                    chunk, _, ends = chunk_of(ph, j)
                    if ends and read_out:
                        read_out(i, chunk, U0[ph] + j, n)
                    if after:
                        after(i, j)

            def stream(ph, read_out):
                if TRIPS[ph] <= 2:
                    for i in range(TRIPS[ph]):
                        trip(ph, i, read_out)
                else:
                    with act.Fori(0, TRIPS[ph]) as i:
                        trip(ph, i, read_out)

            def passed(u, tile, i, n):
                act.wait_ge(tile_pass, at(4 * u + tile, i, 4 * n))

            def tiles_to(dst_of, func=ACT.Copy, T=TB):
                def read_out(i, chunk, u, n):
                    for t in range(4):
                        passed(u, t + 1, i, n)
                        act.activation(dst_of(i, chunk, t), bank[:, t, 0:T], func).then_inc(acc_free, 1)
                return read_out

            act.dma_start(ident[:, :], A["c_ident"]).then_inc(rows_in, 16)
            n_small = 0
            for name, rows in PARAMS:
                src = A[name]
                if name == "conv_w":
                    flat = src[0].rearrange("w (r c) -> (w r) c", c=P)
                elif name == "gla_gk_bias_2":
                    flat = src[0].rearrange("w (r c) -> (w r) c", c=P)
                else:
                    flat = src.rearrange("w (r c) -> (w r) c", c=P)
                r = 0
                while r < rows:
                    g, p0 = divmod(PAR[name] + r, P)
                    m = min(rows - r, P - p0)
                    act.dma_start(prow[p0:p0 + m, g, :], flat[r:r + m, :]).then_inc(small_in, 16)
                    n_small += 1
                    r += m
            for c, name in enumerate(("lam_q1", "lam_k1", "lam_q2", "lam_k2")):
                act.dma_start(lamv[:, c:c + 1], A[name].rearrange("a d -> d a")).then_inc(small_in, 16)
            sink_all = bass.AP(tensor=A["sinks"].tensor, offset=0, ap=[[0, P], [1, SW_HEADS]])
            act.dma_start(sinkb[:, :], sink_all).then_inc(small_in, 16)
            assert n_small + 5 == N_SMALL
            act.dma_start(tabx[0:N_BUCKETS, :], A["rel_bias_table"]).then_inc(hots_in, 16)
            act.dma_start(hots[:, 0, :], A["c_hot_full"]).then_inc(hots_in, 16)
            act.dma_start(hots[:, 1, :], A["c_hot_window"]).then_inc(hots_in, 16)
            for u in range(LEAD):
                split(u)
            for g in range(9):
                act.wait_ge(row_turned, g + 1)
                if g < 8:
                    tt, k = g // 4, 4 * (g % 4)
                    act.activation(xT[:, k:k + 4, tt * P:(tt + 1) * P],
                                   bank[:, g % 8, :].rearrange("p (k t) -> p k t", k=4), ACT.Copy).then_inc(row_taken, 1)
                else:
                    act.activation(xT[:, :, TB:T2], bank[:, g % 8, 0:KD * TM].rearrange("p (k t) -> p k t", k=KD),
                                   ACT.Copy).then_inc(row_taken, 1)
            act.wait_ge(lam_sum, 1)
            act.activation(lam[:, 0:2], bank[:, 6, 0:2], ACT.Exp).then_inc(lam_exp, 1)
            for w in range(2):
                act.wait_ge(line_sum, w + 1)
                act.activation(line[:, w, :], bank[0:N_HEADS, 4 + w, 0:LINE], ACT.Copy).then_inc(line_ready, 1)
            act.wait_ge(line_ready, 2)
            for w, h0, h1 in ((0, 0, DA_HEADS), (1, DA_HEADS, DA_HEADS + SW_HEADS), (0, DA_HEADS + SW_HEADS, N_HEADS)):
                act.dma_start(lines_dram[h0:h1, :, 0:LINE], line[h0:h1, w:w + 1, :].to_broadcast([h1 - h0, P, LINE]))\
                   .then_inc(lines_stored, 16)

            def root(use, T):
                act.wait_ge(inv_ready, use + 1)
                act.activation(rstd[:, 0:T], msq[:, 0:T], ACT.Sqrt).then_inc(rstd_ready, 1)

            def norm_before(b):
                T = T_PRE[b]
                for k in range(KD):
                    m = KD * b + k
                    if b == 0:
                        act.wait_ge(row_taken, 9)
                    else:
                        act.wait_ge(x_updated, KD * (b - 1) + k + 1)
                    if m >= 2:
                        act.wait_ge(sq_used, m - 1)
                    act.activation(sqb[:, k % 2, 0:T], xT[:, k, 0:T], ACT.Square).then_inc(sq_ready, 1)
                root(PRE(b), T)
                for k in range(KD):
                    act.wait_ge(h_ready, KD * b + k + 1)
                    act.activation(ha(ahi, k, 0, T), tmp[:, k % 2, 0:T], ACT.Copy).then_inc(hhi_ready, 1)

            norm_before(0)

            def branch_step(m):
                if m < 24:
                    if 8 <= m < 16:
                        act.wait_ge(max_sink, m - 8 + 1)
                    else:
                        act.wait_ge(max_ready, 2 * m + 2)
                    if m >= 4:
                        act.wait_ge(p_turned, job_of(m - 4) + 1)
                    for q, (c0, c1) in enumerate(((0, P), (P, 384))):
                        act.activation(prob[:, m % 4, c0:c1], sbias[:, m % 2, c0:c1], ACT.Exp, bias=nmax[:, m, q:q + 1],
                                       accum_out=ssum[:, m, q:q + 1]).then_inc(p_ready, 1)
                    if 8 <= m < 16:
                        act.activation(esink[:, m - 8, :], nmax[:, m, :], ACT.Exp, bias=sinkb[:, m - 8:m - 7])\
                           .then_inc(sink_ready, 1)
                if m >= 2 and ends_job(m - 2):
                    job = job_of(m - 2)
                    act.wait_ge(p_turned, job + 1)
                    if job >= 2:
                        act.wait_ge(o_ready, job - 1)
                    act.activation(probT[:, job % 2, :], bank[:, 6, 0:384], ACT.Copy).then_inc(pT_ready, 1)
                if m >= 4 and (m - 4) % 2 and m - 4 < 24:
                    unit = (m - 4) // 2
                    act.wait_ge(o_ready, job_of(m - 4) + 1)
                    if unit < DA_HEADS:
                        act.activation(osb[:, unit, :], bank[:, 7, 0:TB], ACT.Copy).then_inc(o_free, 1)
                    else:
                        act.activation(yhi[:, unit, :], bank[:, 7, 0:TB], ACT.Copy).then_inc(yhi_ready, 1)

            def steps(ph):
                def after(i, j):
                    m = step_beside(ph, i, j)
                    if m is not None:
                        branch_step(m)
                    if ph == "gates" and i == 1:
                        branch_norm(j)
                return after

            def branch_norm(j):
                if j == 3:
                    act.wait_ge(o_free, DA_HEADS)
                    act.activation(osq[:, :, :], osb[:, :, :], ACT.Square).then_inc(a_squared, 1)
                if j == 5:
                    act.wait_ge(a_inv, 2)
                    act.activation(ors[:, :, :], ors[:, :, :], ACT.Sqrt).then_inc(a_rstd, 1)
                if j == 6:
                    act.wait_ge(a_normed, 1)
                    act.activation(yhi[:, 0:DA_HEADS, :], yn[:, :, :], ACT.Copy).then_inc(ya_hi, 1)

            def qkv_out(q, k, v):
                def read_out(i, chunk, u, n):
                    if chunk < 2:
                        for t in range(4):
                            passed(u, t + 1, i, n)
                            act.activation((q, k)[chunk][:, t, :], bank[:, t, 0:TB], ACT.Copy).then_inc(acc_free, 1)
                    else:
                        for tt in range(2):
                            passed(u, (1, 4)[tt], i, n)
                            act.activation(v[:, tt, :], bank[:, tt, :], ACT.Copy).then_inc(acc_free, (1, 3)[tt])
                return read_out

            stream("qkva", qkv_out(qaT, kaT, vatok))
            act.wait_ge(lines_stored, 48)
            trip("qb", 0, tiles_to(lambda i, chunk, t: qbT[:, t, :]), after=steps("qb"))

            def kvb_out(i, chunk, u, n):
                passed(u, 1, i, n)
                act.activation(kbT[:, 0, :], bank[:, 0, 0:TB], ACT.Copy)
                act.activation(kbT[0:64, 1, :], bank[64:128, 0, 0:TB], ACT.Copy)
                act.activation(kbT[64:128, 1, :], bank[0:64, 0, 0:TB], ACT.Copy).then_inc(acc_free, 1)
                for tt in range(2):
                    passed(u, (2, 4)[tt], i, n)
                    ins = act.activation(vbtok[:, tt, :], bank[:, 1 + tt, 0:P], ACT.Copy)
                    ins.then_inc(acc_free, (1, 2)[tt])

            stream("kvb", kvb_out)

            trip("qkvc", 0, qkv_out(qcT, kcT, vctok), after=steps("qkvc"))

            def gates_out(i, chunk, u, n):
                for t in range(4):
                    passed(u, t + 1, i, n)
                    act.activation(gate[:, bass.ds(i * 4 + t, 1), :], bank[:, t:t + 1, 0:TB], ACT.Sigmoid,
                                   bias=par[:, bass.ds(i * 4 + (PAR["b_gate"] + t), 1)]).then_inc(acc_free, 1)

            for i in range(2):
                trip("gates", i, gates_out, after=steps("gates"))
            act.wait_ge(o_free, 12)
            act.wait_ge(y_done, 1)
            with act.Fori(2, TRIPS["gates"]) as i:
                trip("gates", i, gates_out)

            def mix_out(i, chunk, u, n):
                if chunk == 2:
                    for t in range(4):
                        act.wait_ge(mix_sum, at(t + 1, i, 4))
                        act.activation(ahi_tile(i, t), mixtmp[:, 0, t:t + 1, :], ACT.Copy).then_inc(mix_part, 1)

            stream("oabc", mix_out)

            def y_out(b):
                def read_out(i, chunk, u, n):
                    for t in range(4):
                        passed(u, t + 1, i, n)
                        dst = Y[b][:, bass.ds(i * 4 + t, 1), 0:T_POST[b]]
                        act.activation(dst, bank[:, t:t + 1, 0:T_POST[b]], ACT.Copy).then_inc(acc_free, 1)
                return read_out

            stream("wout", y_out(1))
            root(POST(1), TB)
            norm_before(1)

            def up_out(i, chunk, u, n):
                for t in range(4):
                    r = (t % 2) + (t // 2) * FT + 2 * chunk
                    passed(u, 2 * t - 2, i, n)
                    act.activation(cv[:, t, :], bank[:, 4 * chunk + t, 0:TB], ACT.Identity,
                                   bias=par[:, bass.ds(i * 4 + (PAR["conv_b"] + r), 1)],
                                   scale=par[:, bass.ds(i * 4 + (PAR["conv_w"] + 2 * 2 * FT + r), 1)]).then_inc(tap2, 1)
                for t in range(2):
                    act.wait_ge(acc_free, at(4 * (C0["up"] + chunk) + t + 1, i, 8))
                    act.activation(cv[:, t, :], cv[:, t, :], ACT.Gelu_apprx_tanh).then_inc(gelu_done, 1)
                for t in range(2):
                    act.wait_ge(ff_prod, at(2 * chunk + t + 1, i, 4))
                    act.activation(ghi[:, bass.ds(i * 4 + (2 * chunk + t), 1), :], pr[:, t:t + 1, :], ACT.Copy)\
                       .then_inc(ffhi_ready, 1)

            stream("up", up_out)
            stream("down", y_out(2))
            act.wait_ge(tile_pass, 4 * U0["aqk"])
            for t, name in ((cos, "c_cos"), (sin, "c_sin"), (turn, "c_turn")):
                act.dma_start(t[:, :], A[name]).then_inc(rope_in, 16)
            root(POST(2), TB)
            norm_before(2)

            def feature_out(dst, T, func):
                def read_out(i, chunk, u, n):
                    for t in range(4):
                        passed(u, t + 1, i, n)
                        act.activation(dst[:, bass.ds(i * 4 + t, 1), 0:T], bank[:, t:t + 1, 0:T], func).then_inc(acc_free, 1)
                return read_out

            def qk_norm(i, j):
                p, late = divmod(j, 2)
                if not late:
                    act.wait_ge(acc_free, at(4 * C0["aqk"] + p - 3, i, 4))
                    if not under(p - 4, i, 4, 2):
                        act.wait_ge(qk_sum, at(p - 5, i, 4))
                    act.activation(sq2[:, p % 2:p % 2 + 1, :], qk2[:, bass.ds(i * 4 + (p - 4), 1), :], ACT.Square)\
                       .then_inc(qk_sq, 1)
                else:
                    act.wait_ge(qk_inv, at(p - 3, i, 4))
                    act.activation(rs2[:, p % 2, :], rs2[:, p % 2, :], ACT.Sqrt).then_inc(qk_rstd, 1)

            qk_out = feature_out(qk2, T2, ACT.Copy)
            trip("aqk", 0, qk_out)
            trip("aqk", 1, qk_out, before=qk_norm)
            with act.Fori(2, TRIPS["aqk"]) as i:
                trip("aqk", i, qk_out, before=qk_norm)

            def v2_out(i, chunk, u, n):
                for tt in range(3):
                    rows = (P, P, TM)[tt]
                    passed(u, (1, 2, 4)[tt], i, n)
                    act.activation(v2[0:rows, tt:tt + 1, bass.ds(i * 512, 512)], bank[0:rows, tt:tt + 1, :], ACT.Copy)\
                       .then_inc(acc_free, (1, 1, 2)[tt])

            def attend(s):
                h, second = divmod(s, 2)
                for q in ((0, 1), (2,))[second] if h < AT_HEADS else ():
                    rows = (P, P, TM)[q]
                    act.wait_ge(max2_ready, 3 * h + q + 1)
                    if h >= 2:
                        act.wait_ge(p2_turned, 2 * (h - 1))
                    act.activation(p2[0:rows, h % 2, q, :], bank[0:rows, (4, 5, 4)[q], 0:T2], ACT.Exp,
                                   bias=nm2[0:rows, h, q:q + 1], accum_out=sum2[0:rows, h, q:q + 1]).then_inc(p2_ready, 1)
                if second and 1 <= h <= AT_HEADS:
                    hh = h - 1
                    act.wait_ge(p2_turned, 2 * hh + 2)
                    if hh >= 2:
                        act.wait_ge(o2_ready, hh - 1)
                    act.activation(pT2[:, hh % 2, 0:2, TB:T2], bank[:, 5, 0:2 * TM].rearrange("p (k t) -> p k t", k=2),
                                   ACT.Copy).then_inc(pT2_act, 1)
                    act.activation(pT2[0:TM, hh % 2, 2, :], bank[0:TM, 5, 2 * TM:2 * TM + T2], ACT.Copy).then_inc(pT2_act, 1)

            trip("av", 0, v2_out, before=lambda i, j: qk_norm(TRIPS["aqk"], j))
            trip("av", 1, v2_out, after=lambda i, j: attend(j))
            for i in range(TRIPS["ag"]):
                trip("ag", i, feature_out(gs2, T2, ACT.Silu), after=lambda i, j: attend(8 * (i + 1) + j))
            act.wait_ge(tile_pass, 4 * U0["aout"])
            for h in range(AT_HEADS):
                act.wait_ge(z2_ready, h + 1)
                act.activation(ha(ahi, h, 0, T2), qk2[:, h, :], ACT.Copy).then_inc(z2hi, 1)
            stream("aout", y_out(3))
            root(POST(3), T2)
            norm_before(3)

            act.wait_ge(h_ready, KD * 4)
            act.dma_start(park_dram, xT[:, :, :].rearrange("p k t -> p (k t)")).then_inc(x_parked, 16)
            for t, name in ((maskf, "c_mask_f"), (maskb, "c_mask_b"), (reset, "c_reset")):
                act.dma_start(t[:, :], A[name]).then_inc(gla_const, 16)
            act.dma_start(up_w[:, :, :], A["gla_gk_up_2"][0].rearrange("d r n -> r d n")).then_inc(gla_const, 16)

            stream("gqk", feature_out(gqk, T2, ACT.Copy))

            def v3_out(i, chunk, u, n):
                for tt in range(3):
                    rows = (P, P, TM)[tt]
                    passed(u, (1, 2, 4)[tt], i, n)
                    act.activation(v3[0:rows, tt:tt + 1, bass.ds(i * 512, 512)], bank[0:rows, tt:tt + 1, :], ACT.Copy)\
                       .then_inc(acc_free, (1, 1, 2)[tt])


            def lr_out(i, chunk, u, n):
                for d in range(2):
                    passed(u, (1, 4)[d], i, n)
                    act.activation(lrT[:, d, :], bank[0:GL_RANK, d, 0:T2], ACT.Copy).then_inc(acc_free, (1, 3)[d])

            stream("lr", lr_out)

            def log_decay(g, j):
                a = zabs[:, g % 2, :, :]
                if j == 0:
                    for t in range(4):
                        n = 4 * g + t
                        act.wait_ge(z_sum, n + 1)
                        if g >= 2:
                            act.wait_ge(z_sub, g - 1)
                        act.activation(zabs[:, g % 2, t, :], bank[:, 4 + t, 0:T2], ACT.Abs,
                                       bias=par[:, PAR["gla_gk_bias_2"] + n:PAR["gla_gk_bias_2"] + n + 1]).then_inc(z_abs, 1)
                if j == 2:
                    act.wait_ge(z_abs, 4 * g + 4)
                    act.activation(a, a, ACT.Exp, scale=-1.0).then_inc(z_exp, 1)
                    act.wait_ge(z_exp, g + 1)
                    act.activation(a, a, ACT.Ln, bias=1.0).then_inc(z_ln, 1)

            for g in range(TRIPS["gv"]):
                trip("gv", g, v3_out, after=log_decay)

            SC = 1.0 / GL_NORMALIZER

            def decays(h):
                return cum[:, 2 * h:2 * h + 2, :], cum[:, 8 + 2 * h:10 + 2 * h, 0:TB]

            def key_decays(h):
                for d, t in enumerate((kendf, kendb)):
                    act.wait_ge(d_sub, 3 * h + 2 + d)
                    act.activation(t[:, :, :], t[:, :, :], ACT.Exp, scale=SC).then_inc(e_d, 1)
                if h:
                    act.wait_ge(sc_sum, 2 * h)
                for d, l in enumerate(decays(h)):
                    act.wait_ge(cum_ready, 16)
                    act.activation(kinv[:, d, :, :], l[:, :, 0:TB], ACT.Exp, scale=-SC).then_inc(e_k, 1)

            def gla(h, j):
                if j == 0 and h == 0:
                    key_decays(0)
                if j == 0 and h < GL_HEADS:
                    lf, lb = decays(h)
                    if h:
                        act.wait_ge(o3_part, h)
                        act.wait_ge(st_ready, 14 * h)
                    for d, l in enumerate((lf, lb)):
                        act.activation(qdec[:, d, :, :], l[:, :, 0:TB], ACT.Exp, scale=SC).then_inc(e_q, 1)
                    act.activation(dec[:, 0, :, 0:4], lf[:, :, GL_CHUNK - 1:TB:GL_CHUNK], ACT.Exp, scale=SC).then_inc(e_dec, 1)
                    act.activation(dec[:, 0, :, 4:5], lf[:, :, T2 - 1:T2], ACT.Exp, scale=SC).then_inc(e_dec, 1)
                    act.activation(dec[:, 1, :, 0:4], lb[:, :, 0:TB:GL_CHUNK], ACT.Exp, scale=SC).then_inc(e_dec, 1)
                if j == 0 and h:
                    act.wait_ge(o3_part, h)
                    if h >= 2:
                        act.wait_ge(z3_ready, h - 1)
                    for c in range(2):
                        act.activation(osq3[:, 2 * c:2 * c + 2, :], bank[:, 6 + c, :].rearrange("p (v t) -> p v t", v=2),
                                       ACT.Square).then_inc(o3_sq, 1)
                if j == 1 and h < GL_HEADS:
                    act.wait_ge(ke_turned, 3 * h + 1)
                    act.activation(keT[:, 0, :, :], bank[:, 5, :].rearrange("p (t k) -> p t k", t=2), ACT.Copy).then_inc(ke_act, 1)
                if j == 1 and h:
                    act.wait_ge(o3_inv, h)
                    act.activation(rstd[:, 0:TB], msq[:, 0:TB], ACT.Sqrt).then_inc(o3_rstd, 1)
                if j == 2:
                    act.wait_ge(ke_turned, 3 * h + 2)
                    act.activation(keTm[:, :], bank[0:TM, 4, 0:GL_K], ACT.Copy).then_inc(ke_act, 1)
                if j == 6 and h + 1 < GL_HEADS:
                    key_decays(h + 1)

            for h in range(GL_HEADS):
                trip("gg", h, feature_out(gg, TB, ACT.Silu), after=gla)
            for j in range(2):
                gla(GL_HEADS, j)
            act.wait_ge(tile_pass, 4 * U0["gout"])
            for h in range(GL_HEADS):
                act.wait_ge(z3_ready, h + 1)
                zhi = ahi[:, 0:KD * T2].rearrange("p (k t) -> p k t", t=T2)[:, 4 * h:4 * h + 4, 0:TB]
                act.activation(zhi, gg[:, 4 * h:4 * h + 4, :], ACT.Copy).then_inc(z3hi, 1)
            with act.Fori(0, TRIPS["gout"] - 1) as i:
                trip("gout", i, y_out(4))
            trip("gout", TRIPS["gout"] - 1, y_out(4))
            root(POST(4), TB)
            for tt in range(2):
                for g in range(4):
                    act.wait_ge(out_turned, 4 * tt + g + 1)
                    act.activation(orow[:, tt, 512 * g:512 * g + 512], bank[:, 4 * tt + g, :], ACT.Copy)\
                       .then_inc(out_taken, 1)

        @block.vector
        def _(dve):
            def split(u, i=0, n=0):
                if not under(u, i, n, N_UNITS) and isinstance(i, int):
                    return
                dve.wait_ge(whi_ready, at(u + 1, i, n))
                dve.tensor_tensor(wlo[:, u % RING, :], raw[:, u % RAW, :], whi[:, u % RING, :].bitcast(F32),
                                  ALU.subtract).then_inc(wlo_ready, 1)

            def trip(ph, i, read_out=None, before=None, after=None):
                n = UNITS[ph]
                for j in range(n):
                    if before:
                        before(i, j)
                    split(U0[ph] + j + LEAD, i, n)
                    chunk, _, ends = chunk_of(ph, j)
                    if ends and read_out:
                        read_out(i, chunk, U0[ph] + j, n)
                    if after:
                        after(i, j)

            def stream(ph, read_out=None):
                if TRIPS[ph] <= 2:
                    for i in range(TRIPS[ph]):
                        trip(ph, i, read_out)
                else:
                    with dve.Fori(0, TRIPS[ph]) as i:
                        trip(ph, i, read_out)

            def column(name, k=0):
                return par[:, PAR[name] + k:PAR[name] + k + 1]

            dve.memset(ones[:, :], 1.0).then_inc(start_set, 1)
            dve.memset(tabx[N_BUCKETS:N_BUCKETS + 1, :], MASKED).then_inc(start_set, 1)
            for u in range(LEAD):
                split(u)
            dve.wait_ge(small_in, 16 * N_SMALL)
            dve.tensor_tensor(lamv[:, 4:5], lamv[:, 0:1], lamv[:, 1:2], ALU.mult).then_inc(lam_prod, 1)
            dve.tensor_tensor(lamv[:, 5:6], lamv[:, 2:3], lamv[:, 3:4], ALU.mult).then_inc(lam_prod, 1)
            dve.tensor_scalar(sinkn[:, :], sinkb[:, :], -1.0, None, ALU.mult).then_inc(lam_ready, 1)
            for g in range(PAR_GROUPS):
                m = min(P, N_PAR - g * P)
                dve.wait_ge(row_turned, 9 + g + 1)
                dve.tensor_copy(par[:, g * P:g * P + m], bank[:, (9 + g) % 8, 0:m]).then_inc(par_ready, 1)
            dve.wait_ge(lam_exp, 1)
            dve.tensor_tensor(lam[:, 2:3], lam[:, 1:2], lam[:, 0:1], ALU.subtract).then_inc(lam_ready, 1)
            dve.wait_ge(par_ready, PAR_GROUPS)
            dve.tensor_scalar(subg[:, :], column("subln"), 1.0 - LAM_INIT, None, ALU.mult).then_inc(lam_ready, 1)
            dve.tensor_scalar(qkgain[:, 0:AT_HEADS], column("attn_q_norm_2").to_broadcast([P, AT_HEADS]), AT_HD ** -0.5,
                              None, ALU.mult).then_inc(lam_ready, 1)
            dve.tensor_scalar(qkgain[:, AT_HEADS:], column("attn_k_norm_2").to_broadcast([P, AT_KV]), 1.0, None, ALU.mult)\
               .then_inc(lam_ready, 1)
            dve.wait_ge(lam_ready, 2)
            dve.tensor_scalar(lam[:, 3:4], lam[:, 2:3], -LAM_INIT, None, ALU.add).then_inc(lam_ready, 1)

            def inverse(use, T, sums, width=D):
                dve.tensor_scalar(msq[:, 0:T], sums, 1.0 / width, EPS, ALU.mult, ALU.add).then_inc(mean_eps, 1)
                dve.wait_ge(mean_eps, use + 1)
                dve.reciprocal(msq[:, 0:T], msq[:, 0:T]).then_inc(inv_ready, 1)
                dve.wait_ge(rstd_ready, use + 1)

            def norm_before(b):
                T = T_PRE[b]
                dve.wait_ge(sq_used, KD * (b + 1))
                inverse(PRE(b), T, bank[:, 4, 0:T])
                for k in range(KD):
                    if k >= 2:
                        dve.wait_ge(act_ready, LO[f"norm{b}"] + k - 1)
                    dve.scalar_tensor_tensor(tmp[:, k % 2, 0:T], xT[:, k, 0:T], par[:, G_PRE[b] + k:G_PRE[b] + k + 1],
                                             rstd[:, 0:T], ALU.mult, ALU.mult).then_inc(h_ready, 1)

            def norm_after(b):
                T = T_POST[b]
                dve.wait_ge(mean_ready, b)
                inverse(POST(b), T, bank[:, 5, 0:T])
                if b == 4:
                    dve.wait_ge(x_back, 16)
                for k in range(KD + 1):
                    if k < KD:
                        if k >= 2:
                            dve.wait_ge(x_updated, KD * (b - 1) + k - 1)
                        dve.scalar_tensor_tensor(tmp[:, k % 2, 0:T], Y[b][:, k, 0:T],
                                                 par[:, G_POST[b] + k:G_POST[b] + k + 1], rstd[:, 0:T],
                                                 ALU.mult, ALU.mult).then_inc(y_scaled, 1)
                    if k >= 1:
                        dve.wait_ge(y_scaled, KD * (b - 1) + k)
                        dve.tensor_tensor(xT[:, k - 1, 0:T], xT[:, k - 1, 0:T], tmp[:, (k - 1) % 2, 0:T], ALU.add)\
                           .then_inc(x_updated, 1)

            norm_before(0)

            def branch_step(m):
                if m == 0:
                    dve.wait_ge(bias_in, 16)
                if m < 24:
                    head = m // 2 if m < 8 else m - 8 + DA_HEADS
                    dve.wait_ge(s_ready, m + 1)
                    if m >= 2:
                        dve.wait_ge(p_ready, 2 * m - 2)
                    dve.scalar_tensor_tensor(sbias[:, m % 2, 0:P], bank[:, 4 + m % 2, 0:P], HD ** -0.5,
                                             bias[:, head, P:TB], ALU.mult, ALU.add).then_inc(s_biased, 1)
                    dve.scalar_tensor_tensor(sbias[:, m % 2, P:384], bank[:, 4 + m % 2, P:384], HD ** -0.5,
                                             bias[:, head, :], ALU.mult, ALU.add).then_inc(s_biased, 1)
                    for q, (c0, c1) in enumerate(((0, P), (P, 384))):
                        dve.wait_ge(s_biased, 2 * m + q + 1)
                        dve.tensor_reduce(nmax[:, m, q:q + 1], sbias[:, m % 2, c0:c1], AX.X, ALU.max, negate=True)\
                           .then_inc(max_ready, 1)
                    if 8 <= m < 16:
                        dve.wait_ge(max_ready, 2 * m + 2)
                        dve.tensor_scalar(nmax[:, m, :], nmax[:, m, :], sinkn[:, m - 8:m - 7], None, ALU.min)\
                           .then_inc(max_sink, 1)
                if 1 <= m <= 24:
                    mm = m - 1
                    dve.wait_ge(p_ready, 2 * mm + 2)
                    if 8 <= mm < 16:
                        dve.wait_ge(sink_ready, mm - 8 + 1)
                        dve.tensor_tensor(ssum[:, mm, :], ssum[:, mm, :], esink[:, mm - 8, :], ALU.add).then_inc(sum_sink, 1)
                        dve.wait_ge(sum_sink, mm - 8 + 1)
                    dve.reciprocal(ssum[:, mm, :], ssum[:, mm, :]).then_inc(inv_sum, 1)
                    dve.wait_ge(inv_sum, mm + 1)
                    cols = ((0, P), (P, 384))
                    if mm >= 8:
                        for q, (c0, c1) in enumerate(cols):
                            dve.tensor_scalar(prob[:, mm % 4, c0:c1], prob[:, mm % 4, c0:c1], ssum[:, mm, q:q + 1], None,
                                              ALU.mult).then_inc(p_scaled, 1)
                    elif mm % 2:
                        dve.tensor_scalar(ssum[:, mm, :], ssum[:, mm, :], lam[:, 3:4], None, ALU.mult).then_inc(p_second, 1)
                        dve.wait_ge(p_second, 3 * (mm // 2) + 1)
                        for q, (c0, c1) in enumerate(cols):
                            dve.tensor_scalar(prob[:, mm % 4, c0:c1], prob[:, mm % 4, c0:c1], ssum[:, mm, q:q + 1], None,
                                              ALU.mult).then_inc(p_second, 1)
                        for q, (c0, c1) in enumerate(cols):
                            dve.wait_ge(p_second, 3 * (mm // 2) + 2 + q)
                            dve.scalar_tensor_tensor(prob[:, (mm - 1) % 4, c0:c1], prob[:, (mm - 1) % 4, c0:c1],
                                                     ssum[:, mm - 1, q:q + 1], prob[:, mm % 4, c0:c1], ALU.mult, ALU.add)\
                               .then_inc(p_scaled, 1)
                if m >= 4 and (m - 4) % 2 and (m - 4) // 2 >= DA_HEADS:
                    unit = (m - 4) // 2
                    dve.wait_ge(yhi_ready, unit - DA_HEADS + 1)
                    dve.tensor_tensor(ylo[:, unit, :], bank[:, 7, 0:TB], yhi[:, unit, :].bitcast(F32), ALU.subtract)\
                       .then_inc(o_free, 1)

            def branch_norm(j):
                if j in (3, 4):
                    c = j - 3
                    dve.wait_ge(a_summed, c + 1)
                    half = ors[:, 2 * c:2 * c + 2, :]
                    dve.tensor_scalar(half, bank[:, 4 + c, :].rearrange("p (h t) -> p h t", h=2), 1.0 / P, EPS,
                                      ALU.mult, ALU.add).then_inc(a_mean, 1)
                    dve.wait_ge(a_mean, c + 1)
                    dve.reciprocal(half, half).then_inc(a_inv, 1)
                if j == 5:
                    dve.wait_ge(a_rstd, 1)
                    dve.scalar_tensor_tensor(yn[:, :, :], osb[:, :, :], subg[:, 0:1], ors[:, :, :], ALU.mult, ALU.mult)\
                       .then_inc(a_normed, 1)

            def steps(ph):
                def after(i, j):
                    m = step_beside(ph, i, j)
                    if m is not None:
                        branch_step(m)
                    if ph == "gates" and i == 1:
                        branch_norm(j)
                return after

            stream("qkva")
            trip("qb", 0, after=steps("qb"))
            stream("kvb")
            trip("qkvc", 0, after=steps("qkvc"))
            for i in range(2):
                trip("gates", i, after=steps("gates"))
            with dve.Fori(2, TRIPS["gates"]) as i:
                trip("gates", i)

            def mix_out(i, chunk, u, n):
                for t in range(4):
                    dve.wait_ge(tile_pass, at(4 * u + t + 1, i, 4 * n))
                    if chunk == 0:
                        dve.wait_ge(act_ready, at(LO["mix"], i, 4))
                    if chunk == 2:
                        dve.wait_ge(mix_two, at(t + 1, i, 4))
                    dst = mixtmp[:, min(chunk, 1), t:t + 1, :]
                    b = 4 * (chunk % 2) + t
                    dve.tensor_tensor(dst, bank[:, b:b + 1, 0:TB], gate[:, bass.ds(i * 4 + (KD * chunk + t), 1), :],
                                      ALU.mult).then_inc(acc_free, 1)

            stream("oabc", mix_out)
            stream("wout")
            norm_after(1)
            norm_before(1)

            def up_out(i, chunk, u, n):
                for t in range(4):
                    r = (t % 2) + (t // 2) * FT + 2 * chunk
                    for back in (1, 2):
                        dve.wait_ge((tap2, tap1)[back - 1], at(4 * chunk + t + 1, i, 8))
                        tap = par[:, bass.ds(i * 4 + (PAR["conv_w"] + (2 - back) * 2 * FT + r), 1)]
                        dve.scalar_tensor_tensor(cv[:, t, back:TB], bank[:, 4 * chunk + t, 0:TB - back], tap,
                                                 cv[:, t, back:TB], ALU.mult, ALU.add).then_inc((tap1, acc_free)[back - 1], 1)
                for t in range(2):
                    dve.wait_ge(gelu_done, at(2 * chunk + t + 1, i, 4))
                    dve.wait_ge(acc_free, at(4 * (C0["up"] + chunk) + t + 3, i, 8))
                    dve.wait_ge(act_ready, at(LO["ff"] + 2 * chunk, i, 4))
                    dve.tensor_tensor(pr[:, t, :], cv[:, t, :], cv[:, 2 + t, :], ALU.mult).then_inc(ff_prod, 1)

            stream("up", up_out)
            stream("down")
            norm_after(2)
            norm_before(2)

            def qk_early(i, j):
                p, late = divmod(j, 2)
                if late:
                    dve.wait_ge(qk_rstd, at(p - 3, i, 4))
                    if not under(p - 4, i, 4, 2):
                        dve.wait_ge(qk_turned, at(p - 5, i, 4))
                        dve.wait_ge(qk_cos, at(p - 5, i, 4))
                    dve.scalar_tensor_tensor(n2[:, p % 2:p % 2 + 1, :], qk2[:, bass.ds(i * 4 + (p - 4), 1), :],
                                             qkgain[:, bass.ds(i * 4 + (p - 4), 1)], rs2[:, p % 2:p % 2 + 1, :],
                                             ALU.mult, ALU.mult).then_inc(qk_normed, 1)

            def qk_late(i, j):
                p, late = divmod(j, 2)
                if not late:
                    dve.wait_ge(qk_sum, at(p - 3, i, 4))
                    dve.tensor_scalar(rs2[:, p % 2, :], bank[:, 4 + p % 2, 0:T2], 1.0 / AT_HD, EPS, ALU.mult, ALU.add)\
                       .then_inc(qk_mean, 1)
                    dve.wait_ge(qk_mean, at(p - 3, i, 4))
                    dve.reciprocal(rs2[:, p % 2, :], rs2[:, p % 2, :]).then_inc(qk_inv, 1)
                else:
                    head = qk2[:, bass.ds(i * 4 + (p - 4), 1), :]
                    dve.wait_ge(qk_turned, at(p - 3, i, 4))
                    dve.tensor_tensor(head, bank[:, 6 + p % 2:7 + p % 2, 0:T2], sin[:, :].rearrange("p (o t) -> p o t", o=1),
                                      ALU.mult).then_inc(qk_sin, 1)
                    dve.wait_ge(qk_sin, at(p - 3, i, 4))
                    dve.wait_ge(qk_cos, at(p - 3, i, 4))
                    dve.tensor_tensor(head, head, nc2[:, p % 2:p % 2 + 1, :], ALU.add).then_inc(qk_done, 1)

            def gated(h):
                dve.wait_ge(acc_free, 4 * C0["ag"] + h + 1)
                dve.wait_ge(o2_taken, h + 1)
                dve.tensor_tensor(qk2[:, h, :], qk2[:, h, :], gs2[:, h, :], ALU.mult).then_inc(z2_ready, 1)

            def attend(s):
                h, second = divmod(s, 2)
                for q in ((0, 1), (2,))[second] if h < AT_HEADS else ():
                    rows = (P, P, TM)[q]
                    dve.wait_ge(s2_ready, 3 * h + q + 1)
                    dve.tensor_reduce(nm2[0:rows, h, q:q + 1], bank[0:rows, (4, 5, 4)[q], 0:T2], AX.X, ALU.max, negate=True)\
                       .then_inc(max2_ready, 1)
                if not second and 2 <= h < AT_HEADS + 2:
                    hh = h - 2
                    dve.wait_ge(o2_ready, hh + 1)
                    dve.tensor_copy(qk2[:, hh, :], bank[:, 7, 0:T2]).then_inc(o2_taken, 1)
                if second and 1 <= h <= AT_HEADS:
                    hh = h - 1
                    dve.wait_ge(p2_turned, 2 * hh + 1)
                    if hh >= 2:
                        dve.wait_ge(o2_ready, hh - 1)
                    dve.tensor_copy(pT2[:, hh % 2, 0:2, 0:TB], bank[:, 6, :].rearrange("p (k t) -> p k t", k=2)).then_inc(pT2_dve, 1)
                if second and h < AT_HEADS:
                    dve.wait_ge(p2_ready, 3 * h + 3)
                    dve.reciprocal(sum2[:, h, 0:2], sum2[:, h, 0:2]).then_inc(inv2, 1)
                    dve.reciprocal(sum2[0:TM, h, 2:3], sum2[0:TM, h, 2:3]).then_inc(inv2, 1)
                    dve.wait_ge(inv2, 2 * h + 2)
                    for q in range(3):
                        rows = (P, P, TM)[q]
                        dve.tensor_scalar(p2[0:rows, h % 2, q, :], p2[0:rows, h % 2, q, :], sum2[0:rows, h, q:q + 1], None,
                                          ALU.mult).then_inc(p2_scaled, 1)
                if second and s >= 17:
                    gated((s - 17) // 2)

            trip("aqk", 0)
            trip("aqk", 1, None, qk_early, qk_late)
            with dve.Fori(2, TRIPS["aqk"]) as i:
                trip("aqk", i, None, qk_early, qk_late)
            trip("av", 0, None, lambda i, j: qk_early(TRIPS["aqk"], j), lambda i, j: qk_late(TRIPS["aqk"], j))
            trip("av", 1, after=lambda i, j: attend(j))
            for i in range(TRIPS["ag"]):
                trip("ag", i, after=lambda i, j: attend(8 * (i + 1) + j))
            for h in range(12, AT_HEADS):
                gated(h)
            stream("aout")
            norm_after(3)
            norm_before(3)
            for ph in ("gqk", "lr"):
                stream(ph)

            def log_decay(g, j):
                if g == 0 and j == 0:
                    dve.wait_ge(x_parked, 16)
                    dve.wait_ge(gla_const, 64)
                if j == 0:
                    for t in range(4):
                        n = 4 * g + t
                        dve.wait_ge(z_abs, n + 1)
                        dve.tensor_scalar(cum[:, n, :], bank[:, 4 + t, 0:T2], column("gla_gk_bias_2", n), 0.0, ALU.add,
                                          ALU.min).then_inc(z_min, 1)
                if j == 3:
                    dve.wait_ge(z_ln, g + 1)
                    dve.wait_ge(z_min, 4 * g + 4)
                    dve.tensor_tensor(cum[:, 4 * g:4 * g + 4, :], cum[:, 4 * g:4 * g + 4, :], zabs[:, g % 2, :, :], ALU.subtract)\
                       .then_inc(z_sub, 1)
                if j >= 4:
                    n = 4 * g + j - 4
                    dve.wait_ge(z_sub, g + 1)
                    if n < KT:
                        dve.tensor_tensor_scan(cum[:, n, :], reset[:, :], cum[:, n, :], 0.0, ALU.mult, ALU.add)\
                           .then_inc(cum_ready, 1)
                    else:
                        back = cum[:, n, 0:TB][:, ::-1]
                        dve.tensor_tensor_scan(back, reset[:, 0:TB], back, 0.0, ALU.mult, ALU.add).then_inc(cum_ready, 1)

            for g in range(TRIPS["gv"]):
                trip("gv", g, after=log_decay)

            def spread(ap, n):
                return bass.AP(tensor=ap.tensor, offset=ap.offset, ap=[list(d) for d in ap.ap] + [[0, n]])

            def to_ends(h):
                lf, lb = cum[:, 2 * h:2 * h + 2, :], cum[:, 8 + 2 * h:10 + 2 * h, 0:TB]
                chunks = "p k (c t) -> p k c t"
                dve.wait_ge(cum_ready, 16)
                if h:
                    dve.wait_ge(ke_turned, 3 * h)
                dve.tensor_tensor(kendf[:, :, 0:TB].rearrange(chunks, t=GL_CHUNK),
                                  spread(lf[:, :, GL_CHUNK - 1:TB:GL_CHUNK], GL_CHUNK),
                                  lf[:, :, 0:TB].rearrange(chunks, t=GL_CHUNK), ALU.subtract).then_inc(d_sub, 1)
                dve.tensor_tensor(kendf[:, :, TB:T2], lf[:, :, T2 - 1:T2].to_broadcast([P, 2, TM]), lf[:, :, TB:T2],
                                  ALU.subtract).then_inc(d_sub, 1)
                dve.tensor_tensor(kendb[:, :, :].rearrange(chunks, t=GL_CHUNK), spread(lb[:, :, 0:TB:GL_CHUNK], GL_CHUNK),
                                  lb.rearrange(chunks, t=GL_CHUNK), ALU.subtract).then_inc(d_sub, 1)

            def state(h, s):
                d, k = s % 2, s // 2
                st = (stf, stb)[d]
                added = (k - 1, 3 - k)[d]
                for f in range(2):
                    dve.wait_ge(ds_ready, 14 * h + 2 * s + f + 1)
                    if k == 0:
                        dve.tensor_copy(st[:, 0, f, :], bank[:, 4 + f, :]).then_inc(st_ready, 1)
                    else:
                        dve.wait_ge(st_ready, 14 * h + 2 * (s - 2) + f + 1)
                        dve.scalar_tensor_tensor(st[:, k % 2, f, :], st[:, (k - 1) % 2, f, :], dec[:, d, f, added:added + 1],
                                                 bank[:, 4 + f, :], ALU.mult, ALU.add).then_inc(st_ready, 1)

            def gla(h, j):
                if j == 0 and h == 0:
                    to_ends(0)
                if j == 0:
                    for d in range(2):
                        dve.wait_ge(e_q, 2 * h + d + 1)
                        dve.scalar_tensor_tensor(qdec[:, d, :, :], qdec[:, d, :, :], GL_K ** -0.5,
                                                 gqk[:, 2 * h:2 * h + 2, 0:TB], ALU.mult, ALU.mult).then_inc(q_dec, 1)
                if j == 1 and h:
                    dve.wait_ge(o3_sum, h)
                    dve.tensor_scalar(msq[:, 0:TB], bank[:, 4, 0:TB], 1.0 / GL_V, EPS, ALU.mult, ALU.add).then_inc(o3_mean, 1)
                    dve.wait_ge(o3_mean, h)
                    dve.reciprocal(msq[:, 0:TB], msq[:, 0:TB]).then_inc(o3_inv, 1)
                if j == 2 and h < GL_HEADS:
                    dve.wait_ge(ke_turned, 3 * h + 3)
                    dve.tensor_copy(keT[:, 1, :, :], bank[:, 5, :].rearrange("p (t k) -> p t k", t=2)).then_inc(ke_dve, 1)
                if j == 2 and h:
                    dve.wait_ge(o3_rstd, h)
                    for v in range(4):
                        dve.scalar_tensor_tensor(osq3[:, v, :], bank[:, 6 + v // 2, (v % 2) * TB:(v % 2 + 1) * TB],
                                                 column("gla_o_norm_2", v), rstd[:, 0:TB], ALU.mult, ALU.mult)\
                           .then_inc(o3_scaled, 1)
                    dve.wait_ge(o3_scaled, 4 * h)
                    dve.wait_ge(acc_free, 4 * (C0["gg"] + h))
                    z = gg[:, 4 * h - 4:4 * h, :]
                    dve.tensor_tensor(z, osq3[:, :, :], z, ALU.mult).then_inc(z3_ready, 1)
                if j == 3:
                    other = tmp[:, 0, 0:TB].rearrange("p (t c) -> p t c", t=2)
                    for d, (dst, mask) in enumerate(((sc[:, :, :], maskf), (other, maskb))):
                        dve.wait_ge(sc_sum, 2 * h + d + 1)
                        both = bass.AP(tensor=mask[:, :].tensor, offset=mask[:, :].offset,
                                       ap=[list(mask[:, :].ap[0]), [0, 2], list(mask[:, :].ap[1])])
                        dve.tensor_tensor(dst, bank[:, 4 + d, 0:TB].rearrange("p (t c) -> p t c", t=2), both, ALU.mult)\
                           .then_inc(sc_part, 1)
                    dve.wait_ge(sc_part, 2 * h + 2)
                    dve.tensor_tensor(sc[:, :, :], sc[:, :, :], other, ALU.add).then_inc(sc_ready, 1)
                if j >= 4:
                    dve.wait_ge(e_dec, 3 * h + 3)
                    for s in (2 * j - 8, 2 * j - 7)[:7 - (2 * j - 8)]:
                        state(h, s)
                if j == 5 and h + 1 < GL_HEADS:
                    to_ends(h + 1)

            for h in range(GL_HEADS):
                trip("gg", h, after=gla)
            for j in range(1, 3):
                gla(GL_HEADS, j)
            with dve.Fori(0, TRIPS["gout"] - 1) as i:
                trip("gout", i)
            trip("gout", TRIPS["gout"] - 1)
            norm_after(4)

        @block.tensor
        def _(pe):
            PASSES = ((0, 0), (0, 1), (1, 0))

            def unit_begin(ph, i, j):
                n = UNITS[ph]
                u = U0[ph] + j
                pe.wait_ge(wlo_ready, at(u + 1, i, n))
                chunk, begins, ends = chunk_of(ph, j)
                return u, C0[ph] + chunk, begins, ends

            def bank_free(ph, c, t, i):
                if not under(c, i, CHUNKS[ph], 1):
                    pe.wait_ge(acc_free, at(4 * (c - 1) + t + 1, i, 4 * CHUNKS[ph]))

            def features(ph, i, j, rhs, T):
                u, c, begins, ends = unit_begin(ph, i, j)
                k0, nk = unit_tiles(ph, j)
                w = [t[:, u % RING, :].rearrange("p (k n) -> p k n", k=2 if nk == 1 else nk) for t in (whi, wlo)]
                of_unit = (0, 1, 2, 3)
                if ph == "up":
                    of_unit, begins, ends = ((0, 1), (2, 3))[j % 2], j % 8 < 2, j % 8 > 5
                turns = ph == "up" or ph == "oabc" and chunk_of(ph, j)[0] > 0
                base = 4 * (chunk_of(ph, j)[0] % 2) if turns else 0
                for t in of_unit:
                    col = t * P if ph != "up" else (t % 2) * P
                    if begins:
                        bank_free(ph, c - 1 if turns else c, t, i)
                    for k in range(nk):
                        for wp, ap in PASSES:
                            mm = pe.matmul(bank[:, base + t, 0:T], w[wp][:, k, col:col + P], rhs(ap, k0 + k),
                                           start=begins and k == 0 and (wp, ap) == (0, 0),
                                           stop=ends and k == nk - 1 and wp == 1)
                    mm.then_inc(tile_pass, 4 // len(of_unit))

            def tokens(ph, i, j, n_tiles, passes, first_bank=0, cols=(0, 512), begun=None):
                u, c, begins, ends = unit_begin(ph, i, j) if begun is None else begun
                k0, nk = unit_tiles(ph, j)
                w = [t[:, u % RING, :].rearrange("p (k n) -> p k n", k=nk) for t in (whi, wlo)]
                for tt in range(n_tiles):
                    if begins:
                        bank_free(ph, c, first_bank + tt, i)
                    for k in range(nk):
                        for wp, ap in PASSES:
                            mm = pe.matmul(bank[:, first_bank + tt, 0:cols[1] - cols[0]], ha((ahi, alo)[ap], k0 + k, tt * P, P),
                                           w[wp][:, k, cols[0]:cols[1]],
                                           start=begins and k == 0 and (wp, ap) == (0, 0),
                                           stop=ends and k == nk - 1 and wp == 1)
                    mm.then_inc(tile_pass, passes[tt])

            def model(T):
                return lambda part, k: ha((ahi, alo)[part], k, 0, T)

            def feature_stream(ph, T, made=None, per_unit=2, base=0, rhs=None):
                with pe.Fori(0, TRIPS[ph]) as i:
                    for j in range(UNITS[ph]):
                        if made is not None:
                            pe.wait_ge(made, base + per_unit * (j + 1))
                        features(ph, i, j, rhs or model(T), T)

            pe.wait_ge(rows_in, 64)
            for g in range(8):
                tt, k = g // 4, 4 * (g % 4)
                for n in range(4):
                    mm = pe.transpose(bank[:, g % 8, n * P:(n + 1) * P], xrow[:, tt, (k + n) * P:(k + n + 1) * P], ident[:, :])
                mm.then_inc(row_turned, 1)
            pe.wait_ge(row_taken, 1)
            for k in range(KD):
                mm = pe.transpose(bank[:, 0, k * TM:(k + 1) * TM], mrow[:, k * P:(k + 1) * P], ident[0:TM, 0:TM])
            mm.then_inc(row_turned, 1)
            pe.wait_ge(small_in, 16 * N_SMALL)
            for g in range(PAR_GROUPS):
                m = min(P, N_PAR - g * P)
                pe.wait_ge(row_taken, (9 + g) - 8 + 1)
                pe.transpose(bank[:, (9 + g) % 8, 0:m], prow[0:m, g, :], ident[0:m, 0:m]).then_inc(row_turned, 1)
            pe.wait_ge(lam_prod, 2)
            pe.wait_ge(start_set, 2)
            pe.wait_ge(row_taken, 7)
            pe.matmul(bank[:, 6, 0:2], ones[0:HD, :], lamv[:, 4:6], start=True, stop=True).then_inc(lam_sum, 1)
            pe.wait_ge(hots_in, 48)
            pe.wait_ge(par_ready, PAR_GROUPS)
            for w in range(2):
                pe.matmul(bank[0:N_HEADS, 4 + w, 0:LINE], tabx[:, :], hots[:, w, :], start=True, stop=True).then_inc(line_sum, 1)

            def norm_before(b):
                T = T_PRE[b]
                if b == 0:
                    pe.wait_ge(line_ready, 2)
                for k in range(KD):
                    pe.wait_ge(sq_ready, KD * b + k + 1)
                    pe.matmul(bank[:, 4, 0:T], ones[:, :], sqb[:, k % 2, 0:T], start=k == 0, stop=k == KD - 1).then_inc(sq_used, 1)

            def norm_after(b):
                T = T_POST[b]
                pe.wait_ge(y_summed, (KD + 1) * b)
                pe.matmul(bank[:, 5, 0:T], ones[:, :], sqacc[:, 0:T], start=True, stop=True).then_inc(mean_ready, 1)

            norm_before(0)
            pe.wait_ge(spare_set, 2)

            def branch_step(m):
                read = {0: ("qkva", 2), 4: ("qkva", 3), 8: ("kvb", 1), 16: ("qkvc", 2), 20: ("qkvc", 3)}.get(m)
                if read:
                    pe.wait_ge(acc_free, 4 * (C0[read[0]] + read[1]))
                if m < 24:
                    r = 64 * (m % 2)
                    if m < 8:
                        q, k = qaT[r:r + 64, m // 2, :], kaT[r:r + 64, m // 2, :]
                    elif m < 16:
                        q, k = qbT[r:r + 64, (m - 8) // 2, :], kbT[r:r + 64, int((m - 8) // 4 != m % 2), :]
                    else:
                        q, k = qcT[r:r + 64, (m - 16) // 2, :], kcT[r:r + 64, (m - 16) // 2, :]
                    if m >= 2:
                        pe.wait_ge(s_biased, 2 * (m - 1))
                    pe.matmul(bank[:, 4 + m % 2, 0:P], q[:, 0:P], k[:, 0:P], start=True, stop=True)
                    pe.matmul(bank[:, 4 + m % 2, P:384], q[:, P:TB], k[:, :], start=True, stop=True).then_inc(s_ready, 1)
                if m >= 2 and ends_job(m - 2):
                    mm_, job = m - 2, job_of(m - 2)
                    src = prob[:, (mm_ if mm_ >= 8 else mm_ - 1) % 4, :]
                    pe.wait_ge(p_scaled, 2 * job + 2)
                    if job >= 1:
                        pe.wait_ge(pT_ready, job)
                    for c in range(3):
                        mm = pe.transpose(bank[:, 6, c * P:(c + 1) * P], src[:, c * P:(c + 1) * P], ident[:, :])
                    mm.then_inc(p_turned, 1)
                if m >= 4 and ends_job(m - 4):
                    mm_, job = m - 4, job_of(m - 4)
                    unit = mm_ // 2
                    pe.wait_ge(pT_ready, job + 1)
                    if mm_ < 8 or mm_ % 2 == 0:
                        pe.wait_ge(o_free, unit)
                    if mm_ < 8:
                        o, v = bank[:, 7, 0:TB], [vatok[:, tt, P * unit:P * unit + P] for tt in range(2)]
                    else:
                        r = 64 * (mm_ % 2)
                        o = bank[r:r + 64, 7, 0:TB]
                        if mm_ < 16:
                            kv = (mm_ - 8) // 4
                            v = [vbtok[:, tt, 64 * kv:64 * kv + 64] for tt in range(2)]
                        else:
                            v = [vctok[:, tt, 64 * (mm_ - 16):64 * (mm_ - 16) + 64] for tt in range(2)]
                    pe.matmul(o, v[0], probT[:, job % 2, 0:TB], start=True, stop=False)
                    pe.matmul(o[:, P:TB], v[1], probT[:, job % 2, TB:384], start=False, stop=True).then_inc(o_ready, 1)

            def beside(ph, i, j):
                m = step_beside(ph, i, j)
                if m is not None:
                    branch_step(m)
                if ph == "gates" and (i, j) == (1, 3):
                    pe.wait_ge(a_squared, 1)
                    pe.wait_ge(s_biased, 48)
                    for c in range(2):
                        pe.matmul(bank[:, 4 + c, :], ones[:, :], osq[:, 2 * c:2 * c + 2, :].rearrange("p h t -> p (h t)"),
                                  start=True, stop=True).then_inc(a_summed, 1)

            def qkv(ph):
                for j in range(UNITS[ph]):
                    if ph == "qkva" and j < 8:
                        pe.wait_ge(act_ready, 2 * j + 2)
                    if j < 16:
                        features(ph, 0, j, model(TB), TB)
                    else:
                        tokens(ph, 0, j, 2, (1, 3))
                    beside(ph, 0, j)

            qkv("qkva")
            for j in range(UNITS["qb"]):
                features("qb", 0, j, model(TB), TB)
                beside("qb", 0, j)
            for j in range(UNITS["kvb"]):
                unit = unit_begin("kvb", 0, j)
                u, c, begins, ends = unit
                k0, nk = unit_tiles("kvb", j)
                w = [t[:, u % RING, :].rearrange("p (k n) -> p k n", k=nk) for t in (whi, wlo)]
                if begins:
                    bank_free("kvb", c, 0, 0)
                for k in range(nk):
                    for wp, ap in PASSES:
                        mm = pe.matmul(bank[:, 0, 0:TB], w[wp][:, k, 0:P], ha((ahi, alo)[ap], k0 + k, 0, TB),
                                       start=begins and k == 0 and (wp, ap) == (0, 0), stop=ends and k == nk - 1 and wp == 1)
                mm.then_inc(tile_pass, 1)
                tokens("kvb", 0, j, 2, (1, 2), first_bank=1, cols=(P, 2 * P), begun=unit)

            qkv("qkvc")
            for i in range(2):
                for j in range(UNITS["gates"]):
                    features("gates", i, j, model(TB), TB)
                    beside("gates", i, j)
            with pe.Fori(2, TRIPS["gates"]) as i:
                for j in range(UNITS["gates"]):
                    features("gates", i, j, model(TB), TB)
            pe.wait_ge(o_free, 12)
            pe.wait_ge(y_done, 1)
            with pe.Fori(0, TRIPS["oabc"]) as i:
                for j in range(UNITS["oabc"]):
                    branch = chunk_of("oabc", j)[0]
                    features("oabc", i, j, lambda part, k: (yhi, ylo)[part][:, 4 * branch + k, :], TB)
            feature_stream("wout", TB, act_ready, 2, LO["mix"])
            norm_after(1)
            norm_before(1)
            with pe.Fori(0, TRIPS["up"]) as i:
                for j in range(UNITS["up"]):
                    pe.wait_ge(act_ready, LO["norm1"] + 4 * (j % 8 // 2) + 4)
                    features("up", i, j, model(TB), TB)
            pe.wait_ge(act_ready, LO["ff"] + FT)
            feature_stream("down", TB, rhs=lambda part, k: (ghi, glo)[part][:, k, :])
            norm_after(2)
            norm_before(2)

            def qk_norm(i, j):
                p, late = divmod(j, 2)
                if not late:
                    pe.wait_ge(qk_sq, at(p - 3, i, 4))
                    if not under(p - 4, i, 4, 2):
                        pe.wait_ge(qk_mean, at(p - 5, i, 4))
                    pe.matmul(bank[:, 4 + p % 2, 0:T2], ones[:, :], sq2[:, p % 2, :], start=True, stop=True).then_inc(qk_sum, 1)
                else:
                    pe.wait_ge(qk_normed, at(p - 3, i, 4))
                    if not under(p - 4, i, 4, 2):
                        pe.wait_ge(qk_sin, at(p - 5, i, 4))
                    pe.matmul(bank[:, 6 + p % 2, 0:T2], turn[:, :], n2[:, p % 2, :], start=True, stop=True).then_inc(qk_turned, 1)

            TOK = ((0, P), (P, P), (TB, TM))

            def attend(s):
                h, second = divmod(s, 2)
                for q in ((0, 1), (2,))[second] if h < AT_HEADS else ():
                    c0, rows = TOK[q]
                    if s == 0 and q == 0:
                        pe.wait_ge(qk_done, 24)
                    if q == 0 and h:
                        pe.wait_ge(p2_ready, 3 * h)
                    if q == 1 and h >= 2:
                        pe.wait_ge(pT2_act, 2 * (h - 1))
                    if q == 2:
                        pe.wait_ge(p2_ready, 3 * h + 1)
                    pe.matmul(bank[0:rows, (4, 5, 4)[q], 0:T2], qk2[:, h, c0:c0 + rows], qk2[:, AT_HEADS + h // 2, :],
                              start=True, stop=True).then_inc(s2_ready, 1)
                if second and 1 <= h <= AT_HEADS:
                    hh = h - 1
                    pe.wait_ge(p2_scaled, 3 * hh + 3)
                    if hh:
                        pe.wait_ge(pT2_dve, hh)
                    for kt in range(2):
                        for q in range(2):
                            mm = pe.transpose(bank[:, 6, kt * TB + q * P:kt * TB + (q + 1) * P],
                                              p2[:, hh % 2, q, kt * P:(kt + 1) * P], ident[:, :])
                    mm.then_inc(p2_turned, 1)
                    if h < AT_HEADS:
                        pe.wait_ge(p2_ready, 3 * h + 2)
                    for kt in range(2):
                        pe.transpose(bank[:, 5, kt * TM:(kt + 1) * TM], p2[0:TM, hh % 2, 2, kt * P:(kt + 1) * P],
                                     ident[0:TM, 0:TM])
                    for q, (c0, rows) in enumerate(TOK):
                        mm = pe.transpose(bank[0:TM, 5, 2 * TM + c0:2 * TM + c0 + rows], p2[0:rows, hh % 2, q, TB:T2],
                                          ident[0:rows, 0:rows])
                    mm.then_inc(p2_turned, 1)
                if not second and 2 <= h < AT_HEADS + 2:
                    hh = h - 2
                    kv = hh // 2
                    pe.wait_ge(pT2_act, 2 * hh + 2)
                    pe.wait_ge(pT2_dve, hh + 1)
                    pe.wait_ge(acc_free, 4 * (C0["av"] + 1 + kv // 4))
                    if hh:
                        pe.wait_ge(o2_taken, hh)
                    for kt, (k0, krows) in enumerate(TOK):
                        mm = pe.matmul(bank[:, 7, 0:T2], v2[0:krows, kt, kv * P:(kv + 1) * P], pT2[0:krows, hh % 2, kt, :],
                                       start=kt == 0, stop=kt == 2)
                    mm.then_inc(o2_ready, 1)

            def aqk_trip(i, norms=True):
                for j in range(UNITS["aqk"]):
                    pe.wait_ge(act_ready, LO["norm2"] + 2 * (j + 1))
                    features("aqk", i, j, model(T2), T2)
                    if norms:
                        qk_norm(i, j)

            aqk_trip(0, norms=False)
            pe.wait_ge(rope_in, 48)
            aqk_trip(1)
            with pe.Fori(2, TRIPS["aqk"]) as i:
                aqk_trip(i)
            for i in range(TRIPS["av"]):
                for j in range(UNITS["av"]):
                    tokens("av", i, j, 3, (1, 1, 2))
                    if i == 0:
                        qk_norm(TRIPS["aqk"], j)
                    else:
                        attend(j)
            for i in range(TRIPS["ag"]):
                for j in range(UNITS["ag"]):
                    features("ag", i, j, model(T2), T2)
                    attend(8 * (i + 1) + j)
            feature_stream("aout", T2, act_ready, 2, LO["z2"])
            norm_after(3)
            norm_before(3)
            feature_stream("gqk", T2, act_ready, 2, LO["norm3"])
            u, c, _, _ = unit_begin("lr", 0, 0)
            for d in range(2):
                bank_free("lr", c, d, 0)
                for k in range(KD):
                    col = (2 * k + d) * GL_RANK
                    for wp, ap in PASSES:
                        mm = pe.matmul(bank[:, d, 0:T2], (whi, wlo)[wp][:, u % RING, col:col + P], ha((ahi, alo)[ap], k, 0, T2),
                                       start=k == 0 and (wp, ap) == (0, 0), stop=k == KD - 1 and wp == 1)
                mm.then_inc(tile_pass, (1, 3)[d])

            def log_decay(g, j):
                if j == 0:
                    if g == 0:
                        pe.wait_ge(acc_free, 4 * (C0["lr"] + 1))
                        pe.wait_ge(gla_const, 64)
                    for n in range(4 * g, 4 * g + 4):
                        d, k = divmod(n, KT)
                        if n >= 4:
                            pe.wait_ge(z_min, n - 3)
                        pe.matmul(bank[:, 4 + n % 4, 0:T2], up_w[:, d, k * P:(k + 1) * P], lrT[:, d, :], start=True, stop=True)\
                          .then_inc(z_sum, 1)

            for g in range(TRIPS["gv"]):
                for j in range(UNITS["gv"]):
                    tokens("gv", g, j, 3, (1, 1, 2))
                    log_decay(g, j)

            def state_step(h, s):
                d, k = s % 2, s // 2
                for f in range(2):
                    if s:
                        pe.wait_ge(st_ready, 14 * h + 2 * (s - 1) + f + 1)
                    else:
                        pe.wait_ge(sc_part, 2 * h + f + 1)
                    if s == 0:
                        keys, vals = keTm[:, f * P:(f + 1) * P], v3[0:TM, 2, h * GL_V:(h + 1) * GL_V]
                    else:
                        cc = (k - 1, 3 - k)[d]
                        r = GL_CHUNK * (cc % 2)
                        keys = keT[r:r + GL_CHUNK, d, cc // 2, f * P:(f + 1) * P]
                        vals = v3[r:r + GL_CHUNK, cc // 2, h * GL_V:(h + 1) * GL_V]
                    pe.matmul(bank[:, 4 + f, :], keys, vals, start=True, stop=True).then_inc(ds_ready, 1)

            def from_state(h, s):
                d, k = s % 2, s // 2
                cc = (k, 2 - k)[d]
                pe.wait_ge(st_ready, 14 * h + 2 * s + 2)
                for v in range(4):
                    c0 = (v % 2) * TB + cc * GL_CHUNK
                    for f in range(2):
                        mm = pe.matmul(bank[:, 6 + v // 2, c0:c0 + GL_CHUNK], (stf, stb)[d][:, k % 2, f, v * P:(v + 1) * P],
                                       qdec[:, d, f, cc * GL_CHUNK:(cc + 1) * GL_CHUNK], start=False,
                                       stop=s == 6, skip_group_check=True)
                return mm

            def scores(h, d):
                pe.wait_ge(q_dec, 2 * h + d + 1)
                pe.wait_ge(k_inv, 2 * h + d + 1)
                for tt in range(2):
                    for f in range(2):
                        mm = pe.matmul(bank[:, 4 + d, tt * P:(tt + 1) * P], kinv[:, d, f, tt * P:(tt + 1) * P],
                                       qdec[:, d, f, tt * P:(tt + 1) * P], start=f == 0, stop=f == 1)
                mm.then_inc(sc_sum, 1)

            def turn_keys(t):
                for tt in range(2):
                    for f in range(2):
                        mm = pe.transpose(bank[:, 5, tt * GL_K + f * P:tt * GL_K + (f + 1) * P], t[:, f, tt * P:(tt + 1) * P],
                                          ident[:, :])
                mm.then_inc(ke_turned, 1)

            def gla(h, j):
                if j == 0 and h:
                    from_state(h - 1, 6).then_inc(o3_part, 1)
                if j == 1 and h:
                    for v in range(4):
                        pe.wait_ge(o3_sq, 2 * (h - 1) + v // 2 + 1)
                        mm = pe.matmul(bank[:, 4, 0:TB], ones[:, :], osq3[:, v, :], start=v == 0, stop=v == 3)
                    mm.then_inc(o3_sum, 1)
                if j == 1 and h < GL_HEADS:
                    pe.wait_ge(k_end, 2 * h + 1)
                    turn_keys(kendf)
                if j == 2:
                    if h:
                        pe.wait_ge(o3_mean, h)
                    for f in range(2):
                        mm = pe.transpose(bank[0:TM, 4, f * P:(f + 1) * P], kendf[:, f, TB:T2], ident[:, :])
                    mm.then_inc(ke_turned, 1)
                    pe.wait_ge(ke_act, 2 * h + 1)
                    pe.wait_ge(k_end, 2 * h + 2)
                    turn_keys(kendb)
                if j == 3:
                    pe.wait_ge(ke_act, 2 * h + 2)
                    scores(h, 0)
                    pe.wait_ge(ke_dve, h + 1)
                    scores(h, 1)
                if j == 4:
                    state_step(h, 0)
                    pe.wait_ge(sc_ready, h + 1)
                    if h:
                        pe.wait_ge(o3_scaled, 4 * h)
                    for v in range(4):
                        for tt in range(2):
                            c0 = (v % 2) * TB + tt * P
                            pe.matmul(bank[:, 6 + v // 2, c0:c0 + P], v3[:, tt, h * GL_V + v * P:h * GL_V + (v + 1) * P],
                                      sc[:, tt, :], start=v % 2 == 0 and tt == 0, stop=False, skip_group_check=True)
                    state_step(h, 1)
                if j >= 5:
                    s = 2 * j - 10
                    from_state(h, s)
                    state_step(h, s + 2)
                    from_state(h, s + 1)
                    if s + 3 < 7:
                        state_step(h, s + 3)

            for h in range(GL_HEADS):
                for j in range(UNITS["gg"]):
                    features("gg", h, j, model(TB), TB)
                    gla(h, j)
            for j in range(2):
                gla(GL_HEADS, j)
            with pe.Fori(0, TRIPS["gout"] - 1) as i:
                for j in range(8):
                    pe.wait_ge(act_ready, LO["z3"] + j // 2 + 1)
                    features("gout", i, j, model(TB), TB)
            for j in range(8):
                features("gout", TRIPS["gout"] - 1, j, model(TB), TB)
            norm_after(4)
            pe.wait_ge(acc_free, 4 * (C0["gout"] + TRIPS["gout"]))
            for tt in range(2):
                for g in range(4):
                    if (tt, g) == (1, 0):
                        pe.wait_ge(rstd_ready, POST(4) + 1)
                    for n in range(4):
                        k = 4 * g + n
                        pe.wait_ge(x_updated, KD * 3 + k + 1)
                        mm = pe.transpose(bank[:, 4 * tt + g, n * P:(n + 1) * P], xT[:, k, tt * P:(tt + 1) * P], ident[:, :])
                    mm.then_inc(out_turned, 1)

        @block.gpsimd
        def _(pool):
            pool.memset(ahi[:, KD * T2:].bitcast(F32), 0.0).then_inc(spare_set, 1)
            pool.memset(alo[:, KD * T2:].bitcast(F32), 0.0).then_inc(spare_set, 1)

            def low(dst, whole, high, done):
                pool.tensor_tensor(dst, whole, high.bitcast(F32), ALU.subtract).then_inc(done, 1)

            def norm_before(b):
                T = T_PRE[b]
                for k in range(KD):
                    pool.wait_ge(hhi_ready, KD * b + k + 1)
                    low(ha(alo, k, 0, T), tmp[:, k % 2, 0:T], ha(ahi, k, 0, T), act_ready)

            def sum_squares(b):
                ph, T = OUT_STREAM[b], T_POST[b]
                if b > 1:
                    pool.wait_ge(mean_ready, b - 1)
                pool.memset(sqacc[:, :], 0.0).then_inc(y_summed, 1)
                with pool.Fori(0, TRIPS[ph]) as i:
                    for t in range(4):
                        pool.wait_ge(acc_free, at(4 * C0[ph] + t + 1, i, 4))
                        y = Y[b][:, bass.ds(i * 4 + t, 1), 0:T]
                        pool.tensor_tensor(sqb[:, t % 2:t % 2 + 1, 0:T], y, y, ALU.mult).then_inc(y_squared, 1)
                        pool.wait_ge(y_squared, at(KD * (b - 1) + t + 1, i, 4))
                        pool.wait_ge(y_summed, at((KD + 1) * (b - 1) + t + 1, i, 4))
                        pool.tensor_tensor(sqacc[:, 0:T], sqacc[:, 0:T], sqb[:, t % 2, 0:T], ALU.add).then_inc(y_summed, 1)

            norm_before(0)
            pool.wait_ge(ya_hi, 1)
            low(ylo[:, 0:DA_HEADS, :], yn[:, :, :], yhi[:, 0:DA_HEADS, :], y_done)
            with pool.Fori(0, TRIPS["oabc"]) as i:
                for chunk in (1, 2):
                    for t in range(4):
                        pool.wait_ge(acc_free, at(4 * (C0["oabc"] + chunk) + t + 1, i, 12))
                        if chunk == 2:
                            pool.wait_ge(mix_two, at(t + 1, i, 4))
                        pool.tensor_tensor(mixtmp[:, 0, t, :], mixtmp[:, 0, t, :], mixtmp[:, 1, t, :], ALU.add)\
                            .then_inc((mix_two, mix_sum)[chunk - 1], 1)
                for t in range(4):
                    pool.wait_ge(mix_part, at(t + 1, i, 4))
                    low(alo_tile(i, t), mixtmp[:, 0, t:t + 1, :], ahi_tile(i, t), act_ready)
            sum_squares(1)
            norm_before(1)
            with pool.Fori(0, TRIPS["up"]) as i:
                for t in range(4):
                    pool.wait_ge(ffhi_ready, at(t + 1, i, 4))
                    low(glo[:, bass.ds(i * 4 + t, 1), :], pr[:, t % 2:t % 2 + 1, :], ghi[:, bass.ds(i * 4 + t, 1), :], act_ready)
            sum_squares(2)
            norm_before(2)
            pool.wait_ge(rope_in, 48)
            for n in range(24):
                pool.wait_ge(qk_normed, n + 1)
                if n >= 2:
                    pool.wait_ge(qk_done, n - 1)
                pool.tensor_tensor(nc2[:, n % 2, :], n2[:, n % 2, :], cos[:, :], ALU.mult).then_inc(qk_cos, 1)
            for h in range(AT_HEADS):
                pool.wait_ge(z2hi, h + 1)
                low(ha(alo, h, 0, T2), qk2[:, h, :], ha(ahi, h, 0, T2), act_ready)
            sum_squares(3)
            norm_before(3)
            for h in range(GL_HEADS):
                keys = gqk[:, KT + 2 * h:KT + 2 * h + 2, :]
                for d, (t, T) in enumerate(((kendf, T2), (kendb, TB))):
                    pool.wait_ge(e_d, 2 * h + d + 1)
                    pool.tensor_tensor(t[:, :, :], t[:, :, :], keys[:, :, 0:T], ALU.mult).then_inc(k_end, 1)
                for d in range(2):
                    pool.wait_ge(e_k, 2 * h + d + 1)
                    pool.tensor_tensor(kinv[:, d, :, :], kinv[:, d, :, :], keys[:, :, 0:TB], ALU.mult).then_inc(k_inv, 1)
            for h in range(GL_HEADS):
                pool.wait_ge(z3hi, h + 1)
                tiles = [t[:, 0:KD * T2].rearrange("p (k t) -> p k t", t=T2)[:, 4 * h:4 * h + 4, 0:TB] for t in (alo, ahi)]
                low(tiles[0], gg[:, 4 * h:4 * h + 4, :], tiles[1], act_ready)
            sum_squares(4)


INS = ["x", "rel_bias_table", "w_in", "b_gate", "lam_q1", "lam_k1", "lam_q2", "lam_k2", "diff_subln_g", "sinks", "w_oa",
       "w_ob", "w_oc", "w_out", "pre_mix_g", "post_mix_g", "pre_ffn_g", "post_ffn_g", "w_up", "conv_w", "conv_b", "w_down",
       "meta_tokens_2", "pre_norm_2", "post_norm_2", "attn_w_in_2", "attn_q_norm_2", "attn_k_norm_2", "attn_w_out_2",
       "gla_w_in_2", "gla_gk_up_2", "gla_gk_bias_2", "gla_o_norm_2", "gla_w_out_2"]


def kernel(**inputs):
    import concourse.bacc as bacc
    from concourse.bass_utils import run_bass_kernel_spmd

    nc = bacc.Bacc("TRN2", target_bir_lowering=False, num_devices=1, dynamic_dma_scratch_size=64)
    arrays = {name: np.ascontiguousarray(inputs[name]) for name in INS}
    arrays |= shape_constants()
    access = {name: nc.dram_tensor(f"in_{name}", a.shape, mybir.dt.from_np(a.dtype), kind="ExternalInput").ap()
              for name, a in arrays.items()}
    access["subln"] = access["diff_subln_g"]
    out = nc.dram_tensor("out", (TB, D), F32, kind="ExternalOutput").ap()
    two_blocks_kernel(nc, access, out)
    result = run_bass_kernel_spmd(nc, [{f"in_{name}": a for name, a in arrays.items()}], core_ids=[0])
    return result.results[0]["out"].reshape(1, TB, D)
```

```python
import math
from contextlib import ExitStack

import numpy as np

import concourse.bass as bass
from concourse import mybir

F32 = mybir.dt.float32
F32R = mybir.dt.float32r
ALU = mybir.AluOpType
ACT = mybir.ActivationFunctionType
AX = mybir.AxisListType

P = 128
D = 2048
KD = D // P
TB = 256
TM = 16
T2 = TB + TM
EPS = 1e-6

DA_HEADS, SW_HEADS, MB_HEADS, HD = 4, 8, 8, 64
N_HEADS = DA_HEADS + SW_HEADS + MB_HEADS
WINDOW = 128
N_BUCKETS, MAX_DIST = 32, 128
QKV = 512
IN_GATES = 3 * QKV + QKV + 2 * P + 3 * QKV
D_FF = 5632
FT = D_FF // P
LAM_INIT = 0.8 - 0.6 * math.exp(-0.3 * 0)
MASKED = -float(2 ** 100)
LINE = 2 * P + P - 1

AT_HEADS, AT_KV, AT_HD = 16, 8, 128
GRID_W, ROPE_THETA, ROPE_AXIS = 64, 10000.0, 64
GL_HEADS, GL_K, GL_V, GL_RANK, GL_CHUNK = 4, 256, 512, 16, 64
GL_NORMALIZER = 16.0
KT = 8

UNIT = 1024
RAW, RING, LEAD = 8, 4, 3

STREAM = [("qkva", 1, 24, 3), ("qb", 1, 8, 1), ("kvb", 1, 4, 1), ("qkvc", 1, 24, 3),
          ("gates", 12, 8, 1), ("oabc", 2, 16, 6),
          ("wout", 4, 8, 1), ("up", 11, 16, 2), ("down", 4, 24, 1), ("aqk", 6, 8, 1), ("av", 2, 8, 1),
          ("ag", 4, 8, 1), ("aout", 4, 8, 1), ("gqk", 4, 8, 1), ("lr", 1, 1, 1), ("gv", 4, 8, 1),
          ("gg", 4, 8, 1), ("gout", 2, 16, 2)]
TRIPS, UNITS, CHUNKS, U0, C0 = {}, {}, {}, {}, {}
_u = _c = 0
for _name, _trips, _units, _chunks in STREAM:
    TRIPS[_name], UNITS[_name], CHUNKS[_name], U0[_name], C0[_name] = _trips, _units, _chunks, _u, _c
    _u += _trips * _units
    _c += _trips * _chunks
N_UNITS = _u

PARAMS = [("pre_mix_g", 16), ("subln", 1), ("b_gate", 48), ("post_mix_g", 16), ("pre_ffn_g", 16), ("conv_w", 264),
          ("conv_b", 88), ("post_ffn_g", 16), ("pre_norm_2", 32), ("post_norm_2", 32), ("attn_q_norm_2", 1),
          ("attn_k_norm_2", 1), ("gla_gk_bias_2", 16), ("gla_o_norm_2", 4)]
PAR = {}
_r = 0
for _name, _rows in PARAMS:
    PAR[_name] = _r
    _r += _rows
N_PAR = _r
PAR_GROUPS = -(-N_PAR // P)
N_PIECES = sum((PAR[n] + r - 1) // P - PAR[n] // P + 1 for n, r in PARAMS)
FIRST_PIECES = sum(PAR[n] < P for n, r in PARAMS)


def at(const, trip, per_trip):
    return trip * per_trip + const


def under(const, trip, per_trip, bound):
    return isinstance(trip, int) and trip * per_trip + const < bound


def shape_constants():
    f32 = np.float32
    dist = 255 - np.arange(LINE)
    n = np.maximum(dist, 0)
    half = N_BUCKETS // 2
    large = half + (np.log(np.maximum(n, 1).astype(f32) / f32(half)) / f32(math.log(MAX_DIST / half))
                    * f32(N_BUCKETS - half)).astype(np.int32)
    bucket = np.where(n < half, n, np.minimum(large, N_BUCKETS - 1))

    def one_hot(valid):
        row = np.where(valid, bucket, N_BUCKETS)
        return (np.arange(N_BUCKETS + 1)[:, None] == row[None]).astype(f32)

    token = np.arange(TB)
    inv = f32(ROPE_THETA) ** (-np.arange(0, ROPE_AXIS, 2, dtype=f32) / f32(ROPE_AXIS))
    angle = np.zeros((P, T2), f32)
    for axis, pos in enumerate((token // GRID_W, token % GRID_W)):
        for half_ in range(2):
            r0 = axis * 64 + half_ * 32
            angle[r0:r0 + 32, :TB] = inv[:, None] * pos.astype(f32)[None]
    turn = np.zeros((P, P), f32)
    for d in range(P):
        if d % 64 < 32:
            turn[d + 32, d] = -1.0
        else:
            turn[d - 32, d] = 1.0
    s, c = np.arange(P)[:, None], np.arange(P)[None]
    same = s // GL_CHUNK == c // GL_CHUNK
    reset = np.ones((P, T2), f32)
    reset[:, 0:T2:GL_CHUNK] = 0.0
    return {
        "c_hot_full": one_hot(dist >= 0), "c_hot_window": one_hot((dist >= 0) & (dist < WINDOW)),
        "c_cos": np.cos(angle).astype(f32), "c_sin": np.sin(angle).astype(f32), "c_turn": turn,
        "c_ident": np.eye(P, dtype=f32), "c_mask_f": (same & (s <= c)).astype(f32),
        "c_mask_b": (same & (s > c)).astype(f32), "c_reset": reset,
    }


def two_blocks_kernel(nc, A, out):
    ctx = ExitStack()
    with ctx:
        place_at = [(nc.sbuf_base + 31) // 32 * 32]

        def sb(name, shape, dt=F32, at_=None):
            size = int(np.prod(shape[1:])) * 4
            off = place_at[0] if at_ is None else at_
            t = nc.alloc_sbuf_tensor_at(name, shape, dt, offset=off)
            if at_ is None:
                place_at[0] = off + (size + 31) // 32 * 32
            return t

        def sem(name):
            return ctx.enter_context(nc.semaphore(name))

        raw = sb("raw", [P, RAW, UNIT])
        whi = sb("whi", [P, RING, UNIT], F32R)
        wlo = sb("wlo", [P, RING, UNIT], F32R)
        act_at = place_at[0]
        ahi = sb("ahi", [P, KD * T2], F32R)
        alo = sb("alo", [P, KD * T2], F32R)
        par = sb("par", [P, N_PAR])
        ident = sb("ident", [P, P])
        ones = sb("ones", [P, P])
        lam = sb("lam", [P, 8])
        subg = lam[:, 4:5]
        eps = lam[:, 5:6]
        qkgain = sb("qkgain", [P, 24])
        xT_at = place_at[0]
        xT = sb("xT", [P, KD, T2])
        msq = sb("msq", [P, T2])
        rstd = sb("rstd", [P, T2])
        sqacc = sb("sqacc", [P, T2])
        tmp_at = place_at[0]
        tmp = sb("tmp", [P, 4, T2])
        R2 = place_at[0]
        LIMIT = nc.sbuf_usable_end

        def region(*parts):
            off, made = R2, []
            for name, shape, dt in parts:
                made.append(sb(name, shape, dt, at_=off))
                off += (int(np.prod(shape[1:])) * 4 + 31) // 32 * 32
            assert off <= LIMIT, (parts[0][0], off, LIMIT)
            return made

        def ha(t, k, c0, n):
            return t[:, k * T2 + c0:k * T2 + c0 + n]

        xn, xrow, mrow, prow, tabx, hots, line, lamv, xsum, xrstd = region(
            ("xn", [P, 2, D], F32), ("xrow", [P, 2, D], F32), ("mrow", [TM, D], F32), ("prow", [P, PAR_GROUPS, P], F32),
            ("tabx", [N_BUCKETS + 1, N_HEADS], F32), ("hots", [N_BUCKETS + 1, 2, LINE], F32),
            ("line", [N_HEADS, 2, LINE], F32), ("lamv", [HD, 6], F32),
            ("xsum", [P, 2], F32), ("xrstd", [P, 2], F32))
        (qaT, kaT, vatok, qbT, kbT, vbtok, qcT, kcT, vctok, bias, yhi, ylo, sbias, prob, probT, osb, sinkb, sinkn, nmax, ssum,
         esink) = region(
            ("qaT", [P, 4, TB], F32), ("kaT", [P, 4, TB], F32), ("vatok", [P, 2, QKV], F32),
            ("qbT", [P, 4, TB], F32), ("kbT", [P, 2, TB], F32), ("vbtok", [P, 2, P], F32),
            ("qcT", [P, 4, TB], F32), ("kcT", [P, 4, TB], F32), ("vctok", [P, 2, QKV], F32),
            ("bias", [P, N_HEADS, TB], F32), ("yhi", [P, 12, TB], F32R), ("ylo", [P, 12, TB], F32R),
            ("sbias", [P, 2, 384], F32), ("prob", [P, 4, 384], F32), ("probT", [P, 2, 384], F32),
            ("osb", [P, 4, TB], F32), ("sinkb", [P, SW_HEADS], F32), ("sinkn", [P, SW_HEADS], F32), ("nmax", [P, 24, 2], F32),
            ("ssum", [P, 24, 2], F32), ("esink", [P, 8, 2], F32))
        bias_at = R2 + 4 * (8 * TB * 2 + 4 * QKV + 4 * TB + 2 * TB + 2 * P)
        osq = sb("osq", [P, 4, TB], F32, at_=bias_at)
        ors = sb("ors", [P, 4, TB], F32, at_=bias_at + 4096)
        yn = sb("yn", [P, 4, TB], F32, at_=bias_at + 8192)
        (gate,) = region(("gate", [P, 48, TB], F32))
        assert R2 + 48 * TB * 4 <= bias_at + N_HEADS * TB * 4
        mixtmp = sb("mixtmp", [P, 2, 4, TB], F32, at_=bias_at + N_HEADS * TB * 4 + 24 * TB * 4)
        (yT,) = region(("yT", [P, KD, T2], F32))
        ghi, glo, cv, pr = region(("ghi", [P, FT, TB], F32R), ("glo", [P, FT, TB], F32R), ("cv", [P, 4, TB], F32),
                                  ("pr", [P, 2, TB], F32))
        yT_ffn = sb("yT_ffn", [P, KD, T2], F32, at_=act_at)
        FIRST_GATED = 4
        qk2, v2, gs2, cos, sin, turn, sq2, rs2, n2, nc2, p2, pT2, nm2, sum2, vt2, z2hi_first, z2lo_first = region(
            ("qk2", [P, 24, T2], F32), ("v2", [P, 3, 1024], F32), ("gs2", [P, KD, T2], F32), ("cos", [P, T2], F32),
            ("sin", [P, T2], F32), ("turn", [P, P], F32), ("sq2", [P, 2, T2], F32), ("rs2", [P, 2, T2], F32),
            ("n2", [P, 2, T2], F32), ("nc2", [P, 2, T2], F32), ("p2", [P, 2, 3, T2], F32), ("pT2", [P, 2, 3, T2], F32),
            ("nm2", [P, AT_HEADS, 3], F32), ("sum2", [P, AT_HEADS, 3], F32), ("vt2", [P, 2, 4, T2], F32),
            ("z2hi_first", [P, FIRST_GATED, T2], F32R), ("z2lo_first", [P, FIRST_GATED, T2], F32R))
        cum = sb("cum", [P, 16, T2], F32, at_=xT_at)
        (gqk, v3, gg, maskf, maskb, reset, vt3, qdec, kinv, kendf, kendb, kfar, kback, sc, scm, osq3, gainrow) = region(
            ("gqk", [P, 16, T2], F32), ("v3", [P, 3, D], F32), ("gg", [P, KD, TB], F32), ("maskf", [P, P], F32),
            ("maskb", [P, P], F32), ("reset", [P, T2], F32), ("vt3", [P, 2, 4, T2], F32), ("qdec", [P, 2, 2, TB], F32),
            ("kinv", [P, 2, 2, TB], F32), ("kendf", [P, 2, T2], F32), ("kendb", [P, 2, TB], F32), ("kfar", [P, 2, 240], F32),
            ("kback", [P, 2, 192], F32), ("sc", [P, 2, TB], F32), ("scm", [TM, TB], F32), ("osq3", [P, 4, TB], F32),
            ("gainrow", [P, D], F32))
        dec = sb("dec", [P, 2, 2, 4], F32, at_=tmp_at + 2 * T2 * 4)
        gate_at = R2 + 4 * (16 * T2 + 3 * D + KD * TB + 2 * P + T2 + 2 * 4 * T2)
        lrT = sb("lrT", [GL_RANK, 2, T2], F32, at_=gate_at)
        up_w = sb("up_w", [GL_RANK, 2, KT * P], F32, at_=gate_at + 2 * T2 * 4)
        zabs = sb("zabs", [P, 2, 4, T2], F32, at_=gate_at + 2 * T2 * 4 + 2 * KT * P * 4)
        z0_at = R2 + 4 * (16 * T2 + 3 * D + KD * TB + 2 * P + T2)
        z0hi = sb("z0hi", [P, 4, TB], F32R, at_=z0_at)
        z0lo = sb("z0lo", [P, 4, TB], F32R, at_=z0_at + 4 * 4 * TB)
        yrow = sb("yrow", [P, 2, D], F32, at_=R2)
        xback = sb("xback", [P, 2, D], F32, at_=xT_at)
        orow = sb("orow", [P, 2, D], F32, at_=R2 + KD * T2 * 4)
        ysum = sb("ysum", [P, 2, 4], F32, at_=tmp_at)
        yroot = sb("yroot", [P, 2], F32, at_=tmp_at + 32)
        xwait = sb("xwait", [P, 2, D], F32, at_=R2 + KD * T2 * 4)

        bank = ctx.enter_context(nc.psum_tensor("bank", [P, 8, 512], F32))

        def rows_of(w, c0, width, k0, nk):
            return w.rearrange("(k p) n -> p k n", p=P)[:, k0:k0 + nk, bass.ds(c0, width)]

        w_in, w_out, w_up, w_down = A["w_in"][0], A["w_out"][0], A["w_up"][0], A["w_down"][0]
        w_o = [A["w_oa"][0], A["w_ob"][0], A["w_oc"][0]]
        attn_in, attn_out = A["attn_w_in_2"][0], A["attn_w_out_2"][0]
        gla_in, gla_out = A["gla_w_in_2"][0], A["gla_w_out_2"][0]
        lines_dram = nc.dram_tensor("bias_lines", [N_HEADS, P, LINE + 1], F32, kind="Internal").ap()
        park_dram = nc.dram_tensor("parked_x", [P, 2 * D], F32, kind="Internal").ap()

        def unit_tiles(ph, j):
            if ph == "kvb":
                return 4 * j, 4
            if ph == "oabc":
                return (2 * (j % 2), 2) if j % 8 < 4 else (j % 8 - 4, 1)
            if ph == "down":
                return (2 * j, 2) if j < 20 else (20 + j, 1)
            if ph == "up":
                return 4 * (j % 8 // 2), 4
            if ph == "lr":
                return 0, KD
            return 2 * (j % 8), 2

        def chunk_of(ph, j):
            if ph == "kvb":
                return 0, j == 0, j == 3
            if ph == "oabc":
                return 3 * (j // 8) + min(j % 8 // 2, 2), j % 8 in (0, 2, 4), j % 8 in (1, 3, 7)
            if ph == "down":
                return 0, j == 0, j == 23
            if ph == "lr":
                return 0, True, True
            return j // 8, j % 8 == 0, j % 8 == 7

        def unit_source(ph, i, j):
            k0, nk = unit_tiles(ph, j)

            def col(c, per):
                return at(c, i, per)

            if ph in ("qkva", "qkvc"):
                first = 0 if ph == "qkva" else 3 * QKV + QKV + 2 * P
                return ((0, 1024), rows_of(w_in, first + QKV * (j // 8), QKV, k0, nk))
            if ph == "qb":
                return ((0, 1024), rows_of(w_in, 3 * QKV, QKV, k0, nk))
            if ph == "kvb":
                return ((0, 1024), rows_of(w_in, 4 * QKV, 2 * P, k0, nk))
            if ph == "gates":
                return ((0, 1024), rows_of(w_in, col(IN_GATES, 512), 512, k0, nk))
            if ph == "oabc":
                return ((0, nk * 512), rows_of(w_o[chunk_of(ph, j)[0] % 3], col(512 * (j // 8), 1024), 512, k0, nk))
            if ph == "up":
                return ((0, 1024), rows_of(w_up, col((j % 2) * D_FF + 256 * (j // 8), 512), 256, k0, nk))
            if ph == "down":
                return ((0, nk * 512), rows_of(w_down, col(0, 512), 512, k0, nk))
            if ph == "lr":
                return ((0, KD * 2 * GL_RANK), rows_of(gla_in, 3 * D, 2 * GL_RANK, 0, KD))
            w, c0 = {"wout": (w_out, 0), "aqk": (attn_in, 0), "av": (attn_in, 3072), "ag": (attn_in, 4096),
                     "aout": (attn_out, 0), "gqk": (gla_in, 0), "gv": (gla_in, 2048), "gg": (gla_in, 4096),
                     "gout": (gla_out, 0)}[ph]
            return ((0, 1024), rows_of(w, col(c0 + 512 * (j // 8), 512 * CHUNKS[ph]), 512, k0, nk))

        raw_loaded = [sem(f"raw_loaded{n}") for n in range(RAW)]
        whi_ready, wlo_ready, tile_pass, acc_free = map(sem, "whi_ready wlo_ready tile_pass acc_free".split())
        x_in = [sem("x_in0"), sem("x_in1")]
        ident_in, meta_in, first_in, small_in, lam_in, hots_in, start_set, table_in = map(
            sem, "ident_in meta_in first_in small_in lam_in hots_in start_set table_in".split())
        x_squared, x_root, x_rstd, xn_ready, xn_turned, par_turned, par_ready, row_turned, row_taken = map(
            sem, "x_squared x_root x_rstd xn_ready xn_turned par_turned par_ready row_turned row_taken".split())
        lam_prod, lam_sum, lam_exp, lam_ready = map(sem, "lam_prod lam_sum lam_exp lam_ready".split())
        line_sum, line_ready, lines_stored, bias_in = map(sem, "line_sum line_ready lines_stored bias_in".split())
        y_squared, y_summed, mean_ready, root_ready, rstd_ready, y_scaled, x_updated, y_scaled_last, x_updated_last, \
            sq_ready, sq_folded, sq_summed, h_ready, hhi_ready, act_ready = map(
                sem, "y_squared y_summed mean_ready root_ready rstd_ready y_scaled x_updated y_scaled_last x_updated_last "
                     "sq_ready sq_folded sq_summed h_ready hhi_ready act_ready".split())
        s_ready, s_biased, max_ready, max_sink, p_ready, sink_ready, sum_sink, inv_sum, p_second, p_scaled, \
            p_turned, pT_ready, o_ready, o_free, yhi_ready, a_out, a_squared, a_summed, a_root, a_rstd, \
            a_normed, ya_hi, y_done = map(
                sem, "s_ready s_biased max_ready max_sink p_ready sink_ready sum_sink inv_sum p_second p_scaled "
                     "p_turned pT_ready o_ready o_free yhi_ready a_out a_squared a_summed a_root a_rstd "
                     "a_normed ya_hi y_done".split())
        mix_two, mix_part, mix_sum = map(sem, "mix_two mix_part mix_sum".split())
        tap2, tap1, gelu_done, ff_prod, ffhi_ready = map(
            sem, "tap2 tap1 gelu_done ff_prod ffhi_ready".split())
        rope_in, qk_sq, qk_sum, qk_root, qk_rstd, qk_normed, qk_turned, qk_cos, qk_sin, qk_done = map(
            sem, "rope_in qk_sq qk_sum qk_root qk_rstd qk_normed qk_turned qk_cos qk_sin qk_done".split())
        s2_ready, max2_ready, p2_ready, inv2, p2_scaled, p2_turned, pT2_act, pT2_dve, o2_ready, o2_taken, z2_ready, v2_turned, v2_taken, \
            z2hi = map(sem, "s2_ready max2_ready p2_ready inv2 p2_scaled p2_turned pT2_act pT2_dve o2_ready o2_taken "
                            "z2_ready v2_turned v2_taken z2hi".split())
        x_parked, x_back, gla_const, z_sum, z_abs, z_min, z_exp, z_ln, z_sub, cum_ready, v3_turned, v3_taken = map(
            sem, "x_parked x_back gla_const z_sum z_abs z_min z_exp z_ln z_sub cum_ready v3_turned v3_taken".split())
        e_q, e_k, e_d, e_dec, d_sub, q_dec, k_inv, k_end, k_far, sc_sum, x_sum, xm_sum, sc_part, sc_own, sc_ready, scm_ready, \
            o3_ready, o3_sq, o3_sum, o3_root, o3_rstd, o3_scaled, z3_ready, z3hi = map(
                sem, "e_q e_k e_d e_dec d_sub q_dec k_inv k_end k_far sc_sum x_sum xm_sum sc_part sc_own sc_ready scm_ready "
                     "o3_ready o3_sq o3_sum o3_root o3_rstd o3_scaled z3_ready z3hi".split())
        xw_turned, xw_taken, gain_in, yr_squared, yr_gained, yr_sum, yr_root, yr_rstd, out_made, stored = map(
            sem, "xw_turned xw_taken gain_in yr_squared yr_gained yr_sum yr_root yr_rstd out_made stored".split())

        LO, lo_tiles = {}, 0
        for name, tiles in (("norm0", KD), ("mix", KD), ("norm1", KD), ("ff", FT), ("norm2", KD), ("z2", AT_HEADS),
                            ("norm3", KD), ("z3", GL_HEADS)):
            LO[name] = lo_tiles
            lo_tiles += tiles

        PRE, POST = (lambda b: 2 * b - 1), (lambda b: 2 * b - 2)
        T_PRE = [TB, TB, T2, T2]
        T_POST = [None, TB, TB, T2]
        G_PRE = [PAR["pre_mix_g"], PAR["pre_ffn_g"], PAR["pre_norm_2"], PAR["pre_norm_2"] + KD]
        G_POST = [None, PAR["post_mix_g"], PAR["post_ffn_g"], PAR["post_norm_2"]]
        AFTER_NORM = [None, "up", "aqk", "gqk"]
        OUT_STREAM = [None, "wout", "down", "aout"]
        Y = [None, yT, yT_ffn, yT]

        def job_of(m):
            return m // 2 if m < 2 * DA_HEADS else m - DA_HEADS

        def ends_job(m):
            return m < 24 and (m >= 2 * DA_HEADS or m % 2 == 1)

        def step_beside(ph, i, j):
            if ph == "qb":
                return j
            if ph == "qkvc" and j < 16 and j % 2 == 0:
                return 8 + j // 2
            if ph == "qkvc" and j in (17, 19, 21):
                return 16 + (j - 17) // 2
            if ph == "gates" and 8 * i + j < 10:
                return 19 + 8 * i + j
            return None

        UPDATE_ORDER = (0, 1, 3, 2)

        X_PIECES = [(tt, g) for tt in range(2) for g in range(4)]
        X_BANK = (6, 7, 4, 5)

        def gated(part, k):
            return (z0hi, z0lo)[part][:, k, :] if k < 4 else ha((ahi, alo)[part], k, 0, TB)

        OUT_PIECES = [(tt, c) for tt in range(2) for c in (0, D // 2)]

        def updated(eng, b, g):
            if g < 3:
                eng.wait_ge(x_updated, 3 * (b - 1) + g + 1)
            else:
                eng.wait_ge(x_updated_last, b)

        def over_tiles(ap):
            return ap.rearrange("p (o t) -> p o t", o=1).to_broadcast([P, 4, ap.shape[1]])

        def turned(k):
            return bank[:, 4 + k // 2 % 4, k % 2 * TB:(k % 2 + 1) * TB]

        PAR_BANK = (0, 4, 5, 6, 7)
        HEAD_AT = (4, 10, 18, 26)
        GATED_AT = tuple(max(8 * h + 7, HEAD_AT[h] + 5) for h in range(GL_HEADS))
        VALUE_STEPS = (0, 1, 2, 9, 11, 13)
        VALUE_BANK = (6, 7, 4)

        def z2_part(part, h):
            if h < FIRST_GATED:
                return (z2hi_first, z2lo_first)[part][:, h, :]
            return ha((ahi, alo)[part], h, 0, T2)

        def ahi_tile(i, t):
            return ahi[:, 0:KD * T2].rearrange("p (k t) -> p k t", t=T2)[:, bass.ds(i * 4 + t, 1), 0:TB]

        def alo_tile(i, t):
            return alo[:, 0:KD * T2].rearrange("p (k t) -> p k t", t=T2)[:, bass.ds(i * 4 + t, 1), 0:TB]

        def ring_waits(eng, ph, i, u, n, landed):
            if landed:
                eng.wait_ge(raw_loaded[u % RAW], at(16 * (u // RAW + 1), i, 2 * n))
            if not under(u, i, n, RING):
                eng.wait_ge(tile_pass, at(4 * (u - RING + 1), i, 4 * n))

        def load_parameters(eng, first):
            for name, rows in PARAMS:
                src = A[name][0] if name in ("conv_w", "gla_gk_bias_2") else A[name]
                flat = src.rearrange("w (r c) -> (w r) c", c=P)
                r = 0
                while r < rows:
                    g, p0 = divmod(PAR[name] + r, P)
                    m = min(rows - r, P - p0)
                    if first == (g == 0):
                        eng.dma_start(prow[p0:p0 + m, g, :], flat[r:r + m, :]).then_inc(first_in if first else small_in, 16)
                    r += m

        block = ctx.enter_context(nc.Block())

        @block.sync
        def _(sp):
            def load_trip(ph, i, first=0, last=None):
                n = UNITS[ph]
                for j in range(first, last or n):
                    u = U0[ph] + j
                    if not under(u, i, n, RAW):
                        sp.wait_ge(wlo_ready, at(u - RAW + 1, i, n))
                    (c0, c1), src = unit_source(ph, i, j)
                    dst = raw[:, u % RAW, c0:c1].rearrange("p (k n) -> p k n", k=src.shape[1])
                    sp.dma_start(dst, src).then_inc(raw_loaded[u % RAW], 16)

            def load(ph):
                if TRIPS[ph] <= 2:
                    for i in range(TRIPS[ph]):
                        load_trip(ph, i)
                else:
                    with sp.Fori(0, TRIPS[ph]) as i:
                        load_trip(ph, i)

            for tt in range(2):
                sp.dma_start(xrow[:, tt, :], A["x"][0, tt * P:(tt + 1) * P, :]).then_inc(x_in[tt], 16)
            load_parameters(sp, True)
            load_trip("qkva", 0, 0, RAW)
            load_parameters(sp, False)
            for c, name in enumerate(("lam_q1", "lam_k1", "lam_q2", "lam_k2")):
                sp.dma_start(lamv[:, c:c + 1], A[name].rearrange("a d -> d a")).then_inc(lam_in, 16)
            sink_all = bass.AP(tensor=A["sinks"].tensor, offset=0, ap=[[0, P], [1, SW_HEADS]])
            sp.dma_start(sinkb[:, :], sink_all).then_inc(lam_in, 16)
            sp.dma_start(tabx[0:N_BUCKETS, :], A["rel_bias_table"]).then_inc(hots_in, 16)
            sp.dma_start(hots[:, 0, :], A["c_hot_full"]).then_inc(hots_in, 16)
            sp.dma_start(hots[:, 1, :], A["c_hot_window"]).then_inc(hots_in, 16)
            sp.dma_start(mrow[:, :], A["meta_tokens_2"]).then_inc(meta_in, 16)
            load_trip("qkva", 0, RAW)
            sp.wait_ge(lines_stored, 48)
            sp.wait_ge(row_turned, 9)
            skewed = bass.AP(tensor=lines_dram.tensor, offset=P - 1, ap=[[LINE, P], [P * (LINE + 1), N_HEADS], [1, TB]])
            sp.dma_start(bias[:, :, :], skewed).then_inc(bias_in, 16)
            for ph in ("qb", "kvb", "qkvc", "gates", "oabc", "wout", "up", "down", "aqk", "av", "ag", "aout", "gqk", "lr", "gv",
                       "gg", "gout"):
                load(ph)
            sp.wait_ge(x_parked, 16)
            sp.wait_ge(e_dec, 2 * GL_HEADS)
            sp.wait_ge(d_sub, 3 * GL_HEADS)
            sp.wait_ge(e_k, 2 * GL_HEADS)
            sp.wait_ge(e_q, 2 * GL_HEADS)
            sp.dma_start(xback[:, :, :].rearrange("p t n -> p (t n)"), park_dram).then_inc(x_back, 16)
            for n, (tt, c) in enumerate(OUT_PIECES):
                sp.wait_ge(out_made, n + 1)
                sp.dma_start(out[tt * P:(tt + 1) * P, c:c + D // 2], orow[:, tt, c:c + D // 2])\
                  .then_inc(stored, 16)
            sp.wait_ge(stored, 16 * len(OUT_PIECES))

        @block.scalar
        def _(act):
            def split(u, i=0, n=0):
                if not under(u, i, n, N_UNITS) and isinstance(i, int):
                    return
                ring_waits(act, None, i, u, n, landed=True)
                act.activation(whi[:, u % RING, :], raw[:, u % RAW, :], ACT.Copy).then_inc(whi_ready, 1)

            def trip(ph, i, read_out, before=None, after=None, split_before=0):
                n = UNITS[ph]
                for j in range(n):
                    if before:
                        before(i, j)
                    if j >= split_before:
                        split(U0[ph] + j + LEAD, i, n)
                    chunk, _, ends = chunk_of(ph, j)
                    if ends and read_out:
                        read_out(i, chunk, U0[ph] + j, n)
                    if after:
                        after(i, j)

            def stream(ph, read_out, split_before=0):
                first = 1 if split_before else 0
                if split_before:
                    trip(ph, 0, read_out, split_before=split_before)
                if TRIPS[ph] <= 2:
                    for i in range(first, TRIPS[ph]):
                        trip(ph, i, read_out)
                else:
                    with act.Fori(first, TRIPS[ph]) as i:
                        trip(ph, i, read_out)

            def passed(u, tile, i, n):
                act.wait_ge(tile_pass, at(4 * u + tile, i, 4 * n))

            def tiles_to(dst_of, func=ACT.Copy, T=TB):
                def read_out(i, chunk, u, n):
                    for t in range(4):
                        passed(u, t + 1, i, n)
                        act.activation(dst_of(i, chunk, t), bank[:, t, 0:T], func).then_inc(acc_free, 1)
                return read_out

            act.dma_start(ident[:, :], A["c_ident"]).then_inc(ident_in, 16)
            def load_roots(n):
                if n:
                    act.wait_ge(table_in, n)
                act.activation(lam[:, 6:7], eps, ACT.Sqrt).then_inc(table_in, 1)

            act.wait_ge(start_set, 3)
            load_roots(0)
            for tt in range(2):
                act.wait_ge(x_in[tt], 16)
                act.activation(xn[:, tt, :], xrow[:, tt, :], ACT.Square, accum_out=xsum[:, tt:tt + 1]).then_inc(x_squared, 1)
                act.wait_ge(x_squared, tt + 1)
                act.activation(xrstd[:, tt:tt + 1], xsum[:, tt:tt + 1], ACT.Sqrt, bias=eps, scale=1.0 / D).then_inc(x_root, 1)

            def first_hi(g):
                act.wait_ge(par_ready, 1)
                act.wait_ge(xn_turned, g + 1)
                for k in (2 * g, 2 * g + 1):
                    act.activation(ha(ahi, k, 0, TB), turned(k), ACT.Identity, scale=par[:, G_PRE[0] + k:G_PRE[0] + k + 1])\
                       .then_inc(hhi_ready, 1)

            split(0)
            for g in range(4):
                if g + 1 < LEAD:
                    split(g + 1)
                first_hi(g)

            def start_step(i, j):
                if j < 4:
                    first_hi(4 + j)
                if j == 6:
                    act.wait_ge(lam_sum, 1)
                    act.activation(lam[:, 0:2], bank[:, 4, 0:2], ACT.Exp).then_inc(lam_exp, 1)
                    for w in range(2):
                        act.wait_ge(line_sum, w + 1)
                        act.activation(line[:, w, :], bank[0:N_HEADS, 5 + w, 0:LINE], ACT.Copy).then_inc(line_ready, 1)
                    act.wait_ge(line_ready, 2)
                    for w, h0, h1 in ((0, 0, DA_HEADS), (1, DA_HEADS, DA_HEADS + SW_HEADS), (0, DA_HEADS + SW_HEADS, N_HEADS)):
                        act.dma_start(lines_dram[h0:h1, :, 0:LINE], line[h0:h1, w:w + 1, :].to_broadcast([h1 - h0, P, LINE]))\
                           .then_inc(lines_stored, 16)
                if 8 <= j < 16:
                    g = j - 8
                    act.wait_ge(row_turned, g + 1)
                    act.activation(xT[:, 2 * g:2 * g + 2, 0:TB], bank[:, 4 + g % 4, :].rearrange("p (k t) -> p k t", k=2),
                                   ACT.Copy).then_inc(row_taken, 1)
                if j == 16:
                    act.wait_ge(row_turned, 9)
                    act.activation(xT[:, :, TB:T2], bank[:, 4, 0:KD * TM].rearrange("p (k t) -> p k t", k=KD), ACT.Copy)\
                       .then_inc(row_taken, 1)

            def root(use, T, sums, made, count):
                act.wait_ge(made, count)
                act.activation(msq[:, 0:T], sums, ACT.Sqrt, bias=eps, scale=1.0 / D).then_inc(root_ready, 1)

            def norm_after(b):
                root(POST(b), T_POST[b], bank[:, 5, 0:T_POST[b]], mean_ready, b)

            def norm_before(b):
                T = T_PRE[b]
                for g in UPDATE_ORDER:
                    updated(act, b, g)
                    act.activation(Y[b][:, 4 * g:4 * g + 4, 0:T], xT[:, 4 * g:4 * g + 4, 0:T], ACT.Square).then_inc(sq_ready, 1)
                split(U0[AFTER_NORM[b]] + LEAD)
                root(PRE(b), T, bank[:, 4, 0:T], sq_summed, b)
                for k in range(KD):
                    act.wait_ge(h_ready, KD * (b - 1) + k + 1)
                    act.activation(ha(ahi, k, 0, T), tmp[:, k % 4, 0:T], ACT.Copy).then_inc(hhi_ready, 1)


            def branch_step(m):
                if m < 24:
                    if 8 <= m < 16:
                        act.wait_ge(max_sink, m - 8 + 1)
                    else:
                        act.wait_ge(max_ready, 2 * m + 2)
                    if m >= 4:
                        act.wait_ge(p_turned, job_of(m - 4) + 1)
                    for q, (c0, c1) in enumerate(((0, P), (P, 384))):
                        act.activation(prob[:, m % 4, c0:c1], sbias[:, m % 2, c0:c1], ACT.Exp, bias=nmax[:, m, q:q + 1],
                                       accum_out=ssum[:, m, q:q + 1]).then_inc(p_ready, 1)
                    if 8 <= m < 16:
                        act.activation(esink[:, m - 8, :], nmax[:, m, :], ACT.Exp, bias=sinkb[:, m - 8:m - 7])\
                           .then_inc(sink_ready, 1)
                if m >= 2 and ends_job(m - 2):
                    job = job_of(m - 2)
                    act.wait_ge(p_turned, job + 1)
                    if job >= 2:
                        act.wait_ge(o_ready, job - 1)
                    act.activation(probT[:, job % 2, :], bank[:, 6, 0:384], ACT.Copy).then_inc(pT_ready, 1)
                if m >= 4 and (m - 4) % 2 and m - 4 < 24:
                    unit = (m - 4) // 2
                    act.wait_ge(o_ready, job_of(m - 4) + 1)
                    if unit < DA_HEADS:
                        act.activation(osb[:, unit, :], bank[:, 7, 0:TB], ACT.Copy).then_inc(o_free, 1)
                    else:
                        act.activation(yhi[:, unit, :], bank[:, 7, 0:TB], ACT.Copy).then_inc(yhi_ready, 1)

            def steps(ph):
                def after(i, j):
                    m = step_beside(ph, i, j)
                    if m is not None:
                        branch_step(m)
                    if ph == "gates" and i == 1:
                        branch_norm(j)
                return after

            def branch_norm(j):
                if j == 3:
                    act.wait_ge(o_free, DA_HEADS)
                    act.activation(osq[:, :, :], osb[:, :, :], ACT.Square).then_inc(a_squared, 1)
                    for c in range(2):
                        act.wait_ge(a_summed, c + 1)
                        act.activation(ors[:, 2 * c:2 * c + 2, :], bank[:, 4 + c, :].rearrange("p (h t) -> p h t", h=2), ACT.Sqrt,
                                       bias=eps, scale=1.0 / P).then_inc(a_root, 1)
                if j == 7:
                    act.wait_ge(a_normed, 1)
                    act.activation(yhi[:, 0:DA_HEADS, :], yn[:, :, :], ACT.Copy).then_inc(ya_hi, 1)

            def qkv_out(q, k, v):
                def read_out(i, chunk, u, n):
                    if chunk < 2:
                        for t in range(4):
                            passed(u, t + 1, i, n)
                            act.activation((q, k)[chunk][:, t, :], bank[:, t, 0:TB], ACT.Copy).then_inc(acc_free, 1)
                    else:
                        for tt in range(2):
                            passed(u, (1, 4)[tt], i, n)
                            act.activation(v[:, tt, :], bank[:, tt, :], ACT.Copy).then_inc(acc_free, (1, 3)[tt])
                return read_out

            trip("qkva", 0, qkv_out(qaT, kaT, vatok), after=start_step)
            act.wait_ge(lines_stored, 48)
            trip("qb", 0, tiles_to(lambda i, chunk, t: qbT[:, t, :]), after=steps("qb"))

            def kvb_out(i, chunk, u, n):
                passed(u, 1, i, n)
                act.activation(kbT[:, 0, :], bank[:, 0, 0:TB], ACT.Copy)
                act.activation(kbT[0:64, 1, :], bank[64:128, 0, 0:TB], ACT.Copy)
                act.activation(kbT[64:128, 1, :], bank[0:64, 0, 0:TB], ACT.Copy).then_inc(acc_free, 1)
                for tt in range(2):
                    passed(u, (2, 4)[tt], i, n)
                    ins = act.activation(vbtok[:, tt, :], bank[:, 1 + tt, 0:P], ACT.Copy)
                    ins.then_inc(acc_free, (1, 2)[tt])

            stream("kvb", kvb_out)

            trip("qkvc", 0, qkv_out(qcT, kcT, vctok), after=steps("qkvc"))

            def gates_out(i, chunk, u, n):
                for t in range(4):
                    passed(u, t + 1, i, n)
                    act.activation(gate[:, bass.ds(i * 4 + t, 1), :], bank[:, t:t + 1, 0:TB], ACT.Sigmoid,
                                   bias=par[:, bass.ds(i * 4 + (PAR["b_gate"] + t), 1)]).then_inc(acc_free, 1)

            for i in range(2):
                trip("gates", i, gates_out, after=steps("gates"))
            with act.Fori(2, 6) as i:
                trip("gates", i, gates_out)
            act.wait_ge(o_free, 12)
            act.wait_ge(y_done, 1)
            with act.Fori(6, TRIPS["gates"]) as i:
                trip("gates", i, gates_out)

            def mix_out(i, chunk, u, n):
                group, branch = divmod(6 * i + chunk, 3)
                if branch == 2:
                    for t in range(4):
                        act.wait_ge(mix_sum, 4 * group + t + 1)
                        act.activation(ahi_tile(group, t), mixtmp[:, 0, t:t + 1, :], ACT.Copy).then_inc(mix_part, 1)

            stream("oabc", mix_out)

            def y_out(b):
                T = T_POST[b]

                def read_out(i, chunk, u, n):
                    for t in range(4):
                        passed(u, t + 1, i, n)
                        act.wait_ge(y_summed, at((KD + 4) * (b - 1) + t + 1, i, 4))
                        act.activation(tmp[:, t, 0:T], bank[:, t, 0:T], ACT.Square).then_inc(y_squared, 1)
                        act.activation(Y[b][:, bass.ds(i * 4 + t, 1), 0:T], bank[:, t:t + 1, 0:T], ACT.Identity,
                                       scale=par[:, bass.ds(i * 4 + (G_POST[b] + t), 1)]).then_inc(acc_free, 1)
                return read_out

            load_roots(1)
            stream("wout", y_out(1))
            norm_after(1)
            norm_before(1)

            def up_out(i, chunk, u, n):
                for t in range(4):
                    r = (t % 2) + (t // 2) * FT + 2 * chunk
                    passed(u, 2 * t - 2, i, n)
                    act.activation(cv[:, t, :], bank[:, 4 * chunk + t, 0:TB], ACT.Identity,
                                   bias=par[:, bass.ds(i * 4 + (PAR["conv_b"] + r), 1)],
                                   scale=par[:, bass.ds(i * 4 + (PAR["conv_w"] + 2 * 2 * FT + r), 1)]).then_inc(tap2, 1)
                for t in range(2):
                    act.wait_ge(acc_free, at(4 * (C0["up"] + chunk) + t + 1, i, 8))
                    act.activation(cv[:, t, :], cv[:, t, :], ACT.Gelu_apprx_tanh).then_inc(gelu_done, 1)

            stream("up", up_out, split_before=1)
            load_roots(2)
            stream("down", y_out(2))
            act.wait_ge(tile_pass, 4 * U0["aqk"])
            for t, name in ((cos, "c_cos"), (sin, "c_sin"), (turn, "c_turn")):
                act.dma_start(t[:, :], A[name]).then_inc(rope_in, 16)
            norm_after(2)
            norm_before(2)

            def feature_out(dst, T, func):
                def read_out(i, chunk, u, n):
                    for t in range(4):
                        passed(u, t + 1, i, n)
                        act.activation(dst[:, bass.ds(i * 4 + t, 1), 0:T], bank[:, t:t + 1, 0:T], func).then_inc(acc_free, 1)
                return read_out

            def qk_norm(i, j):
                p, late = divmod(j, 2)
                if not late:
                    act.wait_ge(acc_free, at(4 * C0["aqk"] + p - 3, i, 4))
                    if not under(p - 4, i, 4, 2):
                        act.wait_ge(qk_sum, at(p - 5, i, 4))
                    act.activation(sq2[:, p % 2:p % 2 + 1, :], qk2[:, bass.ds(i * 4 + (p - 4), 1), :], ACT.Square)\
                       .then_inc(qk_sq, 1)

            def qk_late(i, j):
                p, late = divmod(j, 2)
                if not late:
                    act.wait_ge(qk_sum, at(p - 3, i, 4))
                    act.activation(rs2[:, p % 2, :], bank[:, 4 + p % 2, 0:T2], ACT.Sqrt, bias=eps, scale=1.0 / AT_HD)\
                       .then_inc(qk_root, 1)

            qk_out = feature_out(qk2, T2, ACT.Copy)
            trip("aqk", 0, qk_out, split_before=1)
            trip("aqk", 1, qk_out, qk_norm, qk_late)
            with act.Fori(2, TRIPS["aqk"]) as i:
                trip("aqk", i, qk_out, qk_norm, qk_late)

            def values(s):
                for n, step in enumerate(VALUE_STEPS):
                    if s == step:
                        i, tt = divmod(n, 3)
                        rows = (P, P, TM)[tt]
                        act.wait_ge(v2_turned, n + 1)
                        act.activation(v2[0:rows, tt, i * 512:(i + 1) * 512], bank[0:rows, 7, :], ACT.Copy).then_inc(v2_taken, 1)

            def attend(s):
                h, second = divmod(s, 2)
                for q in ((0, 1), (2,))[second] if h < AT_HEADS else ():
                    rows = (P, P, TM)[q]
                    act.wait_ge(max2_ready, 3 * h + q + 1)
                    if h >= 2:
                        act.wait_ge(p2_turned, 2 * (h - 1))
                    act.activation(p2[0:rows, h % 2, q, :], bank[0:rows, (4, 5, 4)[q], 0:T2], ACT.Exp,
                                   bias=nm2[0:rows, h, q:q + 1], accum_out=sum2[0:rows, h, q:q + 1]).then_inc(p2_ready, 1)
                if second and 1 <= h <= AT_HEADS:
                    hh = h - 1
                    act.wait_ge(p2_turned, 2 * hh + 2)
                    if hh >= 2:
                        act.wait_ge(o2_ready, hh - 1)
                    act.activation(pT2[:, hh % 2, 0:2, TB:T2], bank[:, 5, 0:2 * TM].rearrange("p (k t) -> p k t", k=2),
                                   ACT.Copy).then_inc(pT2_act, 1)
                    act.activation(pT2[0:TM, hh % 2, 2, :], bank[0:TM, 5, 2 * TM:2 * TM + T2], ACT.Copy).then_inc(pT2_act, 1)
                values(s)
                if s >= 18 and s % 2 == 0 and (s - 18) // 2 < FIRST_GATED:
                    gated_hi((s - 18) // 2)

            def gated_hi(h):
                act.wait_ge(z2_ready, h + 1)
                act.activation(z2_part(0, h), qk2[:, h, :], ACT.Copy).then_inc(z2hi, 1)

            trip("av", 0, tiles_to(lambda i, chunk, t: vt2[:, i, t, :], T=T2), lambda i, j: qk_norm(TRIPS["aqk"], j), lambda i, j: qk_late(TRIPS["aqk"], j))
            trip("av", 1, tiles_to(lambda i, chunk, t: vt2[:, i, t, :], T=T2), after=lambda i, j: attend(j - 1) if j else None)
            for i in range(TRIPS["ag"]):
                trip("ag", i, feature_out(gs2, T2, ACT.Silu), after=lambda i, j: attend(8 * (i + 1) + j - 1))
            act.wait_ge(tile_pass, 4 * U0["aout"])
            for h in range(FIRST_GATED, AT_HEADS):
                gated_hi(h)
            load_roots(3)
            stream("aout", y_out(3))
            norm_after(3)
            norm_before(3)

            def x_row(n):
                tt, g = X_PIECES[n]
                act.wait_ge(xw_turned, n + 1)
                act.activation(xwait[:, tt, 512 * g:512 * g + 512], bank[:, X_BANK[n % 4], :], ACT.Copy).then_inc(xw_taken, 1)

            for n in range(2):
                x_row(n)
            gain_all = bass.AP(tensor=A["post_norm_2"].tensor, offset=D, ap=[[0, P], [1, D]])
            act.dma_start(gainrow[:, :], gain_all).then_inc(gain_in, 16)
            for t, name in ((maskf, "c_mask_f"), (maskb, "c_mask_b"), (reset, "c_reset")):
                act.dma_start(t[:, :], A[name]).then_inc(gla_const, 16)
            act.dma_start(up_w[:, :, :], A["gla_gk_up_2"][0].rearrange("d r n -> r d n")).then_inc(gla_const, 16)

            gqk_out = feature_out(gqk, T2, ACT.Copy)
            trip("gqk", 0, gqk_out, after=lambda i, j: x_row(j + 2) if j + 2 < len(X_PIECES) else None, split_before=1)
            act.wait_ge(xw_taken, len(X_PIECES))
            act.dma_start(park_dram, xwait[:, :, :].rearrange("p t n -> p (t n)")).then_inc(x_parked, 16)
            with act.Fori(1, TRIPS["gqk"]) as i:
                trip("gqk", i, gqk_out)

            def lr_out(i, chunk, u, n):
                for d in range(2):
                    passed(u, (1, 4)[d], i, n)
                    act.activation(lrT[:, d, :], bank[0:GL_RANK, d, 0:T2], ACT.Copy).then_inc(acc_free, (1, 3)[d])

            stream("lr", lr_out)

            def log_decay(g, j):
                a = zabs[:, g % 2, :, :]
                if j == 0:
                    for t in range(4):
                        n = 4 * g + t
                        act.wait_ge(z_sum, n + 1)
                        if g >= 2:
                            act.wait_ge(z_sub, g - 1)
                        act.activation(zabs[:, g % 2, t, :], bank[:, 4 + t, 0:T2], ACT.Abs,
                                       bias=par[:, PAR["gla_gk_bias_2"] + n:PAR["gla_gk_bias_2"] + n + 1]).then_inc(z_abs, 1)
                if j == 2:
                    act.wait_ge(z_abs, 4 * g + 4)
                    act.activation(a, a, ACT.Exp, scale=-1.0).then_inc(z_exp, 1)
                    act.wait_ge(z_exp, g + 1)
                    act.activation(a, a, ACT.Ln, bias=1.0).then_inc(z_ln, 1)

            def values(g, tt):
                rows = (P, P, TM)[tt]
                act.wait_ge(v3_turned, 3 * g + tt + 1)
                act.wait_ge(x_parked, 16)
                act.activation(v3[0:rows, tt, g * 512:(g + 1) * 512], bank[0:rows, VALUE_BANK[tt], :], ACT.Copy)\
                   .then_inc(v3_taken, 1)

            def beside_values(g, j):
                log_decay(g, j)
                if g and 2 <= j < 5:
                    values(g - 1, j - 2)

            for g in range(TRIPS["gv"]):
                trip("gv", g, tiles_to(lambda i, chunk, t: vt3[:, i % 2, t, :], T=T2), after=beside_values)

            SC = 1.0 / GL_NORMALIZER

            def decays(h):
                return cum[:, 2 * h:2 * h + 2, :], cum[:, 8 + 2 * h:10 + 2 * h, 0:TB]

            def head_step(h, lag):
                lf, lb = decays(h)
                if lag == -3:
                    for d, t in enumerate((kendf, kendb)):
                        act.wait_ge(d_sub, 3 * h + 2 + d)
                        act.activation(t[:, :, :], t[:, :, :], ACT.Exp, scale=SC).then_inc(e_d, 1)
                    if h:
                        act.wait_ge(sc_sum, 2 * h)
                    for d, l in enumerate((lf, lb)):
                        act.activation(kinv[:, d, :, :], l[:, :, 0:TB], ACT.Exp, scale=-SC).then_inc(e_k, 1)
                if lag == -2:
                    if h:
                        act.wait_ge(x_sum, h)
                    for d, l in enumerate((lf, lb)):
                        act.activation(qdec[:, d, :, :], l[:, :, 0:TB], ACT.Exp, scale=SC).then_inc(e_q, 1)
                    act.activation(dec[:, 0, :, :], lf[:, :, GL_CHUNK - 1:TB:GL_CHUNK], ACT.Exp, scale=SC).then_inc(e_dec, 1)
                    act.activation(dec[:, 1, :, :], lb[:, :, 0:TB:GL_CHUNK], ACT.Exp, scale=SC).then_inc(e_dec, 1)
                if lag == 1:
                    act.wait_ge(xm_sum, h + 1)
                    act.activation(scm[:, :], bank[0:TM, 6, 0:TB], ACT.Copy).then_inc(scm_ready, 1)
                if lag == 3:
                    act.wait_ge(o3_ready, h + 1)
                    if h:
                        act.wait_ge(z3_ready, h)
                    for c in range(2):
                        act.activation(osq3[:, 2 * c:2 * c + 2, :], bank[:, 6 + c, :].rearrange("p (v t) -> p v t", v=2),
                                       ACT.Square).then_inc(o3_sq, 1)
                if lag == 4:
                    act.wait_ge(o3_sum, h + 1)
                    act.activation(msq[:, 0:TB], bank[:, 4, 0:TB], ACT.Sqrt, bias=eps, scale=1.0 / GL_V).then_inc(o3_root, 1)

            def gla(i, j):
                if (i, j) == (0, 0):
                    for tt in range(3):
                        values(TRIPS["gv"] - 1, tt)
                for h in reversed(range(GL_HEADS)):
                    head_step(h, 8 * i + j - HEAD_AT[h])
                if 8 * i + j == GATED_AT[0] + 1:
                    act.wait_ge(z3_ready, 1)
                    act.activation(z0hi[:, :, :], gg[:, 0:4, :], ACT.Copy).then_inc(z3hi, 1)

            for i in range(TRIPS["gg"]):
                trip("gg", i, feature_out(gg, TB, ACT.Silu), after=gla)
            act.wait_ge(tile_pass, 4 * U0["gout"])
            for h in range(1, GL_HEADS):
                act.wait_ge(z3_ready, h + 1)
                zhi = ahi[:, 0:KD * T2].rearrange("p (k t) -> p k t", t=T2)[:, 4 * h:4 * h + 4, 0:TB]
                act.activation(zhi, gg[:, 4 * h:4 * h + 4, :], ACT.Copy).then_inc(z3hi, 1)
            load_roots(4)

            def rows_out(i, chunk, u, n):
                for tt in range(2):
                    passed(u, 2 * tt + 2, i, n)
                    c = 2 * i + chunk
                    act.activation(orow[:, tt, 512 * c:512 * c + 512], bank[:, 2 * chunk + tt, :], ACT.Square,
                                   accum_out=ysum[:, tt, c:c + 1]).then_inc(yr_squared, 1)

            stream("gout", rows_out)
            for tt in range(2):
                act.wait_ge(yr_sum, tt + 1)
                act.activation(yroot[:, tt:tt + 1], yroot[:, tt:tt + 1], ACT.Sqrt, bias=eps, scale=1.0 / D).then_inc(yr_root, 1)

        @block.vector
        def _(dve):
            def split(u, i=0, n=0):
                if not under(u, i, n, N_UNITS) and isinstance(i, int):
                    return
                dve.wait_ge(whi_ready, at(u + 1, i, n))
                dve.tensor_tensor(wlo[:, u % RING, :], raw[:, u % RAW, :], whi[:, u % RING, :].bitcast(F32),
                                  ALU.subtract).then_inc(wlo_ready, 1)

            def trip(ph, i, read_out=None, before=None, after=None, split_before=0):
                n = UNITS[ph]
                for j in range(n):
                    if before:
                        before(i, j)
                    if j >= split_before:
                        split(U0[ph] + j + LEAD, i, n)
                    chunk, _, ends = chunk_of(ph, j)
                    if ends and read_out:
                        read_out(i, chunk, U0[ph] + j, n)
                    if after:
                        after(i, j)

            def stream(ph, read_out=None, split_before=0):
                first = 1 if split_before else 0
                if split_before:
                    trip(ph, 0, read_out, split_before=split_before)
                if TRIPS[ph] <= 2:
                    for i in range(first, TRIPS[ph]):
                        trip(ph, i, read_out)
                else:
                    with dve.Fori(first, TRIPS[ph]) as i:
                        trip(ph, i, read_out)

            def column(name, k=0):
                return par[:, PAR[name] + k:PAR[name] + k + 1]

            dve.memset(ones[:, :], 1.0).then_inc(start_set, 1)
            dve.memset(eps, EPS).then_inc(start_set, 1)
            dve.memset(tabx[N_BUCKETS:N_BUCKETS + 1, :], MASKED).then_inc(start_set, 1)

            def parameters(g):
                m = min(P, N_PAR - g * P)
                dve.wait_ge(par_turned, g + 1)
                dve.tensor_copy(par[:, g * P:g * P + m], bank[:, PAR_BANK[g], 0:m]).then_inc(par_ready, 1)

            def first_lo(g):
                dve.wait_ge(hhi_ready, 2 * g + 2)
                for k in (2 * g, 2 * g + 1):
                    dve.scalar_tensor_tensor(ha(alo, k, 0, TB), turned(k), column("pre_mix_g", k), ha(ahi, k, 0, TB).bitcast(F32),
                                             ALU.mult, ALU.subtract).then_inc(act_ready, 1)

            for tt in range(2):
                dve.wait_ge(x_root, tt + 1)
                dve.reciprocal(xrstd[:, tt:tt + 1], xrstd[:, tt:tt + 1]).then_inc(x_rstd, 1)
                dve.wait_ge(x_rstd, tt + 1)
                for c0, c1 in (((0, D),), ((0, D // 2), (D // 2, D)))[tt]:
                    dve.tensor_scalar(xn[:, tt, c0:c1], xrow[:, tt, c0:c1], xrstd[:, tt:tt + 1], None, ALU.mult)\
                       .then_inc(xn_ready, 1)
                if tt == 0:
                    parameters(0)
            for g in range(4):
                if g < LEAD:
                    split(g)
                first_lo(g)

            def start_step(i, j):
                if j < 4:
                    first_lo(4 + j)
                if j in (4, 5):
                    for g in (2 * j - 7, 2 * j - 6):
                        parameters(g)
                if j == 5:
                    dve.wait_ge(lam_in, 16 * 5)
                    dve.tensor_tensor(lamv[:, 4:5], lamv[:, 0:1], lamv[:, 1:2], ALU.mult).then_inc(lam_prod, 1)
                    dve.tensor_tensor(lamv[:, 5:6], lamv[:, 2:3], lamv[:, 3:4], ALU.mult).then_inc(lam_prod, 1)
                    dve.tensor_scalar(sinkn[:, :], sinkb[:, :], -1.0, None, ALU.mult).then_inc(lam_ready, 1)
                if j == 8:
                    dve.wait_ge(lam_exp, 1)
                    dve.tensor_tensor(lam[:, 2:3], lam[:, 1:2], lam[:, 0:1], ALU.subtract).then_inc(lam_ready, 1)
                    dve.wait_ge(par_ready, PAR_GROUPS)
                    dve.tensor_scalar(subg, column("subln"), 1.0 - LAM_INIT, None, ALU.mult).then_inc(lam_ready, 1)
                    dve.tensor_scalar(qkgain[:, 0:AT_HEADS], column("attn_q_norm_2").to_broadcast([P, AT_HEADS]),
                                      AT_HD ** -0.5, None, ALU.mult).then_inc(lam_ready, 1)
                    dve.tensor_scalar(qkgain[:, AT_HEADS:], column("attn_k_norm_2").to_broadcast([P, AT_KV]), 1.0, None,
                                      ALU.mult).then_inc(lam_ready, 1)
                    dve.wait_ge(lam_ready, 2)
                    dve.tensor_scalar(lam[:, 3:4], lam[:, 2:3], -LAM_INIT, None, ALU.add).then_inc(lam_ready, 1)

            def inverse(use, T):
                dve.wait_ge(root_ready, use + 1)
                dve.reciprocal(rstd[:, 0:T], msq[:, 0:T]).then_inc(rstd_ready, 1)
                dve.wait_ge(rstd_ready, use + 1)

            def norm_before(b):
                T = T_PRE[b]
                for n in (2, 3):
                    k = 4 * UPDATE_ORDER[n]
                    dve.wait_ge(sq_ready, 4 * (b - 1) + n + 1)
                    dve.tensor_tensor(Y[b][:, k:k + 2, 0:T], Y[b][:, k:k + 2, 0:T], Y[b][:, k + 2:k + 4, 0:T], ALU.add)\
                       .then_inc(sq_folded, 1)
                split(U0[AFTER_NORM[b]] + LEAD)
                inverse(PRE(b), T)
                for k in range(KD):
                    if k >= 4:
                        dve.wait_ge(act_ready, LO[f"norm{b}"] + k - 3)
                    dve.scalar_tensor_tensor(tmp[:, k % 4, 0:T], xT[:, k, 0:T], par[:, G_PRE[b] + k:G_PRE[b] + k + 1],
                                             rstd[:, 0:T], ALU.mult, ALU.mult).then_inc(h_ready, 1)

            def norm_after(b):
                T = T_POST[b]
                inverse(POST(b), T)
                for g in range(3):
                    x, y = (t[:, 4 * g:4 * g + 4, 0:T] for t in (xT, Y[b]))
                    dve.tensor_tensor(y, y, over_tiles(rstd[:, 0:T]), ALU.mult).then_inc(y_scaled, 1)
                    dve.wait_ge(y_scaled, 3 * (b - 1) + g + 1)
                    dve.tensor_tensor(x, x, y, ALU.add).then_inc(x_updated, 1)


            def branch_step(m):
                if m == 0:
                    dve.wait_ge(bias_in, 16)
                if m < 24:
                    head = m // 2 if m < 8 else m - 8 + DA_HEADS
                    dve.wait_ge(s_ready, m + 1)
                    if m >= 2:
                        dve.wait_ge(p_ready, 2 * m - 2)
                    dve.scalar_tensor_tensor(sbias[:, m % 2, 0:P], bank[:, 4 + m % 2, 0:P], HD ** -0.5,
                                             bias[:, head, P:TB], ALU.mult, ALU.add).then_inc(s_biased, 1)
                    dve.scalar_tensor_tensor(sbias[:, m % 2, P:384], bank[:, 4 + m % 2, P:384], HD ** -0.5,
                                             bias[:, head, :], ALU.mult, ALU.add).then_inc(s_biased, 1)
                    for q, (c0, c1) in enumerate(((0, P), (P, 384))):
                        dve.wait_ge(s_biased, 2 * m + q + 1)
                        dve.tensor_reduce(nmax[:, m, q:q + 1], sbias[:, m % 2, c0:c1], AX.X, ALU.max, negate=True)\
                           .then_inc(max_ready, 1)
                    if 8 <= m < 16:
                        dve.wait_ge(max_ready, 2 * m + 2)
                        dve.tensor_scalar(nmax[:, m, :], nmax[:, m, :], sinkn[:, m - 8:m - 7], None, ALU.min)\
                           .then_inc(max_sink, 1)
                if 1 <= m <= 24:
                    mm = m - 1
                    dve.wait_ge(p_ready, 2 * mm + 2)
                    if 8 <= mm < 16:
                        dve.wait_ge(sink_ready, mm - 8 + 1)
                        dve.tensor_tensor(ssum[:, mm, :], ssum[:, mm, :], esink[:, mm - 8, :], ALU.add).then_inc(sum_sink, 1)
                        dve.wait_ge(sum_sink, mm - 8 + 1)
                    dve.reciprocal(ssum[:, mm, :], ssum[:, mm, :]).then_inc(inv_sum, 1)
                    dve.wait_ge(inv_sum, mm + 1)
                    cols = ((0, P), (P, 384))
                    if mm >= 8:
                        for q, (c0, c1) in enumerate(cols):
                            dve.tensor_scalar(prob[:, mm % 4, c0:c1], prob[:, mm % 4, c0:c1], ssum[:, mm, q:q + 1], None,
                                              ALU.mult).then_inc(p_scaled, 1)
                    elif mm % 2:
                        dve.tensor_scalar(ssum[:, mm, :], ssum[:, mm, :], lam[:, 3:4], None, ALU.mult).then_inc(p_second, 1)
                        dve.wait_ge(p_second, 3 * (mm // 2) + 1)
                        for q, (c0, c1) in enumerate(cols):
                            dve.tensor_scalar(prob[:, mm % 4, c0:c1], prob[:, mm % 4, c0:c1], ssum[:, mm, q:q + 1], None,
                                              ALU.mult).then_inc(p_second, 1)
                        for q, (c0, c1) in enumerate(cols):
                            dve.wait_ge(p_second, 3 * (mm // 2) + 2 + q)
                            dve.scalar_tensor_tensor(prob[:, (mm - 1) % 4, c0:c1], prob[:, (mm - 1) % 4, c0:c1],
                                                     ssum[:, mm - 1, q:q + 1], prob[:, mm % 4, c0:c1], ALU.mult, ALU.add)\
                               .then_inc(p_scaled, 1)
                if m >= 4 and (m - 4) % 2 and (m - 4) // 2 >= DA_HEADS:
                    unit = (m - 4) // 2
                    dve.wait_ge(yhi_ready, unit - DA_HEADS + 1)
                    dve.tensor_tensor(ylo[:, unit, :], bank[:, 7, 0:TB], yhi[:, unit, :].bitcast(F32), ALU.subtract)\
                       .then_inc(o_free, 1)

            def branch_norm(j):
                if 3 <= j < 7:
                    dve.wait_ge(a_root, (j - 3) // 2 + 1)
                    dve.reciprocal(ors[:, j - 3, :], ors[:, j - 3, :]).then_inc(a_rstd, 1)
                if j == 7:
                    dve.wait_ge(a_rstd, 4)
                    dve.scalar_tensor_tensor(yn[:, :, :], osb[:, :, :], subg[:, 0:1], ors[:, :, :], ALU.mult, ALU.mult)\
                       .then_inc(a_normed, 1)

            def steps(ph):
                def after(i, j):
                    m = step_beside(ph, i, j)
                    if m is not None:
                        branch_step(m)
                    if ph == "gates" and i == 1:
                        branch_norm(j)
                return after

            trip("qkva", 0, after=start_step)
            trip("qb", 0, after=steps("qb"))
            stream("kvb")
            trip("qkvc", 0, after=steps("qkvc"))
            for i in range(2):
                trip("gates", i, after=steps("gates"))
            with dve.Fori(2, TRIPS["gates"]) as i:
                trip("gates", i)

            def mix_out(i, chunk, u, n):
                group, branch = divmod(6 * i + chunk, 3)
                for t in range(4):
                    dve.wait_ge(tile_pass, at(4 * u + t + 1, i, 4 * n))
                    if branch == 0:
                        dve.wait_ge(act_ready, LO["mix"] + 4 * group)
                    if branch == 2:
                        dve.wait_ge(mix_two, 4 * group + t + 1)
                    k, b = KD * branch + 4 * group + t, 4 * (chunk % 2) + t
                    dve.tensor_tensor(mixtmp[:, min(branch, 1), t, :], bank[:, b, 0:TB], gate[:, k, :], ALU.mult).then_inc(acc_free, 1)

            stream("oabc", mix_out)
            stream("wout")
            norm_after(1)
            norm_before(1)

            def up_out(i, chunk, u, n):
                for t in range(4):
                    r = (t % 2) + (t // 2) * FT + 2 * chunk
                    for back in (1, 2):
                        dve.wait_ge((tap2, tap1)[back - 1], at(4 * chunk + t + 1, i, 8))
                        tap = par[:, bass.ds(i * 4 + (PAR["conv_w"] + (2 - back) * 2 * FT + r), 1)]
                        dve.scalar_tensor_tensor(cv[:, t, back:TB], bank[:, 4 * chunk + t, 0:TB - back], tap,
                                                 cv[:, t, back:TB], ALU.mult, ALU.add).then_inc((tap1, acc_free)[back - 1], 1)
                for t in range(2):
                    dve.wait_ge(gelu_done, at(2 * chunk + t + 1, i, 4))
                    dve.wait_ge(acc_free, at(4 * (C0["up"] + chunk) + t + 3, i, 8))
                    dve.wait_ge(act_ready, at(LO["ff"] + 2 * chunk, i, 4))
                    dve.tensor_tensor(pr[:, t, :], cv[:, t, :], cv[:, 2 + t, :], ALU.mult).then_inc(ff_prod, 1)

            stream("up", up_out, split_before=1)
            stream("down")
            norm_after(2)
            norm_before(2)

            def qk_norm(i, j):
                p, odd = divmod(j, 2)
                if odd:
                    return
                if not under(p - 5, i, 4, 0):
                    qk_rotate(p - 1, i)
                dve.wait_ge(qk_root, at(p - 3, i, 4))
                dve.reciprocal(rs2[:, p % 2, :], rs2[:, p % 2, :]).then_inc(qk_rstd, 1)
                dve.wait_ge(qk_rstd, at(p - 3, i, 4))
                if not under(p - 4, i, 4, 2):
                    dve.wait_ge(qk_turned, at(p - 5, i, 4))
                    dve.wait_ge(qk_cos, at(p - 5, i, 4))
                dve.scalar_tensor_tensor(n2[:, p % 2:p % 2 + 1, :], qk2[:, bass.ds(i * 4 + (p - 4), 1), :],
                                         qkgain[:, bass.ds(i * 4 + (p - 4), 1)], rs2[:, p % 2:p % 2 + 1, :],
                                         ALU.mult, ALU.mult).then_inc(qk_normed, 1)

            def qk_rotate(p, i):
                head = qk2[:, bass.ds(i * 4 + (p - 4), 1), :]
                b = 6 + p % 2
                dve.wait_ge(qk_turned, at(p - 3, i, 4))
                dve.tensor_tensor(head, bank[:, b:b + 1, 0:T2], sin[:, :].rearrange("p (o t) -> p o t", o=1),
                                  ALU.mult).then_inc(qk_sin, 1)
                dve.wait_ge(qk_sin, at(p - 3, i, 4))
                dve.wait_ge(qk_cos, at(p - 3, i, 4))
                dve.tensor_tensor(head, head, nc2[:, p % 2:p % 2 + 1, :], ALU.add).then_inc(qk_done, 1)

            def gated(h):
                dve.wait_ge(acc_free, 4 * C0["ag"] + h + 1)
                dve.wait_ge(o2_taken, h + 1)
                dve.tensor_tensor(qk2[:, h, :], qk2[:, h, :], gs2[:, h, :], ALU.mult).then_inc(z2_ready, 1)

            def attend(s):
                h, second = divmod(s, 2)
                for q in ((0, 1), (2,))[second] if h < AT_HEADS else ():
                    rows = (P, P, TM)[q]
                    dve.wait_ge(s2_ready, 3 * h + q + 1)
                    dve.tensor_reduce(nm2[0:rows, h, q:q + 1], bank[0:rows, (4, 5, 4)[q], 0:T2], AX.X, ALU.max, negate=True)\
                       .then_inc(max2_ready, 1)
                if not second and 2 <= h < AT_HEADS + 2:
                    hh = h - 2
                    dve.wait_ge(o2_ready, hh + 1)
                    dve.tensor_copy(qk2[:, hh, :], bank[:, 7, 0:T2]).then_inc(o2_taken, 1)
                if second and 1 <= h <= AT_HEADS:
                    hh = h - 1
                    dve.wait_ge(p2_turned, 2 * hh + 1)
                    if hh >= 2:
                        dve.wait_ge(o2_ready, hh - 1)
                    dve.tensor_copy(pT2[:, hh % 2, 0:2, 0:TB], bank[:, 6, :].rearrange("p (k t) -> p k t", k=2)).then_inc(pT2_dve, 1)
                if second and h < AT_HEADS:
                    dve.wait_ge(p2_ready, 3 * h + 3)
                    dve.reciprocal(sum2[:, h, 0:2], sum2[:, h, 0:2]).then_inc(inv2, 1)
                    dve.reciprocal(sum2[0:TM, h, 2:3], sum2[0:TM, h, 2:3]).then_inc(inv2, 1)
                    dve.wait_ge(inv2, 2 * h + 2)
                    for q in range(3):
                        rows = (P, P, TM)[q]
                        dve.tensor_scalar(p2[0:rows, h % 2, q, :], p2[0:rows, h % 2, q, :], sum2[0:rows, h, q:q + 1], None,
                                          ALU.mult).then_inc(p2_scaled, 1)
                if second and s >= 17:
                    gated((s - 17) // 2)

            trip("aqk", 0, split_before=1)
            trip("aqk", 1, after=qk_norm)
            with dve.Fori(2, TRIPS["aqk"]) as i:
                trip("aqk", i, after=qk_norm)
            trip("av", 0, after=lambda i, j: qk_norm(TRIPS["aqk"], j))
            trip("av", 1, after=lambda i, j: attend(j - 1) if j else qk_rotate(3, TRIPS["aqk"]))
            for i in range(TRIPS["ag"]):
                trip("ag", i, after=lambda i, j: attend(8 * (i + 1) + j - 1))
            for h in range(11, AT_HEADS):
                gated(h)
            stream("aout")
            norm_after(3)
            norm_before(3)
            stream("gqk", split_before=1)
            stream("lr")

            def log_decay(g, j):
                if g == 0 and j == 0:
                    dve.wait_ge(x_parked, 16)
                    dve.wait_ge(gla_const, 64)
                if j == 0:
                    for t in range(4):
                        n = 4 * g + t
                        dve.wait_ge(z_abs, n + 1)
                        dve.tensor_scalar(cum[:, n, :], bank[:, 4 + t, 0:T2], column("gla_gk_bias_2", n), 0.0, ALU.add,
                                          ALU.min).then_inc(z_min, 1)
                if j == 3:
                    dve.wait_ge(z_ln, g + 1)
                    dve.wait_ge(z_min, 4 * g + 4)
                    dve.tensor_tensor(cum[:, 4 * g:4 * g + 4, :], cum[:, 4 * g:4 * g + 4, :], zabs[:, g % 2, :, :], ALU.subtract)\
                       .then_inc(z_sub, 1)
                if j >= 4:
                    n = 4 * g + j - 4
                    dve.wait_ge(z_sub, g + 1)
                    if n < KT:
                        dve.tensor_tensor_scan(cum[:, n, :], reset[:, :], cum[:, n, :], 0.0, ALU.mult, ALU.add)\
                           .then_inc(cum_ready, 1)
                    else:
                        back = cum[:, n, 0:TB][:, ::-1]
                        dve.tensor_tensor_scan(back, reset[:, 0:TB], back, 0.0, ALU.mult, ALU.add).then_inc(cum_ready, 1)

            for g in range(TRIPS["gv"]):
                trip("gv", g, after=log_decay)

            def spread(ap, n):
                return bass.AP(tensor=ap.tensor, offset=ap.offset, ap=[list(d) for d in ap.ap] + [[0, n]])

            def to_ends(h):
                lf, lb = cum[:, 2 * h:2 * h + 2, :], cum[:, 8 + 2 * h:10 + 2 * h, 0:TB]
                chunks = "p k (c t) -> p k c t"
                dve.wait_ge(cum_ready, 16)
                if h:
                    dve.wait_ge(x_sum, h)
                dve.tensor_tensor(kendf[:, :, 0:TB].rearrange(chunks, t=GL_CHUNK),
                                  spread(lf[:, :, GL_CHUNK - 1:TB:GL_CHUNK], GL_CHUNK),
                                  lf[:, :, 0:TB].rearrange(chunks, t=GL_CHUNK), ALU.subtract).then_inc(d_sub, 1)
                dve.tensor_tensor(kendf[:, :, TB:T2], lf[:, :, T2 - 1:T2].to_broadcast([P, 2, TM]), lf[:, :, TB:T2],
                                  ALU.subtract).then_inc(d_sub, 1)
                dve.tensor_tensor(kendb[:, :, :].rearrange(chunks, t=GL_CHUNK), spread(lb[:, :, 0:TB:GL_CHUNK], GL_CHUNK),
                                  lb.rearrange(chunks, t=GL_CHUNK), ALU.subtract).then_inc(d_sub, 1)

            def far_keys(h):
                n = 8 * h

                def times(dst, src, d, u, width):
                    dve.tensor_tensor(dst, src, dec[:, d, :, u:u + 1].to_broadcast([P, 2, width]), ALU.mult).then_inc(k_far, 1)

                dve.wait_ge(e_dec, 2 * h + 2)
                dve.wait_ge(k_end, 2 * h + 2)
                times(kfar[:, :, 0:16], kendf[:, :, TB:T2], 0, 0, TM)
                times(kfar[:, :, 32:96], kendf[:, :, 0:64], 0, 1, GL_CHUNK)
                times(kfar[:, :, 176:240], kendf[:, :, 64:128], 0, 2, GL_CHUNK)
                times(kback[:, :, 0:64], kendb[:, :, 192:256], 1, 2, GL_CHUNK)
                times(kback[:, :, 64:128], kendb[:, :, 128:192], 1, 1, GL_CHUNK)
                dve.wait_ge(k_far, n + 1)
                times(kfar[:, :, 16:32], kfar[:, :, 0:16], 0, 1, TM)
                dve.wait_ge(k_far, n + 4)
                times(kback[:, :, 128:192], kback[:, :, 0:64], 1, 1, GL_CHUNK)
                dve.wait_ge(k_far, n + 6)
                times(kfar[:, :, 96:176], kfar[:, :, 16:96], 0, 2, TM + GL_CHUNK)

            def blocks(ap, p0, p1, c0, step, width):
                rows = ap[p0:p1, :]
                return bass.AP(tensor=rows.tensor, offset=rows.offset + c0, ap=[list(rows.ap[0]), [step, 2], [1, width]])

            def head_step(h, lag):
                if lag == -4:
                    to_ends(h)
                if lag == -1:
                    for d in range(2):
                        dve.wait_ge(e_q, 2 * h + d + 1)
                        dve.scalar_tensor_tensor(qdec[:, d, :, :], qdec[:, d, :, :], GL_K ** -0.5,
                                                 gqk[:, 2 * h:2 * h + 2, 0:TB], ALU.mult, ALU.mult).then_inc(q_dec, 1)
                    far_keys(h)
                flat = sc[:, :, :].rearrange("p s t -> p (s t)")
                if lag == 0:
                    if h:
                        dve.wait_ge(o3_ready, h)
                    own = blocks(flat, 0, P, 0, TB + P, P)
                    other = tmp[:, 0, 0:TB].rearrange("p (t c) -> p t c", t=2)
                    for d, (dst, mask) in enumerate(((own, maskf), (other, maskb))):
                        dve.wait_ge(sc_sum, 2 * h + 2)
                        dve.tensor_tensor(dst, bank[:, 4, d * TB:(d + 1) * TB].rearrange("p (t c) -> p t c", t=2),
                                          blocks(mask[:, :], 0, P, 0, 0, P), ALU.mult).then_inc(sc_part, 1)
                    dve.wait_ge(sc_part, 2 * h + 2)
                    dve.tensor_tensor(own, own, other, ALU.add).then_inc(sc_own, 1)
                if lag == 1:
                    dve.wait_ge(sc_own, h + 1)
                    dve.wait_ge(x_sum, h + 1)
                    dve.tensor_copy(flat[:, P:P + TB], bank[:, 5, 0:TB]).then_inc(sc_ready, 1)
                    dve.tensor_copy(blocks(flat, 0, 64, GL_CHUNK, TB + P, GL_CHUNK),
                                    bank[0:64, 5, TB:TB + P].rearrange("p (t c) -> p t c", t=2)).then_inc(sc_ready, 1)
                    dve.tensor_copy(blocks(flat, 64, P, 0, TB + P, GL_CHUNK),
                                    bank[64:P, 5, TB:TB + P].rearrange("p (t c) -> p t c", t=2)).then_inc(sc_ready, 1)
                if lag == 4:
                    dve.wait_ge(o3_root, h + 1)
                    dve.reciprocal(rstd[:, 0:TB], msq[:, 0:TB]).then_inc(o3_rstd, 1)
                if lag == 5:
                    dve.wait_ge(o3_rstd, h + 1)
                    for v in range(4):
                        dve.scalar_tensor_tensor(osq3[:, v, :], bank[:, 6 + v // 2, (v % 2) * TB:(v % 2 + 1) * TB],
                                                 column("gla_o_norm_2", v), rstd[:, 0:TB], ALU.mult, ALU.mult)\
                           .then_inc(o3_scaled, 1)

            def gla(i, j):
                for h in reversed(range(GL_HEADS)):
                    head_step(h, 8 * i + j - HEAD_AT[h])
                    if 8 * i + j == GATED_AT[h]:
                        dve.wait_ge(o3_scaled, 4 * h + 4)
                        dve.wait_ge(acc_free, 4 * (C0["gg"] + h + 1))
                        z = gg[:, 4 * h:4 * h + 4, :]
                        dve.tensor_tensor(z, osq3[:, :, :], z, ALU.mult).then_inc(z3_ready, 1)

            for i in range(TRIPS["gg"]):
                trip("gg", i, after=gla)

            def rows_out(i, chunk, u, n):
                for tt in range(2):
                    dve.wait_ge(yr_squared, 2 * (2 * i + chunk) + tt + 1)
                    c = 512 * (2 * i + chunk)
                    dve.tensor_tensor(yrow[:, tt, c:c + 512], bank[:, 2 * chunk + tt, :], gainrow[:, c:c + 512], ALU.mult)\
                       .then_inc(yr_gained, 1)

            dve.wait_ge(gain_in, 16)
            stream("gout", rows_out)
            for tt in range(2):
                dve.wait_ge(yr_squared, 6 + tt + 1)
                dve.tensor_reduce(yroot[:, tt:tt + 1], ysum[:, tt, :], AX.X, ALU.add).then_inc(yr_sum, 1)
            dve.wait_ge(x_back, 16)
            dve.wait_ge(yr_gained, 8)
            for tt, c in OUT_PIECES:
                if c == 0:
                    dve.wait_ge(yr_root, tt + 1)
                    dve.reciprocal(yroot[:, tt:tt + 1], yroot[:, tt:tt + 1]).then_inc(yr_rstd, 1)
                    dve.wait_ge(yr_rstd, tt + 1)
                dve.scalar_tensor_tensor(orow[:, tt, c:c + D // 2], yrow[:, tt, c:c + D // 2], yroot[:, tt:tt + 1],
                                         xback[:, tt, c:c + D // 2], ALU.mult, ALU.add).then_inc(out_made, 1)

        @block.tensor
        def _(pe):
            PASSES = ((0, 0), (0, 1), (1, 0))

            def unit_begin(ph, i, j):
                n = UNITS[ph]
                u = U0[ph] + j
                pe.wait_ge(wlo_ready, at(u + 1, i, n))
                chunk, begins, ends = chunk_of(ph, j)
                return u, C0[ph] + chunk, begins, ends

            def bank_free(ph, c, t, i):
                if not under(c, i, CHUNKS[ph], 1):
                    pe.wait_ge(acc_free, at(4 * (c - 1) + t + 1, i, 4 * CHUNKS[ph]))

            def features(ph, i, j, rhs, T, made=None):
                u, c, begins, ends = unit_begin(ph, i, j)
                k0, nk = unit_tiles(ph, j)
                w = [t[:, u % RING, :].rearrange("p (k n) -> p k n", k=2 if nk == 1 else nk) for t in (whi, wlo)]
                of_unit = (0, 1, 2, 3)
                if ph == "up":
                    of_unit, begins, ends = ((0, 1), (2, 3))[j % 2], j % 8 < 2, j % 8 > 5
                turns = ph == "up" or ph == "oabc" and (i, chunk_of(ph, j)[0]) != (0, 0)
                base = 4 * (chunk_of(ph, j)[0] % 2) if turns else 0
                follows = ph in ("wout", "down") and under(0, i, 1, 1)
                for t in of_unit:
                    col = t * P if ph != "up" else (t % 2) * P
                    if begins:
                        bank_free(ph, c - 1 if turns or follows else c, t, i)
                    for k in range(nk):
                        if made is not None and t == of_unit[0]:
                            pe.wait_ge(act_ready, made + k0 + k + 1)
                        for wp, ap in PASSES:
                            mm = pe.matmul(bank[:, base + t, 0:T], w[wp][:, k, col:col + P], rhs(ap, k0 + k),
                                           start=begins and k == 0 and (wp, ap) == (0, 0),
                                           stop=ends and k == nk - 1 and wp == 1)
                    mm.then_inc(tile_pass, 4 // len(of_unit))

            def tokens(ph, i, j, n_tiles, passes, first_bank=0, cols=(0, 512), begun=None):
                u, c, begins, ends = unit_begin(ph, i, j) if begun is None else begun
                k0, nk = unit_tiles(ph, j)
                w = [t[:, u % RING, :].rearrange("p (k n) -> p k n", k=nk) for t in (whi, wlo)]
                for tt in range(n_tiles):
                    if begins:
                        bank_free(ph, c, first_bank + tt, i)
                    for k in range(nk):
                        for wp, ap in PASSES:
                            mm = pe.matmul(bank[:, first_bank + tt, 0:cols[1] - cols[0]], ha((ahi, alo)[ap], k0 + k, tt * P, P),
                                           w[wp][:, k, cols[0]:cols[1]],
                                           start=begins and k == 0 and (wp, ap) == (0, 0),
                                           stop=ends and k == nk - 1 and wp == 1)
                    mm.then_inc(tile_pass, passes[tt])

            def model(T):
                return lambda part, k: ha((ahi, alo)[part], k, 0, T)

            def feature_stream(ph, T, made=None, rhs=None):
                with pe.Fori(0, TRIPS[ph]) as i:
                    for j in range(UNITS[ph]):
                        features(ph, i, j, rhs or model(T), T, made)

            def turn_parameters(g):
                m = min(P, N_PAR - g * P)
                pe.transpose(bank[:, PAR_BANK[g], 0:m], prow[0:m, g, :], ident[0:m, 0:m]).then_inc(par_turned, 1)

            def turn_rows(src, g):
                for k in (2 * g, 2 * g + 1):
                    for tt in range(2):
                        mm = pe.transpose(turned(k)[:, tt * P:(tt + 1) * P], src[:, tt, k * P:(k + 1) * P], ident[:, :])
                return mm

            pe.wait_ge(ident_in, 16)
            pe.wait_ge(first_in, 16 * FIRST_PIECES)
            turn_parameters(0)
            pe.wait_ge(xn_ready, 2)
            for g in range(4):
                turn_rows(xn, g).then_inc(xn_turned, 1)

            def start_step(j):
                if j < 4:
                    pe.wait_ge(xn_ready, 3)
                    pe.wait_ge(act_ready, 2 * j + 2)
                    turn_rows(xn, 4 + j).then_inc(xn_turned, 1)
                if j in (4, 5):
                    pe.wait_ge(small_in, 16 * (N_PIECES - FIRST_PIECES))
                    for g in (2 * j - 7, 2 * j - 6):
                        pe.wait_ge(act_ready, 8 + 2 * g)
                        turn_parameters(g)
                if j == 6:
                    pe.wait_ge(lam_prod, 2)
                    pe.wait_ge(par_ready, 2)
                    pe.matmul(bank[:, 4, 0:2], ones[0:HD, :], lamv[:, 4:6], start=True, stop=True).then_inc(lam_sum, 1)
                    pe.wait_ge(hots_in, 48)
                    for w in range(2):
                        pe.wait_ge(par_ready, 3 + w)
                        pe.matmul(bank[0:N_HEADS, 5 + w, 0:LINE], tabx[:, :], hots[:, w, :], start=True, stop=True)\
                          .then_inc(line_sum, 1)
                if 8 <= j < 16:
                    g = j - 8
                    if g == 0:
                        pe.wait_ge(lam_exp, 1)
                        pe.wait_ge(line_ready, 2)
                        pe.wait_ge(par_ready, PAR_GROUPS)
                    if g >= 4:
                        pe.wait_ge(row_taken, g - 3)
                    turn_rows(xrow, g).then_inc(row_turned, 1)
                if j == 16:
                    pe.wait_ge(meta_in, 16)
                    pe.wait_ge(row_taken, 5)
                    for k in range(KD):
                        mm = pe.transpose(bank[:, 4, k * TM:(k + 1) * TM], mrow[:, k * P:(k + 1) * P], ident[0:TM, 0:TM])
                    mm.then_inc(row_turned, 1)

            def norm_before(b):
                T = T_PRE[b]
                for n, g in enumerate(UPDATE_ORDER):
                    if n < 2:
                        pe.wait_ge(sq_ready, 4 * (b - 1) + n + 1)
                    else:
                        pe.wait_ge(sq_folded, 2 * (b - 1) + n - 1)
                    for k in range(4 * g, 4 * g + (4 if n < 2 else 2)):
                        mm = pe.matmul(bank[:, 4, 0:T], ones[:, :], Y[b][:, k, 0:T], start=k == 0,
                                       stop=k == 4 * UPDATE_ORDER[3] + 1)
                mm.then_inc(sq_summed, 1)

            def norm_after(b):
                T = T_POST[b]
                pe.wait_ge(y_summed, (KD + 4) * b)
                pe.matmul(bank[:, 5, 0:T], ones[:, :], sqacc[:, 0:T], start=True, stop=True).then_inc(mean_ready, 1)


            def branch_step(m):
                read = {0: ("qkva", 2), 4: ("qkva", 3), 8: ("kvb", 1), 16: ("qkvc", 2), 20: ("qkvc", 3)}.get(m)
                if read:
                    pe.wait_ge(acc_free, 4 * (C0[read[0]] + read[1]))
                if m < 24:
                    r = 64 * (m % 2)
                    if m < 8:
                        q, k = qaT[r:r + 64, m // 2, :], kaT[r:r + 64, m // 2, :]
                    elif m < 16:
                        q, k = qbT[r:r + 64, (m - 8) // 2, :], kbT[r:r + 64, int((m - 8) // 4 != m % 2), :]
                    else:
                        q, k = qcT[r:r + 64, (m - 16) // 2, :], kcT[r:r + 64, (m - 16) // 2, :]
                    if m >= 2:
                        pe.wait_ge(s_biased, 2 * (m - 1))
                    pe.matmul(bank[:, 4 + m % 2, 0:P], q[:, 0:P], k[:, 0:P], start=True, stop=True)
                    pe.matmul(bank[:, 4 + m % 2, P:384], q[:, P:TB], k[:, :], start=True, stop=True).then_inc(s_ready, 1)
                if m >= 2 and ends_job(m - 2):
                    mm_, job = m - 2, job_of(m - 2)
                    src = prob[:, (mm_ if mm_ >= 8 else mm_ - 1) % 4, :]
                    pe.wait_ge(p_scaled, 2 * job + 2)
                    if job >= 1:
                        pe.wait_ge(pT_ready, job)
                    for c in range(3):
                        mm = pe.transpose(bank[:, 6, c * P:(c + 1) * P], src[:, c * P:(c + 1) * P], ident[:, :])
                    mm.then_inc(p_turned, 1)
                if m >= 4 and ends_job(m - 4):
                    mm_, job = m - 4, job_of(m - 4)
                    unit = mm_ // 2
                    pe.wait_ge(pT_ready, job + 1)
                    if mm_ < 8 or mm_ % 2 == 0:
                        pe.wait_ge(o_free, unit)
                    if mm_ < 8:
                        o, v = bank[:, 7, 0:TB], [vatok[:, tt, P * unit:P * unit + P] for tt in range(2)]
                    else:
                        r = 64 * (mm_ % 2)
                        o = bank[r:r + 64, 7, 0:TB]
                        if mm_ < 16:
                            kv = (mm_ - 8) // 4
                            v = [vbtok[:, tt, 64 * kv:64 * kv + 64] for tt in range(2)]
                        else:
                            v = [vctok[:, tt, 64 * (mm_ - 16):64 * (mm_ - 16) + 64] for tt in range(2)]
                    pe.matmul(o, v[0], probT[:, job % 2, 0:TB], start=True, stop=False)
                    pe.matmul(o[:, P:TB], v[1], probT[:, job % 2, TB:384], start=False, stop=True).then_inc(o_ready, 1)

            def beside(ph, i, j):
                m = step_beside(ph, i, j)
                if m is not None:
                    branch_step(m)
                if ph == "gates" and (i, j) == (1, 3):
                    pe.wait_ge(a_squared, 1)
                    pe.wait_ge(s_biased, 48)
                    for c in range(2):
                        pe.matmul(bank[:, 4 + c, :], ones[:, :], osq[:, 2 * c:2 * c + 2, :].rearrange("p h t -> p (h t)"),
                                  start=True, stop=True).then_inc(a_summed, 1)

            def qkv(ph):
                for j in range(UNITS[ph]):
                    if ph == "qkva" and j < 8:
                        pe.wait_ge(act_ready, 2 * j + 2)
                    if j < 16:
                        features(ph, 0, j, model(TB), TB)
                    else:
                        tokens(ph, 0, j, 2, (1, 3))
                    beside(ph, 0, j)
                    if ph == "qkva":
                        start_step(j)

            qkv("qkva")
            for j in range(UNITS["qb"]):
                features("qb", 0, j, model(TB), TB)
                beside("qb", 0, j)
            for j in range(UNITS["kvb"]):
                unit = unit_begin("kvb", 0, j)
                u, c, begins, ends = unit
                k0, nk = unit_tiles("kvb", j)
                w = [t[:, u % RING, :].rearrange("p (k n) -> p k n", k=nk) for t in (whi, wlo)]
                if begins:
                    bank_free("kvb", c, 0, 0)
                for k in range(nk):
                    for wp, ap in PASSES:
                        mm = pe.matmul(bank[:, 0, 0:TB], w[wp][:, k, 0:P], ha((ahi, alo)[ap], k0 + k, 0, TB),
                                       start=begins and k == 0 and (wp, ap) == (0, 0), stop=ends and k == nk - 1 and wp == 1)
                mm.then_inc(tile_pass, 1)
                tokens("kvb", 0, j, 2, (1, 2), first_bank=1, cols=(P, 2 * P), begun=unit)

            qkv("qkvc")
            for i in range(2):
                for j in range(UNITS["gates"]):
                    features("gates", i, j, model(TB), TB)
                    beside("gates", i, j)
            with pe.Fori(2, TRIPS["gates"]) as i:
                for j in range(UNITS["gates"]):
                    features("gates", i, j, model(TB), TB)
            pe.wait_ge(o_free, 12)
            pe.wait_ge(y_done, 1)
            for i in range(TRIPS["oabc"]):
                for j in range(UNITS["oabc"]):
                    branch = chunk_of("oabc", j)[0] % 3
                    features("oabc", i, j, lambda part, k: (yhi, ylo)[part][:, 4 * branch + k, :], TB)
            for j in range(UNITS["wout"]):
                features("wout", 0, j, model(TB), TB, LO["mix"])
            with pe.Fori(1, TRIPS["wout"]) as i:
                for j in range(UNITS["wout"]):
                    features("wout", i, j, model(TB), TB, LO["mix"])
            norm_after(1)
            norm_before(1)
            with pe.Fori(0, TRIPS["up"]) as i:
                for j in range(UNITS["up"]):
                    features("up", i, j, model(TB), TB, LO["norm1"] if j < 8 else None)
            def down_trip(i):
                for j in range(UNITS["down"]):
                    features("down", i, j, lambda part, k: (ghi, glo)[part][:, k, :], TB, LO["ff"])

            down_trip(0)
            with pe.Fori(1, TRIPS["down"]) as i:
                down_trip(i)
            norm_after(2)
            norm_before(2)

            def qk_norm(i, j):
                p, odd = divmod(j, 2)
                if odd:
                    return
                if not under(p - 5, i, 4, 0):
                    qk_turn(p - 1, i)
                pe.wait_ge(qk_sq, at(p - 3, i, 4))
                if not under(p - 4, i, 4, 2):
                    pe.wait_ge(qk_root, at(p - 5, i, 4))
                pe.matmul(bank[:, 4 + p % 2, 0:T2], ones[:, :], sq2[:, p % 2, :], start=True, stop=True).then_inc(qk_sum, 1)

            def qk_turn(p, i):
                pe.wait_ge(qk_normed, at(p - 3, i, 4))
                if not under(p - 4, i, 4, 2):
                    pe.wait_ge(qk_sin, at(p - 5, i, 4))
                pe.matmul(bank[:, 6 + p % 2, 0:T2], turn[:, :], n2[:, p % 2, :], start=True, stop=True).then_inc(qk_turned, 1)

            TOK = ((0, P), (P, P), (TB, TM))

            def turn_values(src, b, tt):
                c0, rows = TOK[tt]
                for t in range(4):
                    mm = pe.transpose(bank[0:rows, b, t * P:(t + 1) * P], src[:, t, c0:c0 + rows], ident[:, :])
                return mm

            def attend(s):
                h, second = divmod(s, 2)
                for q in ((0, 1), (2,))[second] if h < AT_HEADS else ():
                    c0, rows = TOK[q]
                    if s == 0 and q == 0:
                        pe.wait_ge(qk_done, 24)
                    if q == 0 and h:
                        pe.wait_ge(p2_ready, 3 * h)
                    if q == 1 and h >= 2:
                        pe.wait_ge(pT2_act, 2 * (h - 1))
                    if q == 2:
                        pe.wait_ge(p2_ready, 3 * h + 1)
                    pe.matmul(bank[0:rows, (4, 5, 4)[q], 0:T2], qk2[:, h, c0:c0 + rows], qk2[:, AT_HEADS + h // 2, :],
                              start=True, stop=True).then_inc(s2_ready, 1)
                if second and 1 <= h <= AT_HEADS:
                    hh = h - 1
                    pe.wait_ge(p2_scaled, 3 * hh + 3)
                    if hh:
                        pe.wait_ge(pT2_dve, hh)
                    for kt in range(2):
                        for q in range(2):
                            mm = pe.transpose(bank[:, 6, kt * TB + q * P:kt * TB + (q + 1) * P],
                                              p2[:, hh % 2, q, kt * P:(kt + 1) * P], ident[:, :])
                    mm.then_inc(p2_turned, 1)
                    if h < AT_HEADS:
                        pe.wait_ge(p2_ready, 3 * h + 2)
                    for kt in range(2):
                        pe.transpose(bank[:, 5, kt * TM:(kt + 1) * TM], p2[0:TM, hh % 2, 2, kt * P:(kt + 1) * P],
                                     ident[0:TM, 0:TM])
                    for q, (c0, rows) in enumerate(TOK):
                        mm = pe.transpose(bank[0:TM, 5, 2 * TM + c0:2 * TM + c0 + rows], p2[0:rows, hh % 2, q, TB:T2],
                                          ident[0:rows, 0:rows])
                    mm.then_inc(p2_turned, 1)
                if not second and 2 <= h < AT_HEADS + 2:
                    hh = h - 2
                    kv = hh // 2
                    pe.wait_ge(pT2_act, 2 * hh + 2)
                    pe.wait_ge(pT2_dve, hh + 1)
                    pe.wait_ge(v2_taken, 3 * (1 + kv // 4))
                    pe.wait_ge(v2_taken, sum(step < s for step in VALUE_STEPS))
                    if hh:
                        pe.wait_ge(o2_taken, hh)
                    for kt, (k0, krows) in enumerate(TOK):
                        mm = pe.matmul(bank[:, 7, 0:T2], v2[0:krows, kt, kv * P:(kv + 1) * P], pT2[0:krows, hh % 2, kt, :],
                                       start=kt == 0, stop=kt == 2)
                    mm.then_inc(o2_ready, 1)
                for n, step in enumerate(VALUE_STEPS):
                    if s == step:
                        i, tt = divmod(n, 3)
                        if tt == 0:
                            pe.wait_ge(acc_free, 4 * (C0["av"] + i + 1))
                        if s > 4:
                            pe.wait_ge(o2_taken, (s - 1) // 2 - 1)
                        if n:
                            pe.wait_ge(v2_taken, n)
                        turn_values(vt2[:, i, :, :], 7, tt).then_inc(v2_turned, 1)

            def aqk_trip(i, norms=True):
                for j in range(UNITS["aqk"]):
                    features("aqk", i, j, model(T2), T2, LO["norm2"])
                    if norms:
                        qk_norm(i, j)

            aqk_trip(0, norms=False)
            pe.wait_ge(rope_in, 48)
            aqk_trip(1)
            with pe.Fori(2, TRIPS["aqk"]) as i:
                aqk_trip(i)
            for i in range(TRIPS["av"]):
                for j in range(UNITS["av"]):
                    features("av", i, j, model(T2), T2)
                    if i == 0:
                        qk_norm(TRIPS["aqk"], j)
                    elif j:
                        attend(j - 1)
                    else:
                        qk_turn(3, TRIPS["aqk"])
            for i in range(TRIPS["ag"]):
                for j in range(UNITS["ag"]):
                    features("ag", i, j, model(T2), T2)
                    attend(8 * (i + 1) + j - 1)
            feature_stream("aout", T2, LO["z2"], z2_part)
            norm_after(3)
            norm_before(3)

            def turn_x(n):
                tt, g = X_PIECES[n]
                if n < 4:
                    updated(pe, 3, g)
                else:
                    pe.wait_ge(xw_taken, n - 3)
                if n == 2:
                    pe.wait_ge(root_ready, PRE(3) + 1)
                for k in range(4):
                    mm = pe.transpose(bank[:, X_BANK[n % 4], k * P:(k + 1) * P], xT[:, 4 * g + k, tt * P:(tt + 1) * P], ident[:, :])
                mm.then_inc(xw_turned, 1)

            for n in range(2):
                turn_x(n)
            for j in range(UNITS["gqk"]):
                features("gqk", 0, j, model(T2), T2, LO["norm3"])
                if j + 2 < len(X_PIECES):
                    turn_x(j + 2)
            with pe.Fori(1, TRIPS["gqk"]) as i:
                for j in range(UNITS["gqk"]):
                    features("gqk", i, j, model(T2), T2, LO["norm3"])
            u, c, _, _ = unit_begin("lr", 0, 0)
            for d in range(2):
                bank_free("lr", c, d, 0)
                for k in range(KD):
                    col = (2 * k + d) * GL_RANK
                    for wp, ap in PASSES:
                        mm = pe.matmul(bank[:, d, 0:T2], (whi, wlo)[wp][:, u % RING, col:col + P], ha((ahi, alo)[ap], k, 0, T2),
                                       start=k == 0 and (wp, ap) == (0, 0), stop=k == KD - 1 and wp == 1)
                mm.then_inc(tile_pass, (1, 3)[d])

            def log_decay(g, j):
                if j == 0:
                    if g == 0:
                        pe.wait_ge(acc_free, 4 * (C0["lr"] + 1))
                        pe.wait_ge(gla_const, 64)
                    if g >= 2:
                        pe.wait_ge(v3_taken, 3 * (g - 1))
                    for n in range(4 * g, 4 * g + 4):
                        d, k = divmod(n, KT)
                        if n >= 4:
                            pe.wait_ge(z_min, n - 3)
                        pe.matmul(bank[:, 4 + n % 4, 0:T2], up_w[:, d, k * P:(k + 1) * P], lrT[:, d, :], start=True, stop=True)\
                          .then_inc(z_sum, 1)

            def values(g, tt):
                pe.wait_ge(acc_free, 4 * (C0["gv"] + g + 1))
                pe.wait_ge(z_min, min(16, 4 * g + 8))
                turn_values(vt3[:, g % 2, :, :], VALUE_BANK[tt], tt).then_inc(v3_turned, 1)

            for g in range(TRIPS["gv"]):
                for j in range(UNITS["gv"]):
                    features("gv", g, j, model(T2), T2)
                    log_decay(g, j)
                    if g and 2 <= j < 5:
                        values(g - 1, j - 2)

            def scores(h):
                for d in range(2):
                    pe.wait_ge(q_dec, 2 * h + d + 1)
                    pe.wait_ge(k_inv, 2 * h + d + 1)
                    if h:
                        pe.wait_ge(o3_root, h)
                    for tt in range(2):
                        for f in range(2):
                            c0 = d * TB + tt * P
                            mm = pe.matmul(bank[:, 4, c0:c0 + P], kinv[:, d, f, tt * P:(tt + 1) * P],
                                           qdec[:, d, f, tt * P:(tt + 1) * P], start=f == 0, stop=f == 1)
                    mm.then_inc(sc_sum, 1)

            def far_scores(h):
                def score(dst, keys, k0, d, t):
                    for f in range(2):
                        mm = pe.matmul(dst, keys[:, f, k0:k0 + dst.shape[0]], qdec[:, d, f, t * GL_CHUNK:(t + 1) * GL_CHUNK],
                                       start=f == 0, stop=f == 1)
                    return mm

                pe.wait_ge(k_far, 8 * h + 8)
                if h:
                    pe.wait_ge(sc_ready, 3 * h)
                    pe.wait_ge(o3_scaled, 4 * h)
                C = GL_CHUNK
                for t, (keys, k0) in enumerate(((kendf, TB), (kfar, 0), (kfar, 16), (kfar, 96))):
                    mm = score(bank[0:TM, 6, t * C:(t + 1) * C], keys, k0, 0, t)
                mm.then_inc(xm_sum, 1)
                score(bank[0:C, 5, 0:C], kfar, 32, 0, 2)
                score(bank[C:P, 5, 0:C], kendf, C, 0, 2)
                score(bank[:, 5, C:2 * C], kfar, 112, 0, 3)
                score(bank[:, 5, 2 * C:3 * C], kback, C, 1, 0)
                score(bank[0:C, 5, 3 * C:4 * C], kendb, 2 * C, 1, 1)
                score(bank[C:P, 5, 3 * C:4 * C], kback, 0, 1, 1)
                for tt in range(2):
                    score(bank[0:C, 5, (4 + tt) * C:(5 + tt) * C], kendf, 2 * tt * C, 0, 2 * tt + 1)
                    mm = score(bank[C:P, 5, (4 + tt) * C:(5 + tt) * C], kendb, (2 * tt + 1) * C, 1, 2 * tt)
                mm.then_inc(x_sum, 1)

            def head_step(h, lag):
                if lag == 0:
                    scores(h)
                if lag == 1:
                    far_scores(h)
                if lag == 3:
                    pe.wait_ge(v3_taken, 3 * TRIPS["gv"])
                    pe.wait_ge(sc_ready, 3 * h + 3)
                    pe.wait_ge(scm_ready, h + 1)
                    for v in range(4):
                        col = h * GL_V + v * P
                        for k, (rows, score) in enumerate(((P, sc[:, 0, :]), (P, sc[:, 1, :]), (TM, scm[:, :]))):
                            mm = pe.matmul(bank[:, 6 + v // 2, (v % 2) * TB:(v % 2 + 1) * TB], v3[0:rows, k, col:col + P], score,
                                           start=k == 0, stop=k == 2)
                    mm.then_inc(o3_ready, 1)
                if lag == 4:
                    pe.wait_ge(sc_part, 2 * h + 2)
                    for v in range(4):
                        pe.wait_ge(o3_sq, 2 * h + v // 2 + 1)
                        mm = pe.matmul(bank[:, 4, 0:TB], ones[:, :], osq3[:, v, :], start=v == 0, stop=v == 3)
                    mm.then_inc(o3_sum, 1)

            for i in range(TRIPS["gg"]):
                for j in range(UNITS["gg"]):
                    features("gg", i, j, model(TB), TB)
                    if (i, j) == (0, 0):
                        for tt in range(3):
                            values(TRIPS["gv"] - 1, tt)
                    for h in range(GL_HEADS):
                        head_step(h, 8 * i + j - HEAD_AT[h])
            for i in range(TRIPS["gout"]):
                for j in range(UNITS["gout"]):
                    u, _, begins, ends = unit_begin("gout", i, j)
                    n = 2 * i + j // 8
                    k0, nk = unit_tiles("gout", j)
                    w = [t[:, u % RING, :].rearrange("p (k n) -> p k n", k=nk) for t in (whi, wlo)]
                    for tt in range(2):
                        b = 2 * (n % 2) + tt
                        if begins and n < 2:
                            pe.wait_ge(acc_free, 4 * (C0["gout"] - 1) + b + 1)
                        elif begins:
                            pe.wait_ge(yr_gained, 2 * (n - 2) + tt + 1)
                        if n == 0:
                            pe.wait_ge(act_ready, LO["z3"] + j // 2 + 1)
                        for k in range(nk):
                            for wp, ap in PASSES:
                                mm = pe.matmul(bank[:, b, :], gated(ap, k0 + k)[:, tt * P:(tt + 1) * P], w[wp][:, k, :],
                                               start=begins and k == 0 and (wp, ap) == (0, 0),
                                               stop=ends and k == nk - 1 and wp == 1)
                        mm.then_inc(tile_pass, 2)

        @block.gpsimd
        def _(pool):
            def low(dst, whole, high, done):
                pool.tensor_tensor(dst, whole, high.bitcast(F32), ALU.subtract).then_inc(done, 1)

            def norm_before(b):
                T = T_PRE[b]
                for k in range(KD):
                    pool.wait_ge(hhi_ready, KD * b + k + 1)
                    low(ha(alo, k, 0, T), tmp[:, k % 4, 0:T], ha(ahi, k, 0, T), act_ready)

            def norm_after(b):
                T = T_POST[b]
                x, y = (t[:, 12:16, 0:T] for t in (xT, Y[b]))
                pool.wait_ge(rstd_ready, POST(b) + 1)
                pool.tensor_tensor(y, y, over_tiles(rstd[:, 0:T]), ALU.mult).then_inc(y_scaled_last, 1)
                pool.wait_ge(y_scaled_last, b)
                pool.tensor_tensor(x, x, y, ALU.add).then_inc(x_updated_last, 1)

            def sum_squares(b):
                ph, T = OUT_STREAM[b], T_POST[b]
                if b > 1:
                    pool.wait_ge(mean_ready, b - 1)
                pool.memset(sqacc[:, :], 0.0).then_inc(y_summed, 4)
                with pool.Fori(0, TRIPS[ph]) as i:
                    for t in range(4):
                        pool.wait_ge(y_squared, at(KD * (b - 1) + t + 1, i, 4))
                        pool.wait_ge(y_summed, at((KD + 4) * (b - 1) + t + 4, i, 4))
                        pool.tensor_tensor(sqacc[:, 0:T], sqacc[:, 0:T], tmp[:, t, 0:T], ALU.add).then_inc(y_summed, 1)

            pool.wait_ge(ya_hi, 1)
            low(ylo[:, 0:DA_HEADS, :], yn[:, :, :], yhi[:, 0:DA_HEADS, :], y_done)
            with pool.Fori(0, KD // 4) as i:
                for chunk in (1, 2):
                    for t in range(4):
                        pool.wait_ge(acc_free, at(4 * (C0["oabc"] + chunk) + t + 1, i, 12))
                        if chunk == 2:
                            pool.wait_ge(mix_two, at(t + 1, i, 4))
                        pool.tensor_tensor(mixtmp[:, 0, t, :], mixtmp[:, 0, t, :], mixtmp[:, 1, t, :], ALU.add)\
                            .then_inc((mix_two, mix_sum)[chunk - 1], 1)
                for t in range(4):
                    pool.wait_ge(mix_part, at(t + 1, i, 4))
                    low(alo_tile(i, t), mixtmp[:, 0, t:t + 1, :], ahi_tile(i, t), act_ready)
            sum_squares(1)
            norm_after(1)
            norm_before(1)
            with pool.Fori(0, TRIPS["up"]) as i:
                for t in range(4):
                    pool.wait_ge(ff_prod, at(t + 1, i, 4))
                    pool.tensor_copy(ghi[:, bass.ds(i * 4 + t, 1), :], pr[:, t % 2:t % 2 + 1, :]).then_inc(ffhi_ready, 1)
                    pool.wait_ge(ffhi_ready, at(t + 1, i, 4))
                    low(glo[:, bass.ds(i * 4 + t, 1), :], pr[:, t % 2:t % 2 + 1, :], ghi[:, bass.ds(i * 4 + t, 1), :], act_ready)
            sum_squares(2)
            norm_after(2)
            norm_before(2)
            pool.wait_ge(rope_in, 48)
            for n in range(24):
                pool.wait_ge(qk_normed, n + 1)
                if n >= 2:
                    pool.wait_ge(qk_done, n - 1)
                pool.tensor_tensor(nc2[:, n % 2, :], n2[:, n % 2, :], cos[:, :], ALU.mult).then_inc(qk_cos, 1)
            for h in range(AT_HEADS):
                pool.wait_ge(z2hi, h + 1)
                if h == FIRST_GATED:
                    pool.wait_ge(tile_pass, 4 * U0["aout"])
                low(z2_part(1, h), qk2[:, h, :], z2_part(0, h), act_ready)
            sum_squares(3)
            norm_after(3)
            norm_before(3)
            for h in range(GL_HEADS):
                keys = gqk[:, KT + 2 * h:KT + 2 * h + 2, :]
                for d, (t, T) in enumerate(((kendf, T2), (kendb, TB))):
                    pool.wait_ge(e_d, 2 * h + d + 1)
                    pool.tensor_tensor(t[:, :, :], t[:, :, :], keys[:, :, 0:T], ALU.mult).then_inc(k_end, 1)
                for d in range(2):
                    pool.wait_ge(e_k, 2 * h + d + 1)
                    pool.tensor_tensor(kinv[:, d, :, :], kinv[:, d, :, :], keys[:, :, 0:TB], ALU.mult).then_inc(k_inv, 1)
            for h in range(GL_HEADS):
                pool.wait_ge(z3hi, h + 1)
                tiles = [t[:, 0:KD * T2].rearrange("p (k t) -> p k t", t=T2)[:, 4 * h:4 * h + 4, 0:TB] for t in (alo, ahi)]
                if h == 0:
                    tiles = z0lo[:, :, :], z0hi[:, :, :]
                if h == 1:
                    pool.wait_ge(tile_pass, 4 * U0["gout"])
                low(tiles[0], gg[:, 4 * h:4 * h + 4, :], tiles[1], act_ready)


INS = ["x", "rel_bias_table", "w_in", "b_gate", "lam_q1", "lam_k1", "lam_q2", "lam_k2", "diff_subln_g", "sinks", "w_oa",
       "w_ob", "w_oc", "w_out", "pre_mix_g", "post_mix_g", "pre_ffn_g", "post_ffn_g", "w_up", "conv_w", "conv_b", "w_down",
       "meta_tokens_2", "pre_norm_2", "post_norm_2", "attn_w_in_2", "attn_q_norm_2", "attn_k_norm_2", "attn_w_out_2",
       "gla_w_in_2", "gla_gk_up_2", "gla_gk_bias_2", "gla_o_norm_2", "gla_w_out_2"]


def kernel(**inputs):
    import concourse.bacc as bacc
    from concourse.bass_utils import run_bass_kernel_spmd

    nc = bacc.Bacc("TRN2", target_bir_lowering=False, num_devices=1, dynamic_dma_scratch_size=64)
    arrays = {name: np.ascontiguousarray(inputs[name]) for name in INS}
    arrays |= shape_constants()
    access = {name: nc.dram_tensor(f"in_{name}", a.shape, mybir.dt.from_np(a.dtype), kind="ExternalInput").ap()
              for name, a in arrays.items()}
    access["subln"] = access["diff_subln_g"]
    out = nc.dram_tensor("out", (TB, D), F32, kind="ExternalOutput").ap()
    two_blocks_kernel(nc, access, out)
    result = run_bass_kernel_spmd(nc, [{f"in_{name}": a for name, a in arrays.items()}], core_ids=[0])
    return result.results[0]["out"].reshape(1, TB, D)
```
